# Optimizing a Trainium2 kernel written in Bass

```python
import math
import jax, jax.numpy as jnp
from jax import lax
import numpy as np

'''One inference step (DEPTH layers) of a Hymba-style hybrid decoder whose token mixing is split
into two parallel head groups: an mLSTM matrix memory (xLSTM, chunkwise-parallel, exact per-token
stabilised recurrence) and a NoPE differential softmax attention (Diff-Transformer). The channel
mixer is a hierarchical MoE (top-1 expert group, then top-2 SwiGLU experts within that group).
16 learned meta tokens are prepended to prompt sequences.

Inputs:
  x_prompt   (BATCH, SEQ, D_MODEL)
  x_sample   (DEC_BATCH, DEC_SEQ, D_MODEL)
  cache_k    (DEPTH, N_POOL, PAGE_SIZE, H_DA, 2*D_QK_DA)  paged diff-attn keys (both maps per head)
  cache_v    (DEPTH, N_POOL, PAGE_SIZE, H_DA, D_V_DA)     paged diff-attn values
  state_C    (DEPTH, DEC_BATCH, H_M, D_V_M, D_QK_M)       stabilised mLSTM matrix memory
  state_n    (DEPTH, DEC_BATCH, H_M, D_QK_M)              stabilised mLSTM normaliser
  state_m    (DEPTH, DEC_BATCH, H_M)                      mLSTM running-max stabiliser
  page_table (DEC_BATCH, N_PAGES) int32
  + weights.
Returns the tuple
  (y_prompt  (BATCH, SEQ, D_MODEL),
   y_sample  (DEC_BATCH, DEC_SEQ, D_MODEL),
   k_prompt  (DEPTH, BATCH, N_META+SEQ, H_DA, 2*D_QK_DA),
   v_prompt  (DEPTH, BATCH, N_META+SEQ, H_DA, D_V_DA),
   C_prompt  (DEPTH, BATCH, H_M, D_V_M, D_QK_M),
   n_prompt  (DEPTH, BATCH, H_M, D_QK_M),
   m_prompt  (DEPTH, BATCH, H_M),
   k_sample  (DEPTH, DEC_BATCH, DEC_SEQ, H_DA, 2*D_QK_DA),
   v_sample  (DEPTH, DEC_BATCH, DEC_SEQ, H_DA, D_V_DA),
   C_sample  (DEPTH, DEC_BATCH, H_M, D_V_M, D_QK_M),
   n_sample  (DEPTH, DEC_BATCH, H_M, D_QK_M),
   m_sample  (DEPTH, DEC_BATCH, H_M))
'''

D_MODEL = 1024
BATCH = 1
SEQ = 512
DEPTH = 1
DEC_BATCH = 8
DEC_SEQ = 1
PAST_LEN = 256
PAGE_SIZE = 128

N_META = 16
MIX_WIDTH = D_MODEL
H_M = 4
D_V_M = MIX_WIDTH // 2 // H_M
D_QK_M = D_V_M // 2
H_DA = 4
D_V_DA = MIX_WIDTH // 2 // H_DA
D_QK_DA = D_V_DA // 2
CHUNK = 128
Q_BLOCK = 128
N_GROUPS = 4
EXPERTS_PER_GROUP = 8
N_EXPERTS = N_GROUPS * EXPERTS_PER_GROUP
TOP_K_IN_GROUP = 2
D_EXPERT = D_MODEL // 4
EPS = 1e-6
FORGET_BIAS = 3.0
PROJ_SIZES = (H_M * D_QK_M, H_M * D_QK_M, H_M * D_V_M, H_M * D_V_M, H_M, H_M,
              H_DA * 2 * D_QK_DA, H_DA * 2 * D_QK_DA, H_DA * D_V_DA)
PROJ_WIDTH = sum(PROJ_SIZES)

kernel_name = 'hymba_mlstm_diffattn_hmoe_step'

def split_points():
    return tuple(int(o) for o in np.cumsum(PROJ_SIZES)[:-1])

def rms_norm(x, g):
    x32 = x.astype(jnp.float32)
    return x32 * lax.rsqrt(jnp.mean(x32 * x32, axis=-1, keepdims=True) + EPS) * g.astype(jnp.float32)

def split_maps(rows):
    r = rows.reshape(rows.shape[0], rows.shape[1], H_DA, 2, D_QK_DA)
    return r[:, :, :, 0].transpose(0, 2, 1, 3), r[:, :, :, 1].transpose(0, 2, 1, 3)

def mixer_inputs(x, g, w_in, b_gates):
    B, T = x.shape[0], x.shape[1]
    h = rms_norm(x, g).astype(x.dtype)
    p = h @ w_in
    mq, mk, mv, mo, mi, mf, dq, dk, dv = jnp.split(p, split_points(), axis=-1)

    def heads(a, hd):
        return a.reshape(B, T, -1, hd).transpose(0, 2, 1, 3).astype(jnp.float32)

    q = heads(mq, D_QK_M)
    k = heads(mk, D_QK_M) * (D_QK_M ** -0.5)
    v = heads(mv, D_V_M)
    gates = jnp.concatenate([mi, mf], axis=-1).astype(jnp.float32) + b_gates.astype(jnp.float32)
    ig = gates[..., :H_M].transpose(0, 2, 1)
    lf = jax.nn.log_sigmoid(gates[..., H_M:]).transpose(0, 2, 1)
    k_rows = dk.reshape(B, T, H_DA, 2 * D_QK_DA)
    v_rows = dv.reshape(B, T, H_DA, D_V_DA)
    q1, q2 = split_maps(dq.reshape(B, T, H_DA, 2 * D_QK_DA))
    return (q, k, v, ig, lf), mo, q1, q2, k_rows, v_rows

def mlstm_chunk(state, xs):
    C, n, m = state
    q, k, v, ig, lf = xs
    L = q.shape[2]
    b = jnp.cumsum(lf, axis=-1)
    causal = jnp.arange(L)[:, None] >= jnp.arange(L)[None, :]
    log_w = jnp.where(causal, b[..., :, None] - b[..., None, :] + ig[..., None, :], -jnp.inf)
    log_inter = b + m[..., None]
    m_row = jnp.maximum(log_inter, jnp.max(log_w, axis=-1))
    w_intra = jnp.exp(log_w - m_row[..., None])
    w_inter = jnp.exp(log_inter - m_row)
    s = jnp.einsum('bhtd,bhsd->bhts', q, k) * w_intra
    num = jnp.einsum('bhts,bhsv->bhtv', s, v) + w_inter[..., None] * jnp.einsum('bhvd,bhtd->bhtv', C, q)
    den = jnp.sum(s, axis=-1) + w_inter * jnp.einsum('bhd,bhtd->bht', n, q)
    h = num / jnp.maximum(jnp.abs(den), jnp.exp(-m_row))[..., None]
    b_last = b[..., -1]
    log_ws = b_last[..., None] - b + ig
    m_new = jnp.maximum(m + b_last, jnp.max(log_ws, axis=-1))
    ws = jnp.exp(log_ws - m_new[..., None])
    wc = jnp.exp(m + b_last - m_new)
    C_new = wc[..., None, None] * C + jnp.einsum('bhs,bhsv,bhsd->bhvd', ws, v, k)
    n_new = wc[..., None] * n + jnp.einsum('bhs,bhsd->bhd', ws, k)
    return (C_new, n_new, m_new), h

def mlstm_prompt(q, k, v, ig, lf):
    B, H = q.shape[0], q.shape[1]
    init = (jnp.zeros((B, H, D_V_M, D_QK_M), jnp.float32),
            jnp.zeros((B, H, D_QK_M), jnp.float32),
            jnp.zeros((B, H), jnp.float32))
    st, h_meta = mlstm_chunk(init, tuple(a[:, :, :N_META] for a in (q, k, v, ig, lf)))
    n_chunks = SEQ // CHUNK

    def to_chunks(a):
        r = a[:, :, N_META:]
        return jnp.moveaxis(r.reshape(B, H, n_chunks, CHUNK, *r.shape[3:]), 2, 0)

    st, h_real = lax.scan(mlstm_chunk, st, tuple(to_chunks(a) for a in (q, k, v, ig, lf)))
    h_real = jnp.moveaxis(h_real, 0, 2).reshape(B, H, SEQ, D_V_M)
    return jnp.concatenate([h_meta, h_real], axis=2), st

def diff_attn(q1, q2, k1, k2, v, q_pos, k_pos, lam):
    scale = D_QK_DA ** -0.5
    mask = k_pos[None, :] <= q_pos[:, None]
    s1 = jnp.einsum('bhqd,bhkd->bhqk', q1, k1).astype(jnp.float32) * scale
    s2 = jnp.einsum('bhqd,bhkd->bhqk', q2, k2).astype(jnp.float32) * scale
    a1 = jax.nn.softmax(jnp.where(mask, s1, -jnp.inf), axis=-1)
    a2 = jax.nn.softmax(jnp.where(mask, s2, -jnp.inf), axis=-1)
    return jnp.einsum('bhqk,bhkv->bhqv', a1 - lam * a2, v)

def diff_attn_prompt(q1, q2, k1, k2, v, lam):
    B, H = q1.shape[0], q1.shape[1]
    T = N_META + SEQ
    k_pos = jnp.arange(T)
    out_meta = diff_attn(q1[:, :, :N_META], q2[:, :, :N_META], k1[:, :, :N_META], k2[:, :, :N_META],
                         v[:, :, :N_META], jnp.arange(N_META), jnp.arange(N_META), lam)
    n_blocks = SEQ // Q_BLOCK

    def to_blocks(a):
        return jnp.moveaxis(a[:, :, N_META:].reshape(B, H, n_blocks, Q_BLOCK, D_QK_DA), 2, 0)

    starts = N_META + jnp.arange(n_blocks) * Q_BLOCK

    def one_block(args):
        q1b, q2b, start = args
        return diff_attn(q1b, q2b, k1, k2, v, start + jnp.arange(Q_BLOCK), k_pos, lam)

    out_real = lax.map(one_block, (to_blocks(q1), to_blocks(q2), starts))
    out_real = jnp.moveaxis(out_real, 0, 2).reshape(B, H, SEQ, D_V_DA)
    return jnp.concatenate([out_meta, out_real], axis=2)

def mixer_output(h_m, mo, a, g_m, g_da, lam_init, w_out, dtype):
    B, T = mo.shape[0], mo.shape[1]
    hm = rms_norm(h_m, g_m).transpose(0, 2, 1, 3).reshape(B, T, H_M * D_V_M) * jax.nn.sigmoid(mo.astype(jnp.float32))
    ha = (rms_norm(a, g_da) * (1.0 - lam_init)).transpose(0, 2, 1, 3).reshape(B, T, H_DA * D_V_DA)
    return jnp.concatenate([hm, ha], axis=-1).astype(dtype) @ w_out

def moe_ffn(h, w_group, b_group, w_router, b_router, w_gate, w_up, w_down):
    N = h.shape[0]
    g_probs = jax.nn.softmax((h @ w_group).astype(jnp.float32) + b_group.astype(jnp.float32), axis=-1)
    g_idx = jnp.argmax(g_probs, axis=-1)
    g_p = jnp.max(g_probs, axis=-1, keepdims=True)
    e_logits = ((h @ w_router).astype(jnp.float32) + b_router.astype(jnp.float32)).reshape(N, N_GROUPS, EXPERTS_PER_GROUP)
    e_in = jnp.einsum('ng,nge->ne', jax.nn.one_hot(g_idx, N_GROUPS, dtype=jnp.float32), e_logits)
    top_v, top_i = lax.top_k(e_in, TOP_K_IN_GROUP)
    top_p = jax.nn.softmax(top_v, axis=-1) * g_p
    expert_id = g_idx[:, None] * EXPERTS_PER_GROUP + top_i
    gates = jnp.sum(jax.nn.one_hot(expert_id, N_EXPERTS, dtype=jnp.float32) * top_p[..., None], axis=1)
    y = jnp.zeros((N, h.shape[1]), jnp.float32)
    for e in range(N_EXPERTS):
        act = jax.nn.silu(h @ w_gate[e]) * (h @ w_up[e])
        y = y + gates[:, e:e + 1] * (act @ w_down[e]).astype(jnp.float32)
    return y.astype(h.dtype)

def setup_inputs(seed: int = 0) -> dict:
    key = jax.random.key(seed)
    ks = jax.random.split(key, 32)
    n_pages = PAST_LEN // PAGE_SIZE
    n_pool = (DEC_BATCH * n_pages * 5) // 4
    nrm = jax.random.normal
    f32 = jnp.float32
    page_table = jax.random.permutation(ks[7], n_pool)[:DEC_BATCH * n_pages].reshape(DEC_BATCH, n_pages).astype(jnp.int32)
    b_gates = jnp.concatenate([0.1 * nrm(ks[11], (DEPTH, H_M), f32),
                               FORGET_BIAS + 0.5 * nrm(ks[12], (DEPTH, H_M), f32)], axis=-1)
    return {
        'x_prompt': nrm(ks[0], (BATCH, SEQ, D_MODEL), f32),
        'x_sample': nrm(ks[1], (DEC_BATCH, DEC_SEQ, D_MODEL), f32),
        'cache_k': nrm(ks[2], (DEPTH, n_pool, PAGE_SIZE, H_DA, 2 * D_QK_DA), f32),
        'cache_v': nrm(ks[3], (DEPTH, n_pool, PAGE_SIZE, H_DA, D_V_DA), f32),
        'state_C': nrm(ks[4], (DEPTH, DEC_BATCH, H_M, D_V_M, D_QK_M), f32),
        'state_n': nrm(ks[5], (DEPTH, DEC_BATCH, H_M, D_QK_M), f32),
        'state_m': nrm(ks[6], (DEPTH, DEC_BATCH, H_M), f32),
        'page_table': page_table,
        'meta_tokens': nrm(ks[8], (N_META, D_MODEL), f32),
        'norm_mix': 1.0 + 0.02 * nrm(ks[9], (DEPTH, D_MODEL), f32),
        'w_in': nrm(ks[10], (DEPTH, D_MODEL, PROJ_WIDTH), f32) * D_MODEL ** -0.5,
        'b_gates': b_gates,
        'head_norm_m': 1.0 + 0.02 * nrm(ks[13], (DEPTH, D_V_M), f32),
        'lambda_q1': 0.1 * nrm(ks[14], (DEPTH, D_QK_DA), f32),
        'lambda_k1': 0.1 * nrm(ks[15], (DEPTH, D_QK_DA), f32),
        'lambda_q2': 0.1 * nrm(ks[16], (DEPTH, D_QK_DA), f32),
        'lambda_k2': 0.1 * nrm(ks[17], (DEPTH, D_QK_DA), f32),
        'head_norm_da': 1.0 + 0.02 * nrm(ks[18], (DEPTH, D_V_DA), f32),
        'w_out': nrm(ks[19], (DEPTH, MIX_WIDTH, D_MODEL), f32) * MIX_WIDTH ** -0.5,
        'norm_ffn': 1.0 + 0.02 * nrm(ks[20], (DEPTH, D_MODEL), f32),
        'w_group': nrm(ks[21], (DEPTH, D_MODEL, N_GROUPS), f32) * D_MODEL ** -0.5,
        'b_group': 0.01 * nrm(ks[22], (DEPTH, N_GROUPS), f32),
        'w_router': nrm(ks[23], (DEPTH, D_MODEL, N_EXPERTS), f32) * D_MODEL ** -0.5,
        'b_router': 0.01 * nrm(ks[24], (DEPTH, N_EXPERTS), f32),
        'w_gate_e': nrm(ks[25], (DEPTH, N_EXPERTS, D_MODEL, D_EXPERT), f32) * D_MODEL ** -0.5,
        'w_up_e': nrm(ks[26], (DEPTH, N_EXPERTS, D_MODEL, D_EXPERT), f32) * D_MODEL ** -0.5,
        'w_down_e': nrm(ks[27], (DEPTH, N_EXPERTS, D_EXPERT, D_MODEL), f32) * D_EXPERT ** -0.5,
        'norm_final': 1.0 + 0.02 * nrm(ks[28], (D_MODEL,), f32),
    }

def reference(x_prompt, x_sample, cache_k, cache_v, state_C, state_n, state_m, page_table,
              meta_tokens, norm_mix, w_in, b_gates, head_norm_m, lambda_q1, lambda_k1, lambda_q2,
              lambda_k2, head_norm_da, w_out, norm_ffn, w_group, b_group, w_router, b_router,
              w_gate_e, w_up_e, w_down_e, norm_final):
    T = N_META + SEQ
    xp = jnp.concatenate([jnp.broadcast_to(meta_tokens.astype(x_prompt.dtype)[None], (BATCH, N_META, D_MODEL)), x_prompt], axis=1)
    xs = x_sample
    kp_l, vp_l, Cp_l, np_l, mp_l = [], [], [], [], []
    ks_l, vs_l, Cs_l, ns_l, ms_l = [], [], [], [], []
    for l in range(DEPTH):
        lam_init = 0.8 - 0.6 * math.exp(-0.3 * l)
        lam = (jnp.exp(jnp.sum(lambda_q1[l].astype(jnp.float32) * lambda_k1[l].astype(jnp.float32)))
               - jnp.exp(jnp.sum(lambda_q2[l].astype(jnp.float32) * lambda_k2[l].astype(jnp.float32))) + lam_init)

        m_in, mo_p, q1p, q2p, kr_p, vr_p = mixer_inputs(xp, norm_mix[l], w_in[l], b_gates[l])
        hm_p, (C_p, n_p, m_p) = mlstm_prompt(*m_in)
        k1p, k2p = split_maps(kr_p)
        a_p = diff_attn_prompt(q1p, q2p, k1p, k2p, vr_p.transpose(0, 2, 1, 3).astype(jnp.float32), lam)
        xp = xp + mixer_output(hm_p, mo_p, a_p, head_norm_m[l], head_norm_da[l], lam_init, w_out[l], xp.dtype)

        m_in_s, mo_s, q1s, q2s, kr_s, vr_s = mixer_inputs(xs, norm_mix[l], w_in[l], b_gates[l])
        st0 = (state_C[l].astype(jnp.float32), state_n[l].astype(jnp.float32), state_m[l].astype(jnp.float32))
        (C_s, n_s, m_s), hm_s = mlstm_chunk(st0, m_in_s)
        k_past = cache_k[l][page_table].reshape(DEC_BATCH, PAST_LEN, H_DA, 2 * D_QK_DA)
        v_past = cache_v[l][page_table].reshape(DEC_BATCH, PAST_LEN, H_DA, D_V_DA)
        k_all = jnp.concatenate([k_past, kr_s.astype(k_past.dtype)], axis=1)
        v_all = jnp.concatenate([v_past, vr_s.astype(v_past.dtype)], axis=1)
        k1s, k2s = split_maps(k_all)
        a_s = diff_attn(q1s, q2s, k1s, k2s, v_all.transpose(0, 2, 1, 3).astype(jnp.float32),
                        PAST_LEN + jnp.arange(DEC_SEQ), jnp.arange(PAST_LEN + DEC_SEQ), lam)
        xs = xs + mixer_output(hm_s, mo_s, a_s, head_norm_m[l], head_norm_da[l], lam_init, w_out[l], xs.dtype)

        hp = rms_norm(xp, norm_ffn[l]).astype(xp.dtype).reshape(BATCH * T, D_MODEL)
        hs = rms_norm(xs, norm_ffn[l]).astype(xs.dtype).reshape(DEC_BATCH * DEC_SEQ, D_MODEL)
        y = moe_ffn(jnp.concatenate([hp, hs], axis=0), w_group[l], b_group[l], w_router[l], b_router[l],
                    w_gate_e[l], w_up_e[l], w_down_e[l])
        xp = xp + y[:BATCH * T].reshape(BATCH, T, D_MODEL)
        xs = xs + y[BATCH * T:].reshape(DEC_BATCH, DEC_SEQ, D_MODEL)

        kp_l.append(kr_p.astype(cache_k.dtype)); vp_l.append(vr_p.astype(cache_v.dtype))
        Cp_l.append(C_p.astype(state_C.dtype)); np_l.append(n_p.astype(state_n.dtype)); mp_l.append(m_p.astype(state_m.dtype))
        ks_l.append(kr_s.astype(cache_k.dtype)); vs_l.append(vr_s.astype(cache_v.dtype))
        Cs_l.append(C_s.astype(state_C.dtype)); ns_l.append(n_s.astype(state_n.dtype)); ms_l.append(m_s.astype(state_m.dtype))

    y_prompt = rms_norm(xp, norm_final)[:, N_META:].astype(x_prompt.dtype)
    y_sample = rms_norm(xs, norm_final).astype(x_sample.dtype)
    return (y_prompt, y_sample,
            jnp.stack(kp_l), jnp.stack(vp_l), jnp.stack(Cp_l), jnp.stack(np_l), jnp.stack(mp_l),
            jnp.stack(ks_l), jnp.stack(vs_l), jnp.stack(Cs_l), jnp.stack(ns_l), jnp.stack(ms_l))


_drawn_inputs = setup_inputs


def setup_inputs(seed=0):
    import zlib

    import numpy as np

    out = dict(_drawn_inputs(seed))
    spreads = {}
    factors = {'head_norm_m': 12.229,
     'head_norm_da': 8.634,
     'b_group': 3.101,
     'norm_final': 7.442,
     'lambda_q1': 5.78,
     'norm_ffn': 4.344,
     'b_router': 7.302}
    for name, (base, spread) in spreads.items():
        noise = np.random.default_rng([zlib.crc32(name.encode()), seed]).standard_normal(out[name].shape)
        drawn = base * np.exp(spread * noise) if base else spread * noise
        out[name] = __import__('jax').numpy.asarray(drawn.astype(out[name].dtype))
    for name, factor in factors.items():
        out[name] = (out[name] * factor).astype(out[name].dtype)
    return out
```

```python
import math
from contextlib import ExitStack

import concourse.bass as bass
from concourse import mybir

D = 1024
SEQ = 512
NMETA = 16
NDEC = 8
PAST = 256
PAGE = 128
NPAGES = PAST // PAGE
NPOOL = 20
H = 4
DQ = 64
DV = 128
NEXP = 32
NGRP = 4
EPG = NEXP // NGRP
DE = 256
KC = D // 128
FC = DE // 128
EPS = 1e-6
LAM_INIT = 0.8 - 0.6 * math.exp(-0.3 * 0)

NT = SEQ // 128
T4 = NT
S0 = 32
N4 = S0 + NDEC
TOK = SEQ + N4
NTILES = NT + 1

SLOTS = 64
PAIRS = NEXP // 2
ASSIGN = 2 * (SEQ + NMETA + NDEC)
XBLOCKS = (ASSIGN - 1) // SLOTS
XPAIRS = (XBLOCKS + 3) // 4 * 2
XBLOCKS = 2 * XPAIRS
XROW = NEXP * SLOTS
DUMP = XROW + XBLOCKS * SLOTS
GROWS = DUMP + 128
MAXQ = (SEQ + NMETA + NDEC) // SLOTS

W_COLS = dict(mqk=0, mv=512, mo=1024, gates=1536, dq=1544, dk=2056, dv=2568)
BLOCKS = ["dq", "dk", "dv", "mqk", "mv", "mo", "wo0", "wo1"]
PROJ = BLOCKS[:6]
FEATURE = ("dq", "dk", "mqk")
UNITS = [(j, h) for j in (4, 0, 1, 2, 3) for h in range(H)]


def nrows(j):
    return 128 if j < NT else N4


def col(j):
    return 128 * j


def schedule():
    order = [("xt", j) for j in range(NTILES)] + [("gates",)]

    def block(b):
        items = [("acc", b, m) for m in range(4)] + [("small", b)]
        if b == "dq":
            items += [("tok", "dq", T4)]
        if b == "dk":
            items += [("tok", "dk", j) for j in range(NTILES)]
        if b == "mqk":
            items += [("tok", "mq", T4)] + [("tok", "mk", j) for j in range(NTILES)]
        if b in ("mv", "mo", "dv"):
            items += [("tok", b, T4)]
        return items

    order += block("dq") + block("dk") + [("rows",)] + block("dv") + [("decscore",)]
    back = block("mqk") + [("decmix",)] + block("mv") + block("mo")
    prev = None
    for n, u in enumerate(UNITS):
        order.append(("qk",) + u)
        take = math.ceil(len(back) / (len(UNITS) - n))
        order += back[:take]
        back = back[take:]
        if prev:
            order += [("tp",) + prev, ("pv",) + prev]
        prev = u
    order += [("mqk_s", 0), ("tp",) + prev, ("pv",) + prev]
    for h in range(H):
        if h:
            order.append(("mqk_s", h))
        order.append(("mpv", h))
    order += [("mdec",), ("cfin",)]
    for j in (0, 1, 2, 3, 4):
        order += [("ot", j), ("wo", j, 0), ("wo", j, 1)]
        if j:
            order += [("rt", j - 1), ("logit", j - 1)]
    order += [("rt", 4), ("logit", 4), ("rank",)]
    return order


ORDER = schedule()


def banks_of(item):
    kind = item[0]
    if kind in ("xt", "ot", "rt"):
        return ("a0", "a1") if item[1] % 2 == 0 and kind == "xt" else ("S",)
    if kind == "gates":
        return ("t", "p")
    if kind == "acc":
        return ("a%d" % (item[2] % 2),)
    if kind == "wo":
        return ("a%d" % item[2],)
    return {"small": ("t",), "tok": ("p",), "rows": ("t",), "decscore": ("t",), "decmix": ("p", "t", "p2"),
            "qk": ("S",), "tp": ("t", "p") if item[-1] is not None and item[0] == "tp" and item[1] < NT else ("p",), "pv": ("p",), "mqk_s": ("S", "t", "p"), "mpv": ("a0", "a1"),
            "mdec": ("t",), "cfin": ("t",), "logit": ("t",), "rank": ("p",)}[kind]


def fillings():
    count, nth = {}, {}
    for item in ORDER:
        for b in banks_of(item):
            region = "p" if b == "p2" else b
            nth[item, b] = count.get(region, 0)
            count[region] = count.get(region, 0) + 1
    return nth, count


NTH, TOTAL = fillings()
NCONST = 17
NFIN = 11
RSQ8 = [6, 7, 9, 11, 13]
RSQF = [8, 10, 12, 14, 15]
OFF = [0, 512, 896, 1152]


def build(nc, x_prompt, x_sample, cache_k, cache_v, state_C, state_n, state_m, page_table, meta_tokens,
          norm_mix, w_in, b_gates, head_norm_m, lambda_q1, lambda_k1, lambda_q2, lambda_k2, head_norm_da,
          w_out, norm_ffn, w_group, b_group, w_router, b_router, w_gate_e, w_up_e, w_down_e, norm_final,
          y_prompt, y_sample, k_prompt, v_prompt, C_prompt, n_prompt, m_prompt, k_sample, v_sample,
          C_sample, n_sample, m_sample):
    f32, i32, u32 = mybir.dt.float32, mybir.dt.int32, mybir.dt.uint32
    ALU, ACT, AX = mybir.AluOpType, mybir.ActivationFunctionType, mybir.AxisListType
    ctx = ExitStack()
    with ctx:
        def sb(name, shape, dt=f32):
            return ctx.enter_context(nc.sbuf_tensor(name, shape, dt))

        def sem(name):
            return ctx.enter_context(nc.semaphore(name))

        def dram(name, shape):
            return nc.dram_tensor(name, shape, f32, kind="Internal").ap()

        slot_rows = dram("slot_rows", (GROWS, D))
        slot_out = dram("slot_out", (GROWS, D))
        dec_q, dec_k = dram("dec_q", (NDEC, 512)), dram("dec_k", (NDEC, 512))
        dec_mq, dec_mk = dram("dec_mq", (NDEC, 256)), dram("dec_mk", (NDEC, 256))
        dec_w = dram("dec_w", (2, NDEC, H))
        dec_ps = dram("dec_ps", (NDEC * 8,))
        g_rows = dram("g_rows", (H, TOK))

        X = sb("X", [128, NTILES, D])
        HO = sb("HO", [128, NTILES, D])
        hT = sb("hT", [128, KC, TOK])
        WS = sb("WS", [128, 18432])
        FT = sb("FT", [128, 12 * TOK])
        DVt = sb("DVt", [128, NTILES, H * DV])
        MVA = sb("MVA", [128, NTILES, H, DV + 1])
        MO = sb("MO", [128, NTILES, H * DV])
        MK = sb("MK", [128, NTILES, H * DQ])
        ident, ones, tri = sb("ident", [128, 128]), sb("ones", [128, 128]), sb("tri", [128, 128])
        maskneg = sb("maskneg", [128, 128])
        gm, gda = sb("gm", [128, DV]), sb("gda", [128, DV])
        gmix, gffn = sb("gmix", [128, KC]), sb("gffn", [128, KC])
        wr = sb("wr", [128, KC, NGRP + NEXP])
        wg = sb("wg", [128, KC, 36])
        br = sb("br", [128, NGRP + NEXP])
        bgi, bgf = sb("bgi", [H, 1]), sb("bgf", [H, 1])
        lamv = sb("lamv", [128, 4, DQ])
        lam = sb("lam", [128, 6])
        neghalf = sb("neghalf", [128, 8])
        ss, rr = sb("ss", [128, 16]), sb("rr", [128, 16])
        ss8, rr8 = sb("ss8", [128, 8]), sb("rr8", [128, 8])
        RC = sb("RC", [128, NTILES, 68])
        sgn, sgi = sb("sgn", [64, 4]), sb("sgi", [64, 1], i32)
        rsum = sb("rsum", [128, NTILES * H])
        den = sb("den", [128, 3, 1])
        negG_t, c1 = sb("negG", [H, 1]), sb("c1", [128, 1])
        negG = negG_t[:, :]
        nold = sb("nold", [N4, H, DQ])
        cq, dwb = sb("cq", [128, NDEC * H]), sb("dwb", [128, 2, NDEC * H])
        Lt = sb("Lt", [128, NTILES, NGRP + NEXP])
        xf = sb("xf", [1, XBLOCKS])
        pidx = sb("pidx", [128, 1], i32)
        pfl = sb("pfl", [128, 1])
        vT4 = sb("vT4", [128, 3, 4, N4])
        sums = sb("sums", [128, 8])
        pages = sb("pages", [128, NDEC * NPAGES], i32)
        Sd = sb("Sd", [128, NPAGES, 64])
        Sq = sb("Sq", [64, PAST + 4])
        Wd = sb("Wd", [128, NPAGES, 32])
        dcol = sb("dcol", [64, 8])
        padT = sb("padT", [128, H, N4])
        qk64 = sb("qk64", [64, 2, DQ])
        dr = sb("dr", [N4, 64])

        dqT = FT[:, 0:4 * TOK].rearrange("p (m t) -> p m t", t=TOK)
        dkT = FT[:, 4 * TOK:8 * TOK].rearrange("p (m t) -> p m t", t=TOK)
        mqkT = FT[:, 8 * TOK:12 * TOK].rearrange("p (m t) -> p m t", t=TOK)
        feat = {"dq": dqT, "dk": dkT, "mqk": mqkT}
        hn = [HO[:, 0, :], HO[:, 1, :]]
        tokst = [HO[:, 2, 0:512], HO[:, 2, 512:1024]]
        blkslot = [WS[:, 4096 * s:4096 * (s + 1)].rearrange("p (k n) -> p k n", n=512) for s in range(3)]
        SC = WS[:, 12288:18432]
        GB = SC[:, 0:H * TOK].rearrange("p (h t) -> p h t", t=TOK)
        WT = SC[:, 2208:2208 + 1280]
        WTm = SC[0:NMETA, 3488:3488 + TOK]
        P2 = [SC[:, o:o + 2 * 528].rearrange("p (m s) -> p m s", m=2) for o in (2208, 4040)]
        AT = SC[:, 5096:5096 + 640].rearrange("p (b t) -> p b t", t=128)
        R = SC[:, 4040:4040 + TOK]
        zrow, junk = SC[:, 0:D], SC[:, D:2 * D]
        mflat = MO[:, :, :].rearrange("p a b -> p (a b)")
        hoflat = HO[:, 3:5, :].rearrange("p a b -> p (a b)")
        rF, rE, rB, rI = (mflat[0:H, TOK * n:TOK * (n + 1)] for n in range(4))
        rA, rG, rM = (hoflat[0:H, TOK * n:TOK * (n + 1)] for n in range(3))
        MQ4 = wg[:, :, :].rearrange("p a b -> p (a b)")[0:N4, 0:256]
        nnew = Sq[0:N4, 0:256].rearrange("p (h d) -> p h d", d=DQ)
        cfin = vT4[:, :, :, :].rearrange("p a b c -> p (a b c)")[:, 0:256].rearrange("p (h d) -> p h d", d=DQ)
        nfin = lamv[:, :, :].rearrange("p a b -> p (a b)")[0:1, 0:256]
        gfin = MK[:, :, :].rearrange("p a b -> p (a b)")[:, 0:D]
        kring = [MO[:, n, :] for n in range(5)]
        C0 = WS[:, 8192:8192 + 2048].rearrange("p (b d) -> p b d", d=DQ)
        QB = WS[:, 10240:10240 + 2048].rearrange("p (b d) -> p b d", d=DQ)
        sqd, junk2 = WS[:, 10240:10240 + D], WS[:, 10240 + D:10240 + 2 * D]

        bank = [ctx.enter_context(nc.psum_tensor("bank%d" % n, [128, 512], f32)) for n in (0, 1)]
        Sps = ctx.enter_context(nc.psum_tensor("scores", [128, 2, 1024], f32))
        pt_, pp_ = (ctx.enter_context(nc.psum_tensor(n, [128, 512], f32)) for n in ("bank_t", "bank_p"))
        PS = {"a0": bank[0], "a1": bank[1], "t": pt_, "p": pp_}

        filled = {b: sem("filled_" + b) for b in ("a0", "a1", "S", "t", "p")}
        freed = {b: sem("freed_" + b) for b in ("a0", "a1", "S", "t", "p")}
        x_in = [sem("x_in%d" % j) for j in range(NTILES)]
        const_in, const_made, pad_zeroed = sem("const_in"), sem("const_made"), sem("pad_zeroed")
        gmix_in, ident_made, dr_zeroed, wg_zeroed = sem("gmix_in"), sem("ident_made"), sem("dr_zeroed"), sem("wg_zeroed")
        rows_free = sem("rows_free")
        gfin_in = sem("gfin_in")
        block_in = [sem("block_in%d" % s) for s in range(3)]
        block_used = sem("block_used")
        squares = sem("squares")
        rsq = sem("rsq")
        sums_ready = sem("sums_ready")
        hn_ready = sem("hn_ready")
        act_step, dve_step, pool_step, sp_step = (sem(n) for n in ("act_step", "dve_step", "pool_step", "sp_step"))
        rows_ln = sem("rows_ln")
        rows_scan = sem("rows_scan")
        rows_exp = sem("rows_exp")
        g_out, g_in, m_out = sem("g_out"), sem("g_in"), sem("m_out")
        tok_out = sem("tok_out")
        dq_out, dk_out, dm_out = sem("dq_out"), sem("dk_out"), sem("dm_out")
        fin_out = sem("fin_out")
        page_in = [sem("page_in%d" % n) for n in range(5)]
        page_used = sem("page_used")
        vpage_used = sem("vpage_used")
        pages_ready, ptab_in = sem("pages_ready"), sem("ptab_in")
        qk64_in = sem("qk64_in")
        dec_max, dec_exp, dec_coef, dec_mixed = sem("dec_max"), sem("dec_exp"), sem("dec_coef"), sem("dec_mixed")
        decps_out, decps_in = sem("decps_out"), sem("decps_in")
        pad_ready = sem("pad_ready")
        maxed, mixed = sem("maxed"), sem("mixed")
        lam_sum, lam_exp = sem("lam_sum"), sem("lam_exp")
        decay_made, decay_masked, decay_used, product = (sem(n) for n in (
            "decay_made", "decay_masked", "decay_used", "product"))
        st_in, dw_made, dw_out, dw_in, qb_in, qb_used, kb_in, cn_ready = (sem(n) for n in (
            "st_in", "dw_made", "dw_out", "dw_in", "qb_in", "qb_used", "kb_in", "cn_ready"))
        dm_ready, dm_exp = sem("dm_ready"), sem("dm_exp")
        wsk_ready = sem("wsk_ready")
        cfin_ready = sem("cfin_ready")
        ho_ready = sem("ho_ready")
        x2_ready, xn_ready = sem("x2_ready"), sem("xn_ready")
        zeroed, zero_out = sem("zeroed"), sem("zero_out")
        gexp_in, gexp = sem("gexp_in"), sem("gexp")
        m_ready, pos_ready, table_ready = sem("m_ready"), sem("pos_ready"), sem("table_ready")
        scattered = sem("scattered")
        two = lambda n: [sem("%s%d" % (n, s)) for s in range(2)]
        xg_in, xt_filled, xt_evac, gu_filled, silu_done, act_done, at_filled, at_evac, dn_filled, y0, y1, y_out = (
            two(n) for n in ("xg_in", "xt_filled", "xt_evac", "gu_filled", "silu_done", "act_done", "at_filled",
                             "at_evac", "dn_filled", "y_first", "y_second", "y_out"))
        gu_in = [sem("gu_in%d" % n) for n in range(4)]
        dn_in = [sem("dn_in%d" % n) for n in range(4)]
        y_in = [sem("y_in%d" % n) for n in range(4)]
        y_free = sem("y_free")
        fsq, yfin = sem("final_squares"), sem("y_final")

        eslot = [WS[:, 12288:18432], FT[:, 0:6144], WS[:, 0:6144], WS[:, 6144:12288]]
        Wgu = [e[:, 0:4096].rearrange("p (g k n) -> p g k n", g=2, n=DE) for e in eslot]
        Wdn = [e[:, 4096:6144].rearrange("p (f n) -> p f n", n=D) for e in eslot]
        XG = [DVt[:, 0:2, :].rearrange("p a b -> p (a b)"), DVt[:, 2:4, :].rearrange("p a b -> p (a b)")]
        mvflat = MVA[:, :, :, :].rearrange("p a b c -> p (a b c)")
        YO = [mvflat[:, 0:D], mvflat[:, D:2 * D]]
        hflat = hT[:, :, :].rearrange("p k t -> p (k t)")
        xT = [hflat[:, 1024 * s:1024 * (s + 1)].rearrange("p (k t) -> p k t", t=128) for s in range(2)]
        SG = [hflat[:, 2048 + 256 * s:2304 + 256 * s] for s in range(2)]
        AB = [hflat[:, 2560 + 256 * s:2816 + 256 * s] for s in range(2)]
        aT = [hflat[:, 3072 + 256 * s:3328 + 256 * s].rearrange("p (f t) -> p f t", t=128) for s in range(2)]
        moflat = MO[:, :, :].rearrange("p a b -> p (a b)")
        at = [0]

        def piece(n):
            at[0] += n
            return moflat[:, at[0] - n:at[0]]

        L = Lt[:, :, :]
        Gx = piece(20).rearrange("p (j g) -> p j g", g=4)
        Go = piece(20).rearrange("p (j g) -> p j g", g=4)
        Gk = piece(20).rearrange("p (j g) -> p j g", g=4)
        E8 = [piece(40).rearrange("p (j e) -> p j e", e=8) for _ in range(5)]
        T160 = piece(160)
        M1, M2, MM = (piece(160) for _ in range(3))
        c5 = [piece(5) for _ in range(12)]
        PREF = piece(192)
        CX = piece(32 * MAXQ)
        e32 = [piece(32) for _ in range(6)]
        XT32 = piece(XBLOCKS * 32)
        kiota = sb("kiota", [128, 8])
        qiota = sb("qiota", [128, MAXQ])
        eiota = sb("eiota", [128, 32])
        xiota = sb("xiota", [1, XBLOCKS])
        iscr = sb("iscr", [128, 32], i32)
        valid = sb("valid", [128, NTILES])
        dump = sb("dump", [128, 2, NTILES])
        POS = sb("POS", [128, 2, NTILES], u32)
        TE = sb("TE", [1, XBLOCKS + 1], i32)
        pw = sb("pw", [128, 2, NTILES])
        YG = [WS[:, 2048 * n:2048 * n + 1024] for n in range(2)], [WS[:, 2048 * n + 1024:2048 * n + 2048] for n in range(2)]

        def before(eng, item, b):
            if NTH[item, b]:
                eng.wait_ge(freed["p" if b == "p2" else b], NTH[item, b])

        def after(eng, item, b):
            eng.wait_ge(filled["p" if b == "p2" else b], NTH[item, b] + 1)

        def drained(eng, item, b):
            eng.wait_ge(freed["p" if b == "p2" else b], NTH[item, b] + 1)

        def reuse(eng, done, turns):
            if not (isinstance(turns, int) and turns == 0):
                eng.wait_ge(done, turns)

        def count(kind, *rest):
            n = 0
            for item in ORDER:
                if item[0] == kind:
                    n += 1
                    if item[1:] == rest:
                        return n

        DEC = [(b, p) for b in range(NDEC) for p in range(NPAGES)]
        UIDX = {u: n for n, u in enumerate(UNITS)}
        block = ctx.enter_context(nc.Block())

        @block.sync
        def _(sp):
            for j in range(NT):
                sp.dma_start(X[:, j, :], x_prompt[0, 128 * j:128 * (j + 1), :]).then_inc(x_in[j], 16)
            sp.wait_ge(pad_zeroed, 1)
            sp.dma_start(X[0:NMETA, T4, :], meta_tokens).then_inc(x_in[T4], 16)
            sp.dma_start(X[S0:N4, T4, :], x_sample[:, 0, :]).then_inc(x_in[T4], 16)

            def load_block(n):
                b = BLOCKS[n]
                if n >= 3:
                    sp.wait_ge(block_used, n - 2)
                src = (w_out[0].rearrange("(p k) n -> p k n", k=KC)[:, :, 512 * int(b[2]):512 * int(b[2]) + 512]
                       if b[:2] == "wo" else
                       w_in[0].rearrange("(p k) n -> p k n", k=KC)[:, :, W_COLS[b]:W_COLS[b] + 512])
                sp.dma_start(blkslot[n % 3], src).then_inc(block_in[n % 3], 16)

            for n in range(3):
                load_block(n)
            for item in ORDER:
                kind = item[0]
                if kind == "small" and PROJ.index(item[1]) + 3 < len(BLOCKS):
                    load_block(PROJ.index(item[1]) + 3)
                elif kind == "tok":
                    name, j = item[1:]
                    drained(sp, item, "p")
                    n = count(*item) - 1
                    if name == "dk":
                        s = tokst[n % 2]
                        if j < NT:
                            sp.dma_start(k_prompt[0, 0, NMETA + 128 * j:NMETA + 128 * (j + 1)]
                                         .rearrange("t h d -> t (h d)"), s).then_inc(tok_out, 16)
                        else:
                            sp.dma_start(k_prompt[0, 0, 0:NMETA].rearrange("t h d -> t (h d)"),
                                         s[0:NMETA]).then_inc(tok_out, 16)
                            sp.dma_start(k_sample[0, :, 0].rearrange("t h d -> t (h d)"),
                                         s[S0:N4]).then_inc(tok_out, 16)
                            sp.dma_start(dec_k, s[S0:N4]).then_inc(dk_out, 16)
                            sp.wait_ge(dk_out, 16)
                            sp.wait_ge(dq_out, 16)
                            sp.dma_start(qk64[:, 0, :], dec_q.rearrange("b (u d) -> (b u) d", d=DQ)).then_inc(qk64_in, 16)
                            sp.dma_start(qk64[:, 1, :], dec_k.rearrange("b (u d) -> (b u) d", d=DQ)).then_inc(qk64_in, 16)
                    elif name == "dq":
                        sp.dma_start(dec_q, tokst[n % 2][S0:N4]).then_inc(dq_out, 16)
                    elif name == "mq":
                        sp.dma_start(dec_mq, MQ4[S0:N4]).then_inc(dm_out, 16)
                    elif name == "mk" and j == T4:
                        sp.dma_start(dec_mk, MK[S0:N4, T4, :]).then_inc(dm_out, 16)
                    elif name == "dv":
                        for i in range(NT):
                            sp.dma_start(v_prompt[0, 0, NMETA + 128 * i:NMETA + 128 * (i + 1)]
                                         .rearrange("t h d -> t (h d)"), DVt[:, i, :]).then_inc(fin_out, 16)
                        sp.dma_start(v_prompt[0, 0, 0:NMETA].rearrange("t h d -> t (h d)"),
                                     DVt[0:NMETA, T4, :]).then_inc(fin_out, 16)
                        sp.dma_start(v_sample[0, :, 0].rearrange("t h d -> t (h d)"),
                                     DVt[S0:N4, T4, :]).then_inc(fin_out, 16)
                elif kind == "rows":
                    sp.wait_ge(rows_scan, 2)
                    sp.dma_start(g_rows, rG).then_inc(g_out, 16)
                    sp.dma_start(m_prompt[0, 0, :].rearrange("(h a) -> h a", a=1), rM[:, TOK - 1:TOK],
                                 allow_slow_non_contiguous=True).then_inc(m_out, 16)
                    sp.wait_ge(g_out, 16)
                    sp.wait_ge(zero_out, 32)
                    sp.dma_start(GB, g_rows.rearrange("h t -> (h t)").partition_broadcast(128)
                                 .rearrange("p (h t) -> p h t", t=TOK)).then_inc(g_in, 16)
                elif kind == "decmix":
                    sp.wait_ge(dec_coef, 1)
                    sp.dma_start(dec_ps.rearrange("(r a) -> r a", a=1), Sq[:, PAST:PAST + 1],
                                 allow_slow_non_contiguous=True).then_inc(decps_out, 16)
                    sp.wait_ge(decps_out, 16)
                    sp.dma_start(dr[S0:N4, 40:48], dec_ps.rearrange("(b u) -> b u", u=8)).then_inc(decps_in, 16)
                elif kind == "mdec":
                    sp.wait_ge(block_used, 6)
                    sp.dma_start(C0, state_C[0].rearrange("b h v d -> v (b h) d")).then_inc(st_in, 16)
                    sp.wait_ge(dm_out, 32)
                    sp.dma_start(QB, dec_mq.rearrange("b n -> (b n)").partition_broadcast(128)
                                 .rearrange("p (b d) -> p b d", d=DQ)).then_inc(qb_in, 16)
                    sp.wait_ge(dw_made, 1)
                    sp.dma_start(dec_w[0], dr[S0:N4, 8:12]).then_inc(dw_out, 16)
                    sp.dma_start(dec_w[1], dr[S0:N4, 12:16]).then_inc(dw_out, 16)
                    sp.wait_ge(dw_out, 32)
                    sp.dma_start(dwb[:, :, :], dec_w.rearrange("a b h -> (a b h)").partition_broadcast(128)
                                 .rearrange("p (a b) -> p a b", a=2)).then_inc(dw_in, 16)
                    sp.dma_start(m_sample[0], dr[S0:N4, 4:8]).then_inc(fin_out, 16)
                    sp.wait_ge(qb_used, 1)
                    sp.dma_start(QB, dec_mk.rearrange("b n -> (b n)").partition_broadcast(128)
                                 .rearrange("p (b d) -> p b d", d=DQ)).then_inc(kb_in, 16)
                    sp.wait_ge(cn_ready, 2)
                    sp.dma_start(C_sample[0].rearrange("b h v d -> v (b h) d"), C0).then_inc(fin_out, 16)
                    sp.dma_start(n_sample[0], nnew[S0:N4]).then_inc(fin_out, 16)
                elif kind == "cfin":
                    drained(sp, item, "t")
                    sp.dma_start(C_prompt[0, 0].rearrange("h v d -> v h d"), cfin).then_inc(fin_out, 16)
                    sp.dma_start(n_prompt[0, 0].rearrange("h d -> (h d)").rearrange("(a n) -> a n", a=1),
                                 nfin).then_inc(fin_out, 16)
                    sp.dma_start(gfin, norm_final.partition_broadcast(128)).then_inc(gfin_in, 16)

            def expert_weights(i, s, u, e):
                w = 2 * s + u
                for g, src in enumerate((w_gate_e, w_up_e)):
                    sp.dma_start(Wgu[w][:, g], src[0, e].rearrange("(p k) n -> p k n", k=KC)).then_inc(gu_in[w], 16)
                sp.dma_start(Wdn[w], w_down_e[0, e].rearrange("(p f) n -> p f n", f=FC)).then_inc(dn_in[w], 16)

            def slot_load(i, s):
                sp.dma_start(XG[s], slot_rows[bass.DynSlice((2 * i + s) * 128, 128), :]).then_inc(xg_in[s], 16)

            def pair_loads(i, s, experts):
                sp.wait_ge(xt_filled[s], i)
                slot_load(i, s)
                sp.wait_ge(dn_filled[s], i)
                for u in range(2):
                    expert_weights(i, s, u, experts[u])

            sp.wait_ge(filled["a1"], NTH[("mpv", H - 1), "a1"] + 1)
            for u in range(2):
                expert_weights(0, 0, u, u)
            sp.wait_ge(fin_out, 16 * NFIN)
            sp.wait_ge(block_used, len(BLOCKS))
            sp.wait_ge(squares, 2 * NTILES)
            for u in range(2):
                expert_weights(0, 1, u, 2 + u)
            sp.wait_ge(scattered, 16 * 2 * NTILES)
            for s in range(2):
                slot_rows_first = slot_rows[128 * s:128 * (s + 1), :]
                sp.dma_start(XG[s], slot_rows_first).then_inc(xg_in[s], 16)
            with sp.Fori(1, PAIRS // 2) as i:
                for s in range(2):
                    pair_loads(i, s, [4 * i + 2 * s, 4 * i + 2 * s + 1])
            sp.wait_ge(table_ready, 1)
            more = sp.value_load(TE[0:1, XBLOCKS:XBLOCKS + 1], min_val=0, max_val=XBLOCKS)
            with sp.If(more > 0):
                with sp.Fori(PAIRS // 2, (PAIRS + XPAIRS) // 2) as i:
                    for s in range(2):
                        ids = [sp.value_load(TE[0:1, bass.DynSlice(4 * i + 2 * s + u - 2 * PAIRS, 1)],
                                             min_val=0, max_val=NEXP - 1) for u in range(2)]
                        pair_loads(i, s, ids)

            for n, j in enumerate((0, 1, 2, 3, 4)):
                sp.wait_ge(yfin, n + 1)
                if j < NT:
                    sp.dma_start(y_prompt[0, 128 * j:128 * (j + 1), :], X[:, j, :]).then_inc(fin_out, 16)
                else:
                    sp.dma_start(y_sample[:, 0, :], X[S0:N4, T4, :]).then_inc(fin_out, 16)
            sp.wait_ge(fin_out, 16 * (NFIN + NTILES))
            sp.wait_ge(tok_out, 16 * 6)

        @block.gpsimd
        def _(pool):
            steps = [0]

            def link(ins):
                steps[0] += 1
                ins.then_inc(pool_step, 1)
                pool.wait_ge(pool_step, steps[0])

            pool.dma_start(pages[:, :], page_table.rearrange("b p -> (b p)").partition_broadcast(128)).then_inc(ptab_in, 16)
            link(pool.memset(dr[:, :], 0.0))
            pool.nop().then_inc(dr_zeroed, 1)
            link(pool.memset(ident[:, :], 0.0))
            link(pool.affine_select(out=ident[:, :], in_=ident[:, :], compare_op=ALU.not_equal, fill=1.0,
                                    base=0, pattern=[[-1, 128]], channel_multiplier=1))
            pool.nop().then_inc(ident_made, 1)
            link(pool.memset(maskneg[:, :], 0.0))
            link(pool.memset(ones[:, :], 1.0))
            link(pool.affine_select(out=maskneg[:, :], in_=maskneg[:, :], compare_op=ALU.is_ge, fill=-1e30,
                                    base=0, pattern=[[-1, 128]], channel_multiplier=1))
            link(pool.affine_select(out=tri[:, :], in_=ones[:, :], compare_op=ALU.is_gt, fill=0.0,
                                    base=0, pattern=[[1, 128]], channel_multiplier=-1))
            link(pool.memset(neghalf[:, :], -0.5))
            link(pool.iota(pidx[:, :], [[0, 1]], base=0, channel_multiplier=1))
            link(pool.iota(iscr[:, 0:8], [[-1, 8]], base=8, channel_multiplier=0))
            link(pool.tensor_copy(kiota[:, :], iscr[:, 0:8]))
            link(pool.iota(iscr[:, 0:MAXQ], [[SLOTS, MAXQ]], base=SLOTS, channel_multiplier=0))
            link(pool.tensor_copy(qiota[:, :], iscr[:, 0:MAXQ]))
            link(pool.iota(iscr[:, 0:32], [[SLOTS, 32]], base=0, channel_multiplier=0))
            link(pool.tensor_copy(eiota[:, :], iscr[:, 0:32]))
            link(pool.iota(iscr[:, 0:XBLOCKS], [[1, XBLOCKS]], base=0, channel_multiplier=0))
            link(pool.tensor_copy(xiota[:, :], iscr[0:1, 0:XBLOCKS]))
            link(pool.memset(valid[:, 0:NT], 1.0))
            link(pool.memset(valid[:, NT:], 0.0))
            link(pool.memset(valid[0:NMETA, NT:], 1.0))
            link(pool.memset(valid[S0:N4, NT:], 1.0))
            pool.nop().then_inc(const_made, 1)

            roots = [0]

            def rsqrt(dst, src, width, wait_sem, wait_val):
                pool.wait_ge(wait_sem, wait_val)
                link(pool.tensor_scalar(dst, src, 1.0 / width, EPS, ALU.mult, ALU.add))
                n = dst.shape[1]
                pool.tensor_tensor(dst, dst, neghalf[0:dst.shape[0], 0:n], ALU.pow).then_inc(rsq, 1)
                roots[0] += 1
                pool.wait_ge(rsq, roots[0])

            for j in range(NTILES):
                n = nrows(j)
                rsqrt(rr[0:n, j:j + 1], ss[0:n, j:j + 1], D, squares, j + 1)

            ring = [0]

            def gather(cache, b, p):
                n = ring[0]
                slot = n % 4
                if n >= 4:
                    if n < 16 + 4:
                        pool.wait_ge(page_used, min(n - 3, 16))
                    if n >= 20:
                        pool.wait_ge(vpage_used, n - 19)
                pool.indirect_dma_start(
                    kring[slot], None, cache[0].rearrange("n t h d -> (n t) (h d)"),
                    bass.IndirectOffsetOnAxis(ap=pages[:, b * NPAGES + p:b * NPAGES + p + 1].bitcast(u32), axis=0))\
                    .then_inc(page_in[slot], 16)
                ring[0] += 1

            pool.wait_ge(pages_ready, 1)
            pool.wait_ge(rows_free, 1)
            for n, (b, p) in enumerate(DEC):
                gather(cache_k, b, p)
                if p == 0:
                    if n == 0:
                        pool.wait_ge(dq_out, 16)
                    if b:
                        pool.wait_ge(page_used, 2 * b)
                    pool.dma_start(kring[4], dec_q[b].partition_broadcast(128)).then_inc(page_in[4], 16)
            for b, p in DEC:
                gather(cache_v, b, p)

            for h in range(H):
                pool.wait_ge(decay_made, h + 1)
                for i in range(NT):
                    blk = WT[:, OFF[i]:OFF[i] + 128]
                    link(pool.affine_select(out=blk, in_=blk, compare_op=ALU.is_ge, fill=0.0, base=0,
                                            pattern=[[1, 128]], channel_multiplier=-1))
                pool.affine_select(out=WTm[:, 0:NMETA], in_=WTm[:, 0:NMETA], compare_op=ALU.is_ge, fill=0.0, base=0,
                                   pattern=[[1, NMETA]], channel_multiplier=-1).then_inc(decay_masked, 1)
                pool.wait_ge(decay_masked, h + 1)

            k = 0
            for j in (0, 1, 2, 3, 4):
                n = nrows(j)
                k += 1
                rsqrt(rr8[0:n, :], ss8[0:n, :], DV, sums_ready, k)
                if j:
                    m = nrows(j - 1)
                    rsqrt(rr[0:m, 5 + j - 1:5 + j], ss[0:m, 5 + j - 1:5 + j], D, squares, NTILES + j)
            rsqrt(rr[0:N4, 9:10], ss[0:N4, 9:10], D, squares, 2 * NTILES)

            pool.wait_ge(pos_ready, 1)
            pool.wait_ge(zero_out, 32)
            for j in range(NTILES):
                n = nrows(j)
                for c in range(2):
                    pool.indirect_dma_start(slot_rows, bass.IndirectOffsetOnAxis(ap=POS[0:n, c, j:j + 1], axis=0),
                                            HO[0:n, j, :], None).then_inc(scattered, 16)

            def store(i, s):
                pool.wait_ge(y0[s], i + 1)
                pool.wait_ge(y1[s], i + 1)
                pool.dma_start(slot_out[bass.DynSlice((2 * i + s) * 128, 128), :], YO[s]).then_inc(y_out[s], 16)

            for s in range(2):
                store(0, s)
            with pool.Fori(1, PAIRS // 2) as i:
                for s in range(2):
                    store(i, s)
            for s in range(2):
                pool.wait_ge(y_out[s], 16 * (PAIRS // 2))
            more = pool.value_load(TE[0:1, XBLOCKS:XBLOCKS + 1], min_val=0, max_val=XBLOCKS)
            with pool.If(more > 0):
                with pool.Fori(PAIRS // 2, (PAIRS + XPAIRS) // 2) as i:
                    for s in range(2):
                        store(i, s)
                for s in range(2):
                    pool.wait_ge(y_out[s], 16 * ((PAIRS + XPAIRS) // 2))
            def fetch(j):
                n = nrows(j)
                for c in range(2):
                    if j >= 2:
                        pool.wait_ge(y_free, j - 1)
                    pool.indirect_dma_start(YG[c][j % 2][0:n], None, slot_out,
                                            bass.IndirectOffsetOnAxis(ap=POS[0:n, c, j:j + 1], axis=0))\
                        .then_inc(y_in[2 * (j % 2) + c], 16)
            fetch(0)
            fetch(1)
            for j in range(NTILES):
                if j + 2 < NTILES:
                    fetch(j + 2)
                n = nrows(j)
                rsqrt(rr[0:n, 10 + j:11 + j], ss[0:n, 10 + j:11 + j], D, fsq, j + 1)

        @block.scalar
        def _(act):
            steps = [0]

            def link(ins):
                steps[0] += 1
                ins.then_inc(act_step, 1)
                act.wait_ge(act_step, steps[0])

            act.dma_start(gmix[:, :], norm_mix[0].rearrange("(p k) -> p k", k=KC)).then_inc(gmix_in, 16)
            small = [(gffn[:, :], norm_ffn[0].rearrange("(p k) -> p k", k=KC)),
                     (bgi[:, :], b_gates[0, 0:H].rearrange("(h a) -> h a", a=1)),
                     (bgf[:, :], b_gates[0, H:2 * H].rearrange("(h a) -> h a", a=1)),
                     (wr[:, :, 0:NGRP], w_group[0].rearrange("(p k) n -> p k n", k=KC)),
                     (wr[:, :, NGRP:], w_router[0].rearrange("(p k) n -> p k n", k=KC)),
                     (br[:, 0:NGRP], b_group[0].partition_broadcast(128)),
                     (br[:, NGRP:], b_router[0].partition_broadcast(128)),
                     (gm[:, :], head_norm_m[0].partition_broadcast(128)),
                     (gda[:, :], head_norm_da[0].partition_broadcast(128)),
                     (nold[S0:N4], state_n[0]),
                     (dr[S0:N4, 0:4], state_m[0])]
            small += [(lamv[:, n, :], v[0].partition_broadcast(128))
                      for n, v in enumerate((lambda_q1, lambda_k1, lambda_q2, lambda_k2))]
            g = w_in[0].rearrange("(p k) n -> p k n", k=KC)[:, :, W_COLS["gates"]:W_COLS["gates"] + 8]
            act.wait_ge(wg_zeroed, 1)
            act.dma_start(wg[:, :, 0:H], g[:, :, 0:H]).then_inc(const_in, 16)
            act.dma_start(wg[:, :, 32:32 + H], g[:, :, H:2 * H]).then_inc(const_in, 16)
            act.wait_ge(dr_zeroed, 1)
            assert len(small) + 2 == NCONST
            for dst, src in small:
                act.dma_start(dst, src, allow_slow_non_contiguous=True).then_inc(const_in, 16)

            for j in range(NTILES):
                n = nrows(j)
                act.wait_ge(x_in[j], 16 if j < NT else 32)
                if j:
                    act.wait_ge(squares, j)
                act.activation(junk[0:n, :], X[0:n, j, :], ACT.Square, accum_out=ss[0:n, j:j + 1]).then_inc(squares, 1)
            act.wait_ge(zeroed, 1)
            act.dma_start(slot_rows[0:DUMP].rearrange("(t p) n -> p t n", p=128),
                          zrow[:, None, :].to_broadcast([128, DUMP // 128, D])).then_inc(zero_out, 16)
            act.dma_start(slot_out[DUMP:GROWS], zrow[:, :]).then_inc(zero_out, 16)
            act.wait_ge(const_in, 16 * NCONST)

            def copy(dst, src, scale=1.0):
                return act.activation(dst, src, ACT.Copy, scale=scale)

            for item in ORDER:
                kind = item[0]
                if kind == "gates":
                    after(act, item, "t")
                    after(act, item, "p")
                    act.activation(rI[:, 0:N4], PS["p"][0:H, 0:N4], ACT.Identity, bias=bgi[:, :])
                    act.activation(rI[:, N4:TOK], PS["t"][0:H, :], ACT.Identity, bias=bgi[:, :])
                    act.activation(rF[:, 0:N4], PS["p"][32:32 + H, 0:N4], ACT.Identity, bias=bgf[:, :]).then_inc(freed["p"], 1)
                    act.activation(rF[:, N4:TOK], PS["t"][32:32 + H, :], ACT.Identity, bias=bgf[:, :]).then_inc(freed["t"], 1)
                    drained(act, item, "t")
                    link(act.activation(rE[:, :], rF[:, :], ACT.Abs))
                    link(act.activation(rE[:, :], rE[:, :], ACT.Exp, scale=-1.0))
                    act.activation(rE[:, :], rE[:, :], ACT.Ln, bias=1.0).then_inc(rows_ln, 1)
                elif kind == "acc":
                    b, m = item[1:]
                    after(act, item, "a%d" % (m % 2))
                    src = PS["a%d" % (m % 2)]
                    if b in FEATURE:
                        scale = DQ ** -0.5 if b == "dq" or (b == "mqk" and m >= 2) else 1.0
                        ins = copy(feat[b][:, m, 0:512], src[:, :], scale)
                    elif b == "dv":
                        ins = copy(DVt[:, m, :], src[:, :])
                    elif b == "mv":
                        ins = copy(MVA[:, m, :, 0:DV], src[:, :].rearrange("p (h d) -> p h d", d=DV))
                    else:
                        if m == 0:
                            act.wait_ge(vpage_used, 16)
                        ins = act.activation(MO[:, m, :], src[:, :], ACT.Exp, scale=-1.0)
                    ins.then_inc(freed["a%d" % (m % 2)], 1)
                elif kind == "small":
                    b = item[1]
                    after(act, item, "t")
                    src = PS["t"][:, 0:4 * N4].rearrange("p (m t) -> p m t", t=N4)
                    if b == "mqk":
                        link(copy(mqkT[:, 0:2, 512:TOK], src[:, 0:2]))
                        ins = copy(mqkT[:, 2:4, 512:TOK], src[:, 2:4], DQ ** -0.5)
                    elif b in FEATURE:
                        ins = copy(feat[b][:, :, 512:TOK], src, DQ ** -0.5 if b == "dq" else 1.0)
                    else:
                        ins = copy(vT4[:, ("dv", "mv", "mo").index(b)], src)
                    ins.then_inc(freed["t"], 1)
                elif kind == "tok":
                    name, j = item[1:]
                    n = nrows(j)
                    k = count(*item) - 1
                    after(act, item, "p")
                    src = PS["p"][0:n, :]
                    if name in ("dq", "dk"):
                        if name == "dk":
                            act.wait_ge(tok_out, 16 * j)
                            act.wait_ge(dq_out, 16)
                        ins = copy(tokst[k % 2][0:n], src)
                    elif name == "mq":
                        act.wait_ge(tok_out, 16 * 6)
                        act.wait_ge(dk_out, 16)
                        ins = copy(MQ4, src[:, 0:256])
                    elif name == "mk":
                        ins = copy(MK[0:n, j, :], src[:, 0:256])
                    elif name == "dv":
                        ins = copy(DVt[0:n, T4, :], src)
                    elif name == "mv":
                        ins = copy(MVA[0:n, T4, :, 0:DV], src.rearrange("p (h d) -> p h d", d=DV))
                    else:
                        ins = act.activation(MO[0:n, T4, :], src, ACT.Exp, scale=-1.0)
                    ins.then_inc(freed["p"], 1)
                elif kind == "rows":
                    act.wait_ge(rows_scan, 3)
                    link(act.activation(R[32:32 + H, :], rA[:, :], ACT.Exp, bias=negG))
                    link(copy(R[32:32 + H, S0:N4], rF[:, S0:N4]))
                    act.activation(R[64:64 + H, :], rM[:, :], ACT.Exp, scale=-1.0).then_inc(rows_exp, 1)
                    after(act, item, "t")
                    copy(RC[:, 0:NT, :], PS["t"][:, 0:NT * 68].rearrange("p (j r) -> p j r", r=68))
                    copy(RC[0:N4, T4, :], PS["t"][0:N4, NT * 68:NTILES * 68]).then_inc(freed["t"], 1)
                    act.wait_ge(lam_sum, 1)
                    act.activation(lam[:, 2:4], lam[:, 0:2], ACT.Exp).then_inc(lam_exp, 1)
                elif kind == "decscore":
                    act.wait_ge(dec_max, 1)
                    act.activation(Sq[:, 0:PAST + 1], Sq[:, 0:PAST + 1], ACT.Exp, bias=dcol[:, 1:2],
                                   accum_out=dcol[:, 2:3]).then_inc(dec_exp, 1)
                elif kind == "qk":
                    j, h = item[1:]
                    n = 128 if j < NT else NMETA
                    w = 128 * (j + 1) + NMETA if j < NT else NMETA
                    u = UIDX[j, h]
                    act.wait_ge(maxed, u + 1)
                    P = P2[u % 2]
                    act.activation(P[0:n, 0, 0:w], Sps[0:n, 0, 0:w], ACT.Exp, bias=sums[0:n, 0:1], accum_out=sums[0:n, 2:3])
                    act.activation(P[0:n, 1, 0:w], Sps[0:n, 1, 0:w], ACT.Exp, bias=sums[0:n, 1:2],
                                   accum_out=sums[0:n, 3:4]).then_inc(freed["S"], 1)
                elif kind == "tp":
                    j, h = item[1:]
                    n = 128 if j < NT else NMETA
                    after(act, item, "p")
                    if j < NT:
                        after(act, item, "t")
                        copy(AT[:, 0:j + 1, 0:n], PS["t"][:, 0:128 * (j + 1)].rearrange("p (b t) -> p b t", t=128))\
                            .then_inc(freed["t"], 1)
                    copy(AT[0:NMETA, 4, 0:n], PS["p"][0:NMETA, 0:n]).then_inc(freed["p"], 1)
                elif kind == "pv":
                    j, h = item[1:]
                    n = 128 if j < NT else NMETA
                    after(act, item, "p")
                    act.activation(HO[0:n, j, 512 + DV * h:512 + DV * (h + 1)], PS["p"][0:n, 0:DV], ACT.Copy,
                                   scale=rsum[0:n, UIDX[j, h]:UIDX[j, h] + 1]).then_inc(freed["p"], 1)
                elif kind == "mqk_s":
                    h = item[1]
                    if h == 0:
                        act.wait_ge(g_in, 16)
                    else:
                        drained(act, ("mpv", h - 1), "a1")
                    for i in range(NT):
                        act.activation(WT[:, OFF[i]:OFF[i] + 512 - 128 * i], GB[:, h, N4 + 128 * i:TOK], ACT.Exp,
                                       scale=-1.0, bias=RC[:, i, h:h + 1])
                    act.activation(WTm[:, 0:NMETA], GB[0:NMETA, h, 0:NMETA], ACT.Exp, scale=-1.0, bias=RC[0:NMETA, T4, h:h + 1])
                    act.activation(WTm[:, N4:TOK], GB[0:NMETA, h, N4:TOK], ACT.Exp, scale=-1.0,
                                   bias=RC[0:NMETA, T4, h:h + 1]).then_inc(decay_made, 1)
                elif kind == "mdec":
                    act.wait_ge(dm_ready, 1)
                    act.activation(dr[S0:N4, 8:16], dr[S0:N4, 16:24], ACT.Exp).then_inc(dm_exp, 1)
                    act.activation(dr[S0:N4, 24:28], dr[S0:N4, 4:8], ACT.Exp, scale=-1.0).then_inc(dm_exp, 1)
                elif kind == "cfin":
                    after(act, item, "t")
                    copy(cfin, PS["t"][:, 0:H * DQ].rearrange("p (h d) -> p h d", d=DQ))
                    copy(nfin, PS["t"][0:1, 256:512]).then_inc(freed["t"], 1)
                elif kind == "wo" and item[2] == 1:
                    j = item[1]
                    n = nrows(j)
                    drained(act, item, "a1")
                    act.wait_ge(squares, NTILES + j)
                    act.activation(junk2[0:n, :], X[0:n, j, :], ACT.Square,
                                   accum_out=ss[0:n, 5 + j:6 + j]).then_inc(squares, 1)
                elif kind == "rank":
                    act.wait_ge(gexp_in, 1)
                    act.activation(Gx, Gx, ACT.Exp).then_inc(gexp, 1)
                    act.wait_ge(gexp_in, 2)
                    act.activation(c5[5], c5[4], ACT.Exp).then_inc(gexp, 1)

            def silu(i, s):
                act.wait_ge(gu_filled[s], i + 1)
                reuse(act, act_done[s], i)
                act.activation(SG[s], PS["t" if s else "p"][:, 0:DE], ACT.Silu).then_inc(silu_done[s], 1)

            def pair(i, s):
                silu(i, s)
                act.wait_ge(at_filled[s], i + 1)
                reuse(act, dn_filled[s], i)
                copy(aT[s], Sps[:, 1, 512:768].rearrange("p (f t) -> p f t", t=128)).then_inc(at_evac[s], 1)
                act.wait_ge(dn_filled[s], i + 1)
                reuse(act, y_out[s], 16 * i)
                copy(YO[s][:, 0:512], Sps[:, 0, 0:512]).then_inc(y0[s], 1)

            for s in range(2):
                pair(0, s)
            with act.Fori(1, PAIRS // 2) as i:
                for s in range(2):
                    pair(i, s)
            act.wait_ge(table_ready, 1)
            more = act.value_load(TE[0:1, XBLOCKS:XBLOCKS + 1], min_val=0, max_val=XBLOCKS)
            with act.If(more > 0):
                with act.Fori(PAIRS // 2, (PAIRS + XPAIRS) // 2) as i:
                    for s in range(2):
                        pair(i, s)
            for j in range(NTILES):
                n = nrows(j)
                act.wait_ge(x2_ready, j + 1)
                if j:
                    act.wait_ge(fsq, j)
                act.activation(junk2[0:n, :], X[0:n, j, :], ACT.Square,
                               accum_out=ss[0:n, 10 + j:11 + j]).then_inc(fsq, 1)

        @block.vector
        def _(dve):
            v = nc.vector
            steps = [0]

            def link(ins):
                steps[0] += 1
                ins.then_inc(dve_step, 1)
                dve.wait_ge(dve_step, steps[0])

            v.memset(X[0:N4, T4, :], 0.0).then_inc(pad_zeroed, 1)
            v.memset(wg[:, :, :], 0.0).then_inc(wg_zeroed, 1)
            v.memset(zrow[:, :], 0.0).then_inc(zeroed, 1)
            link(v.memset(R[:, :], 0.0))
            link(v.memset(padT[:, :, :], 0.0))
            link(v.memset(MVA[:, :, :, DV:DV + 1], 1.0))
            dve.wait_ge(const_made, 1)
            dve.wait_ge(ptab_in, 16)
            link(v.tensor_copy(pfl[:, :], pidx[:, :]))
            v.tensor_scalar(pages[:, :], pages[:, :], float(PAGE), pfl[:, :], ALU.mult, ALU.add).then_inc(pages_ready, 1)
            for c in range(2):
                link(v.tensor_scalar(dump[:, c, :], valid[:, :], -1.0, 1.0, ALU.mult, ALU.add))
                link(v.tensor_scalar(c1[:, :], pfl[:, :], float(DUMP + 64 * c), None, ALU.add))
                link(v.tensor_scalar(dump[:, c, :], dump[:, c, :], c1[:, :], None, ALU.mult))

            def transposed(item, src_banks, g, j):
                n = nrows(j)
                for half in range(2):
                    b, src = src_banks[half]
                    if b is not None:
                        after(dve, item, b)
                    o = hT[:, 4 * half:4 * half + 4, col(j):col(j) + n]
                    s_ = src[:, :].rearrange("p (k t) -> p k t", t=128)[:, :, 0:n]
                    if g is None:
                        ins = v.tensor_copy(o, s_)
                    else:
                        ins = v.tensor_tensor(o, s_, g[:, 4 * half:4 * half + 4, None].to_broadcast([128, 4, n]), ALU.mult)
                    if b in ("a0", "a1"):
                        ins.then_inc(freed[b], 1)
                    elif half == 1:
                        ins.then_inc(freed["S"], 1)

            def tbanks(item):
                if banks_of(item) == ("a0", "a1"):
                    return [("a0", bank[0]), ("a1", bank[1])]
                return [("S", Sps[:, 0, 0:512]), (None, Sps[:, 0, 512:1024])]

            kdec = [0]
            for item in ORDER:
                kind = item[0]
                if kind == "xt":
                    j = item[1]
                    n = nrows(j)
                    dve.wait_ge(rsq, j + 1)
                    if j == 0:
                        dve.wait_ge(gmix_in, 16)
                    v.tensor_scalar(hn[j % 2][0:n], X[0:n, j, :], rr[0:n, j:j + 1], None, ALU.mult).then_inc(hn_ready, 1)
                    transposed(item, tbanks(item), gmix, j)
                elif kind == "gates":
                    dve.wait_ge(const_in, 16 * NCONST)
                    link(v.tensor_tensor(lamv[:, 0, :], lamv[:, 0, :], lamv[:, 1, :], ALU.mult))
                    link(v.tensor_tensor(lamv[:, 1, :], lamv[:, 2, :], lamv[:, 3, :], ALU.mult))
                    v.tensor_reduce(lam[:, 0:2], lamv[:, 0:2, :], AX.X, ALU.add).then_inc(lam_sum, 1)
                    dve.wait_ge(rows_ln, 1)
                    link(v.scalar_tensor_tensor(rF, rF, 0.0, rE, ALU.min, ALU.subtract))
                    link(v.memset(rE, 1.0))
                    link(v.tensor_copy(rB, rF))
                    link(v.memset(rB[:, NMETA:N4], 0.0))
                    link(v.tensor_tensor_scan(rB, rE, rB, 0.0, ALU.mult, ALU.add))
                    link(v.tensor_tensor(rA, rI, rB, ALU.subtract))
                    link(v.memset(rA[:, NMETA:N4], -1e30))
                    v.tensor_tensor_scan(rG, rE, rA, 0.0, ALU.mult, ALU.max).then_inc(rows_scan, 1)
                    dve.wait_ge(rows_scan, 1)
                    v.tensor_tensor(rM, rB, rG, ALU.add).then_inc(rows_scan, 1)
                    link(v.tensor_scalar(negG, rG[:, TOK - 1:TOK], -1.0, None, ALU.mult))
                    dve.wait_ge(rows_scan, 2)
                    link(v.tensor_copy(R[0:H, :], rA))
                    v.tensor_copy(R[0:H, S0:N4], rI[:, S0:N4]).then_inc(rows_scan, 1)
                elif kind == "rows":
                    dve.wait_ge(lam_exp, 1)
                    dve.wait_ge(g_out, 16)
                    dve.wait_ge(m_out, 16)
                    dve.wait_ge(rows_exp, 1)
                    link(v.tensor_tensor(lam[:, 4:5], lam[:, 3:4], lam[:, 2:3], ALU.subtract))
                    link(v.tensor_scalar(lam[:, 4:5], lam[:, 4:5], -LAM_INIT, None, ALU.add))
                    link(v.tensor_scalar(sgi[:, :], pidx[0:64, :], 1, None, ALU.bitwise_and))
                    link(v.tensor_copy(sgn[:, 0:1], sgi[:, :]))
                    link(v.tensor_scalar(sgn[:, 1:2], lam[0:64, 4:5], -1.0, None, ALU.add))
                    link(v.tensor_tensor(sgn[:, 2:3], sgn[:, 0:1], sgn[:, 1:2], ALU.mult))
                    link(v.tensor_scalar(sgn[:, 3:4], sgn[:, 2:3], 1.0, None, ALU.add))
                    link(v.tensor_scalar(gda[:, :], gda[:, :], 1.0 - LAM_INIT, None, ALU.mult))
                    link(v.memset(HO[0:S0, T4, :], 0.0))
                    v.nop().then_inc(rows_free, 1)
                elif kind == "decscore":
                    for n, (b, p) in enumerate(DEC):
                        dve.wait_ge(page_in[n % 4], 16 * (n // 4 + 1))
                        if p == 0:
                            dve.wait_ge(page_in[4], 16 * (b + 1))
                        link(v.tensor_tensor(kring[n % 4], kring[n % 4], kring[4], ALU.mult))
                        v.tensor_reduce(Sd[:, p, 8 * b:8 * b + 8], kring[n % 4].rearrange("p (u d) -> p u d", d=DQ),
                                        AX.X, ALU.add).then_inc(page_used, 1)
                    dve.wait_ge(qk64_in, 32)
                    link(v.tensor_tensor(qk64[:, 0, :], qk64[:, 0, :], qk64[:, 1, :], ALU.mult))
                    link(v.tensor_reduce(Sq[:, PAST:PAST + 1], qk64[:, 0, :], AX.X, ALU.add))
                    after(dve, item, "t")
                    v.tensor_copy(Sq[:, 0:PAST], PS["t"][0:64, 0:PAST]).then_inc(freed["t"], 1)
                    drained(dve, item, "t")
                    v.tensor_reduce(dcol[:, 1:2], Sq[:, 0:PAST + 1], AX.X, ALU.max, negate=True).then_inc(dec_max, 1)
                    dve.wait_ge(dec_exp, 1)
                    link(v.reciprocal(dcol[:, 3:4], dcol[:, 2:3]))
                    link(v.tensor_tensor(dcol[:, 3:4], dcol[:, 3:4], sgn[:, 3:4], ALU.mult))
                    v.tensor_scalar(Sq[:, 0:PAST + 1], Sq[:, 0:PAST + 1], dcol[:, 3:4], None, ALU.mult).then_inc(dec_coef, 1)
                elif kind == "decmix":
                    after(dve, item, "p")
                    v.tensor_reduce(Wd[:, :, :], PS["p"][:, 0:128].rearrange("p (a r m) -> p a r m", a=NPAGES, m=2),
                                    AX.X, ALU.add).then_inc(freed["p"], 1)
                    after(dve, item, "t")
                    v.tensor_copy(padT[:, :, S0:N4], PS["t"][:, 0:32].rearrange("p (b h) -> p h b", h=H)).then_inc(freed["t"], 1)
                    dve.wait_ge(decps_in, 16)
                    link(v.tensor_reduce(dr[S0:N4, 48:52], dr[S0:N4, 40:48].rearrange("p (h m) -> p h m", m=2), AX.X, ALU.add))
                    drained(dve, ("tok", "dv", T4), "p")
                    after(dve, item, "p2")
                    for h in range(H):
                        ins = v.scalar_tensor_tensor(HO[S0:N4, T4, 512 + DV * h:512 + DV * (h + 1)],
                                                     DVt[S0:N4, T4, DV * h:DV * (h + 1)], dr[S0:N4, 48 + h:49 + h],
                                                     PS["p"][S0:N4, DV * h:DV * (h + 1)], ALU.mult, ALU.add)
                    ins.then_inc(freed["p"], 1)
                elif kind == "qk":
                    j, h = item[1:]
                    u = UIDX[j, h]
                    n = 128 if j < NT else NMETA
                    w = 128 * (j + 1) + NMETA if j < NT else NMETA
                    d0 = 128 * j if j < NT else 0
                    P = P2[u % 2]
                    after(dve, item, "S")
                    diag = Sps[0:n, :, d0:d0 + n]
                    link(v.tensor_tensor(diag, diag, maskneg[0:n, None, 0:n].to_broadcast([n, 2, n]), ALU.add))
                    v.tensor_reduce(sums[0:n, 0:2], Sps[0:n, :, 0:w], AX.X, ALU.max, negate=True).then_inc(maxed, 1)
                    drained(dve, item, "S")
                    link(v.reciprocal(sums[0:n, 4:6], sums[0:n, 2:4]))
                    link(v.tensor_copy(rsum[0:n, u:u + 1], sums[0:n, 4:5]))
                    link(v.scalar_tensor_tensor(sums[0:n, 6:7], sums[0:n, 2:3], lam[0:n, 4:5], sums[0:n, 5:6], ALU.mult, ALU.mult))
                    v.scalar_tensor_tensor(P[0:n, 0, 0:w], P[0:n, 1, 0:w], sums[0:n, 6:7], P[0:n, 0, 0:w],
                                           ALU.mult, ALU.add).then_inc(mixed, 1)
                elif kind == "mqk_s":
                    h = item[1]
                    dve.wait_ge(decay_masked, h + 1)
                    after(dve, item, "S")
                    for i in range(NT):
                        ins = v.tensor_tensor(WT[:, OFF[i]:OFF[i] + 512 - 128 * i], WT[:, OFF[i]:OFF[i] + 512 - 128 * i],
                                              Sps[:, i // 2, 512 * (i % 2):512 * (i % 2) + 512 - 128 * i], ALU.mult)
                    ins.then_inc(freed["S"], 1)
                    after(dve, item, "t")
                    v.tensor_tensor(WTm[:, N4:TOK], WTm[:, N4:TOK], PS["t"][0:NMETA, :], ALU.mult).then_inc(freed["t"], 1)
                    after(dve, item, "p")
                    v.tensor_tensor(WTm[:, 0:NMETA], WTm[:, 0:NMETA], PS["p"][0:NMETA, 0:NMETA], ALU.mult).then_inc(freed["p"], 1)
                elif kind == "mpv":
                    h = item[1]
                    for b, jj, n in (("a0", (0, 3), 128), ("a1", (3, 4), 128), ("a1", (4, 5), NMETA)):
                        after(dve, item, b)
                        o = 129 * (jj[0] - (3 if b == "a1" else 0))
                        k = jj[1] - jj[0]
                        src = PS[b][0:n, o:o + 129 * k].rearrange("p (j d) -> p j d", d=129)
                        dd = src[:, :, DV:DV + 1]
                        link(v.scalar_tensor_tensor(den[0:n, 0:k, :], dd, -1.0, RC[0:n, jj[0]:jj[1], 64 + h:65 + h],
                                                    ALU.mult, ALU.max))
                        link(v.tensor_tensor(den[0:n, 0:k, :], den[0:n, 0:k, :], dd, ALU.max))
                        link(v.reciprocal(den[0:n, 0:k, :], den[0:n, 0:k, :]))
                        ins = v.tensor_tensor(HO[0:n, jj[0]:jj[1], DV * h:DV * (h + 1)], src[:, :, 0:DV],
                                              den[0:n, 0:k, :].to_broadcast([n, k, DV]), ALU.mult)
                        if b == "a0" or jj[0] == 4:
                            ins.then_inc(freed[b], 1)
                            drained(dve, item, b)
                        else:
                            link(ins)
                elif kind == "mdec":
                    r8 = slice(S0, N4)
                    ig, lf = RC[r8, T4, 0:4], RC[r8, T4, 32:36]
                    dve.wait_ge(const_in, 16 * NCONST)
                    link(v.tensor_tensor(dr[r8, 28:32], dr[r8, 0:4], lf, ALU.add))
                    link(v.tensor_tensor(dr[r8, 4:8], dr[r8, 28:32], ig, ALU.max))
                    link(v.tensor_tensor(dr[r8, 16:20], dr[r8, 28:32], dr[r8, 4:8], ALU.subtract))
                    v.tensor_tensor(dr[r8, 20:24], ig, dr[r8, 4:8], ALU.subtract).then_inc(dm_ready, 1)
                    dve.wait_ge(dm_exp, 2)
                    v.nop().then_inc(dw_made, 1)
                    drained(dve, ("tok", "mq", T4), "p")
                    drained(dve, ("tok", "mk", T4), "p")
                    q = MQ4[r8].rearrange("p (h d) -> p h d", d=DQ)
                    k = MK[r8, T4, :].rearrange("p (h d) -> p h d", d=DQ)
                    link(v.tensor_tensor(nnew[r8], q, k, ALU.mult))
                    link(v.tensor_reduce(dr[r8, 32:36], nnew[r8], AX.X, ALU.add))
                    link(v.tensor_tensor(nnew[r8], q, nold[r8], ALU.mult))
                    link(v.tensor_reduce(dr[r8, 36:40], nnew[r8], AX.X, ALU.add))
                    link(v.tensor_tensor(dr[r8, 32:36], dr[r8, 32:36], dr[r8, 12:16], ALU.mult))
                    link(v.tensor_tensor(dr[r8, 36:40], dr[r8, 36:40], dr[r8, 8:12], ALU.mult))
                    link(v.tensor_tensor(dr[r8, 36:40], dr[r8, 36:40], dr[r8, 32:36], ALU.add))
                    link(v.scalar_tensor_tensor(dr[r8, 60:64], dr[r8, 36:40], -1.0, dr[r8, 24:28], ALU.mult, ALU.max))
                    link(v.tensor_tensor(dr[r8, 36:40], dr[r8, 36:40], dr[r8, 60:64], ALU.max))
                    link(v.reciprocal(dr[r8, 36:40], dr[r8, 36:40]))
                    link(v.tensor_tensor(dr[r8, 52:56], dr[r8, 32:36], dr[r8, 36:40], ALU.mult))
                    link(v.tensor_tensor(dr[r8, 56:60], dr[r8, 8:12], dr[r8, 36:40], ALU.mult))
                    link(v.tensor_tensor(nold[r8], nold[r8], dr[r8, 8:12, None].to_broadcast([NDEC, H, DQ]), ALU.mult))
                    link(v.tensor_tensor(nnew[r8], k, dr[r8, 12:16, None].to_broadcast([NDEC, H, DQ]), ALU.mult))
                    v.tensor_tensor(nnew[r8], nnew[r8], nold[r8], ALU.add).then_inc(cn_ready, 1)
                    dve.wait_ge(st_in, 16)
                    dve.wait_ge(qb_in, 16)
                    link(v.tensor_tensor(QB, QB, C0, ALU.mult))
                    v.tensor_reduce(cq[:, :], QB, AX.X, ALU.add).then_inc(qb_used, 1)
                    dve.wait_ge(qb_used, 1)
                    after(dve, ("decmix",), "p2")
                    v.tensor_copy(padT[:, :, S0:N4], cq[:, :].rearrange("p (b h) -> p h b", h=H)).then_inc(pad_ready, 1)
                    after(dve, item, "t")
                    for h in range(H):
                        link(v.tensor_scalar(HO[r8, T4, DV * h:DV * (h + 1)], PS["t"][r8, DV * h:DV * (h + 1)],
                                             dr[r8, 56 + h:57 + h], None, ALU.mult))
                    v.nop().then_inc(freed["t"], 1)
                    for h in range(H):
                        link(v.scalar_tensor_tensor(HO[r8, T4, DV * h:DV * (h + 1)], MVA[r8, T4, h, 0:DV], dr[r8, 52 + h:53 + h],
                                                    HO[r8, T4, DV * h:DV * (h + 1)], ALU.mult, ALU.add))
                    dve.wait_ge(dw_in, 16)
                    dve.wait_ge(kb_in, 16)
                    link(v.tensor_tensor(cq[:, :].rearrange("p (b h) -> p b h", h=H),
                                         vT4[:, 1, :, S0:N4].rearrange("p h b -> p b h"),
                                         dwb[:, 1, :].rearrange("p (b h) -> p b h", h=H), ALU.mult))
                    link(v.tensor_tensor(QB, QB, cq[:, :, None].to_broadcast([128, 32, DQ]), ALU.mult))
                    link(v.tensor_tensor(C0, C0, dwb[:, 0, :, None].to_broadcast([128, 32, DQ]), ALU.mult))
                    v.tensor_tensor(C0, C0, QB, ALU.add).then_inc(cn_ready, 1)
                    for j in range(NTILES):
                        n = 128 if j < NT else NMETA
                        link(v.tensor_tensor(MK[0:n, j, :].rearrange("p (h d) -> p h d", d=DQ),
                                             MK[0:n, j, :].rearrange("p (h d) -> p h d", d=DQ),
                                             RC[0:n, j, 32:36, None].to_broadcast([n, H, DQ]), ALU.mult))
                    v.nop().then_inc(wsk_ready, 1)
                    drained(dve, ("acc", "mo", 3), "a1")
                    drained(dve, ("tok", "mo", T4), "p")
                    for ap in (MO[:, 0:NT, :], MO[0:N4, T4, :]):
                        link(v.tensor_scalar(ap, ap, 1.0, None, ALU.add))
                        link(v.reciprocal(ap, ap))
                elif kind == "ot":
                    j = item[1]
                    n = nrows(j)
                    if j == 0:
                        drained(dve, ("pv",) + UNITS[-1], "p")
                    sq = sqd[0:n, :]
                    link(v.tensor_tensor(sq, HO[0:n, j, :], HO[0:n, j, :], ALU.mult))
                    v.tensor_reduce(ss8[0:n, :], sq.rearrange("p (u d) -> p u d", d=DV), AX.X, ALU.add).then_inc(sums_ready, 1)
                    dve.wait_ge(rsq, RSQ8[j])
                    ho = HO[0:n, j, :].rearrange("p (u d) -> p u d", d=DV)
                    link(v.tensor_tensor(ho, ho, rr8[0:n, :, None].to_broadcast([n, 8, DV]), ALU.mult))
                    link(v.tensor_tensor(ho[:, 0:4], ho[:, 0:4], gm[0:n, None, :].to_broadcast([n, 4, DV]), ALU.mult))
                    link(v.tensor_tensor(ho[:, 4:8], ho[:, 4:8], gda[0:n, None, :].to_broadcast([n, 4, DV]), ALU.mult))
                    v.tensor_tensor(HO[0:n, j, 0:512], HO[0:n, j, 0:512], MO[0:n, j, :], ALU.mult).then_inc(ho_ready, 1)
                    transposed(item, tbanks(item), None, j)
                elif kind == "wo":
                    j, half = item[1:]
                    n = nrows(j)
                    b = "a%d" % half
                    after(dve, item, b)
                    xs = X[0:n, j, 512 * half:512 * half + 512]
                    v.tensor_tensor(xs, xs, PS[b][0:n, :], ALU.add).then_inc(freed[b], 1)
                elif kind == "rt":
                    j = item[1]
                    n = nrows(j)
                    dve.wait_ge(rsq, RSQF[j])
                    v.tensor_scalar(HO[0:n, j, :], X[0:n, j, :], rr[0:n, 5 + j:6 + j], None, ALU.mult).then_inc(xn_ready, 1)
                    transposed(item, tbanks(item), gffn, j)
                elif kind == "logit":
                    j = item[1]
                    n = nrows(j)
                    if j == 0:
                        link(v.memset(Lt[:, :, :], 0.0))
                    after(dve, item, "t")
                    v.tensor_tensor(Lt[0:n, j, :], PS["t"][0:n, 0:36], br[0:n, :], ALU.add).then_inc(freed["t"], 1)
                elif kind == "rank":
                    drained(dve, ("logit", T4), "t")
                    b4 = lambda a: a[:, :, None].to_broadcast([128, NTILES, 4])
                    b8 = lambda a: a[:, :, None].to_broadcast([128, NTILES, 8])
                    gl = L[:, :, 0:4]
                    gmax, gsum, v1, v2, dlt, ex, key, p1 = c5[0], c5[1], c5[2], c5[3], c5[4], c5[5], c5[6], c5[7]

                    def first(onehot, vals, best, width, tmp):
                        bw = lambda a: a[:, :, None].to_broadcast([128, NTILES, width])
                        link(v.tensor_tensor(tmp, vals, bw(best), ALU.is_equal))
                        link(v.tensor_tensor(tmp, tmp, kiota[:, None, 0:width].to_broadcast([128, NTILES, width]), ALU.mult))
                        link(v.tensor_reduce(key, tmp, AX.X, ALU.max))
                        link(v.tensor_tensor(onehot, tmp, bw(key), ALU.is_equal))

                    link(v.tensor_reduce(gmax, gl, AX.X, ALU.max))
                    v.tensor_tensor(Gx, gl, b4(gmax), ALU.subtract).then_inc(gexp_in, 1)
                    first(Go, gl, gmax, 4, Gk)
                    t4 = T160.rearrange("p (j g e) -> p j g e", g=4, e=8)
                    link(v.tensor_tensor(t4[:, :, 0], L[:, :, 4:12], b8(Go[:, :, 0]), ALU.mult))
                    for g_ in range(1, 4):
                        link(v.tensor_tensor(t4[:, :, g_], L[:, :, 4 + 8 * g_:12 + 8 * g_], b8(Go[:, :, g_]), ALU.mult))
                    ein, o1, o2, tmp, rest = E8
                    link(v.tensor_tensor(ein, t4[:, :, 0], t4[:, :, 1], ALU.add))
                    link(v.tensor_tensor(ein, ein, t4[:, :, 2], ALU.add))
                    link(v.tensor_tensor(ein, ein, t4[:, :, 3], ALU.add))
                    link(v.tensor_reduce(v1, ein, AX.X, ALU.max))
                    first(o1, ein, v1, 8, tmp)
                    link(v.scalar_tensor_tensor(rest, o1, -3e38, ein, ALU.mult, ALU.add))
                    link(v.tensor_reduce(v2, rest, AX.X, ALU.max))
                    first(o2, rest, v2, 8, tmp)
                    v.tensor_tensor(dlt, v2, v1, ALU.subtract).then_inc(gexp_in, 1)
                    for dst, o in ((M1, o1), (M2, o2)):
                        d4 = dst.rearrange("p (j g e) -> p j g e", g=4, e=8)
                        for g_ in range(4):
                            link(v.tensor_tensor(d4[:, :, g_], o, b8(Go[:, :, g_]), ALU.mult))
                        d3 = dst.rearrange("p (j e) -> p j e", e=32)
                        link(v.tensor_tensor(d3, d3, valid[:, :, None].to_broadcast([128, NTILES, 32]), ALU.mult))
                    v.tensor_tensor(MM, M1, M2, ALU.add).then_inc(m_ready, 1)
                    dve.wait_ge(gexp, 2)
                    link(v.tensor_reduce(gsum, Gx, AX.X, ALU.add))
                    link(v.tensor_scalar(p1, ex, 1.0, None, ALU.add))
                    link(v.tensor_tensor(p1, p1, gsum, ALU.mult))
                    link(v.reciprocal(pw[:, 0, :], p1))
                    link(v.tensor_tensor(pw[:, 1, :], pw[:, 0, :], ex, ALU.mult))
                    after(dve, item, "p")
                    v.tensor_copy(PREF, PS["p"][:, 0:192]).then_inc(freed["p"], 1)
                    drained(dve, item, "p")
                    rank = PREF[:, 0:160].rearrange("p (j e) -> p j e", e=32)
                    cnt = PREF[:, 160:192]
                    extra, xend, dd, one32 = e32[0], e32[1], e32[2], e32[3]
                    cx = CX.rearrange("p (e q) -> p e q", q=MAXQ)
                    link(v.tensor_tensor(cx, cnt[:, :, None].to_broadcast([128, 32, MAXQ]),
                                         qiota[:, None, :].to_broadcast([128, 32, MAXQ]), ALU.is_gt))
                    link(v.tensor_reduce(extra, cx, AX.X, ALU.add))
                    link(v.memset(one32, 1.0))
                    link(v.tensor_tensor_scan(xend, one32, extra, 0.0, ALU.mult, ALU.add))
                    link(v.tensor_tensor(dd, xend, extra, ALU.subtract))
                    link(v.tensor_scalar(dd, dd, float(SLOTS), float(XROW - SLOTS), ALU.mult, ALU.add))
                    link(v.tensor_tensor(dd, dd, eiota[:, :], ALU.subtract))
                    t3 = T160.rearrange("p (j e) -> p j e", e=32)
                    link(v.tensor_scalar(t3, rank, float(SLOTS), None, ALU.is_ge))
                    link(v.tensor_tensor(t3, t3, dd[:, None, :].to_broadcast([128, NTILES, 32]), ALU.mult))
                    link(v.tensor_tensor(t3, t3, rank, ALU.add))
                    link(v.tensor_tensor(t3, t3, eiota[:, None, :].to_broadcast([128, NTILES, 32]), ALU.add))
                    for c, m_ in enumerate((M1, M2)):
                        link(v.tensor_tensor(m_, m_, T160, ALU.mult))
                        link(v.tensor_reduce(c5[8 + c], m_.rearrange("p (j e) -> p j e", e=32), AX.X, ALU.add))
                        link(v.tensor_tensor(POS[:, c, :], c5[8 + c], dump[:, c, :], ALU.add))
                    v.nop().then_inc(pos_ready, 1)
                    x3 = XT32[0:1, :].rearrange("p (x e) -> p x e", e=32)
                    link(v.tensor_tensor(x3, xend[0:1, None, :].to_broadcast([1, XBLOCKS, 32]),
                                         xiota[:, :, None].to_broadcast([1, XBLOCKS, 32]), ALU.is_le))
                    link(v.tensor_reduce(xf[0:1, 0:XBLOCKS], x3, AX.X, ALU.add))
                    link(v.tensor_scalar(TE[0:1, 0:XBLOCKS], xf[0:1, 0:XBLOCKS], float(NEXP - 1), None, ALU.min))
                    link(v.tensor_copy(TE[0:1, XBLOCKS:XBLOCKS + 1], xend[0:1, 31:32]))
                    v.nop().then_inc(table_ready, 1)

            def pair(i, s):
                dve.wait_ge(xt_filled[s], i + 1)
                reuse(dve, gu_filled[s], i)
                for half in range(2):
                    ins = v.tensor_tensor(xT[s][:, 4 * half:4 * half + 4, :],
                                          bank[half][:, :].rearrange("p (k t) -> p k t", t=128),
                                          gffn[:, 4 * half:4 * half + 4, None].to_broadcast([128, 4, 128]), ALU.mult)
                ins.then_inc(xt_evac[s], 1)
                dve.wait_ge(silu_done[s], i + 1)
                reuse(dve, at_filled[s], i)
                v.tensor_tensor(AB[s], SG[s], PS["t" if s else "p"][:, DE:2 * DE], ALU.mult).then_inc(act_done[s], 1)
                dve.wait_ge(dn_filled[s], i + 1)
                reuse(dve, y_out[s], 16 * i)
                v.tensor_copy(YO[s][:, 512:1024], Sps[:, 0, 512:1024]).then_inc(y1[s], 1)

            def finish(j):
                n = nrows(j)
                dve.wait_ge(rsq, 3 * NTILES + j + 1)
                if j == 0:
                    dve.wait_ge(gfin_in, 16)
                link(v.tensor_scalar(X[0:n, j, :], X[0:n, j, :], rr[0:n, 10 + j:11 + j], None, ALU.mult))
                v.tensor_tensor(X[0:n, j, :], X[0:n, j, :], gfin[0:n], ALU.mult).then_inc(yfin, 1)

            for s in range(2):
                pair(0, s)
            with dve.Fori(1, PAIRS // 2) as i:
                for s in range(2):
                    pair(i, s)
            more = dve.value_load(TE[0:1, XBLOCKS:XBLOCKS + 1], min_val=0, max_val=XBLOCKS)
            with dve.If(more > 0):
                with dve.Fori(PAIRS // 2, (PAIRS + XPAIRS) // 2) as i:
                    for s in range(2):
                        pair(i, s)
            for j in range(NTILES):
                n = nrows(j)
                for c in range(2):
                    dve.wait_ge(y_in[2 * (j % 2) + c], 16 * (j // 2 + 1))
                    ins = v.scalar_tensor_tensor(X[0:n, j, :], YG[c][j % 2][0:n], pw[0:n, c, j:j + 1], X[0:n, j, :],
                                                 ALU.mult, ALU.add)
                    if c == 0:
                        link(ins)
                    else:
                        ins.then_inc(x2_ready, 1)
                dve.wait_ge(x2_ready, j + 1)
                v.nop().then_inc(y_free, 1)
                if j:
                    finish(j - 1)
            finish(T4)

        @block.tensor
        def _(pe):
            def transpose_rows(rows, item, j):
                n = nrows(j)
                names = banks_of(item)
                for half in range(2):
                    b = names[half] if len(names) == 2 else "S"
                    if half == 0 or b != "S":
                        before(pe, item, b)
                    dst = bank[half][:, :] if b != "S" else Sps[:, 0, 512 * half:512 * half + 512]
                    for k in range(4):
                        mm = pe.transpose(dst[:, 128 * k:128 * k + n], rows[0:n, 4 * half + k:D:KC], ident[0:n, 0:n])
                    if b != "S" or half == 1:
                        mm.then_inc(filled[b], 1)

            for item in ORDER:
                kind = item[0]
                if kind == "xt":
                    j = item[1]
                    if j == 0:
                        pe.wait_ge(ident_made, 1)
                    pe.wait_ge(hn_ready, j + 1)
                    transpose_rows(hn[j % 2], item, j)
                elif kind == "gates":
                    for j in range(NTILES):
                        drained(pe, ("xt", j), banks_of(("xt", j))[-1])
                    pe.wait_ge(const_in, 16 * NCONST)
                    before(pe, item, "t")
                    before(pe, item, "p")
                    for b, c0, c1_ in (("t", 0, 512), ("p", 512, TOK)):
                        for k in range(KC):
                            mm = pe.matmul(PS[b][0:36, 0:c1_ - c0], wg[:, k, :], hT[:, k, c0:c1_],
                                           start=(k == 0), stop=(k == KC - 1))
                        mm.then_inc(filled[b], 1)
                elif kind == "acc":
                    b, m = item[1:]
                    r = "a%d" % (m % 2)
                    n = BLOCKS.index(b)
                    w = blkslot[n % 3]
                    if m == 0:
                        pe.wait_ge(block_in[n % 3], 16 * (n // 3 + 1))
                    before(pe, item, r)
                    for k in range(KC):
                        if b in FEATURE:
                            mm = pe.matmul(PS[r][:, :], w[:, k, 128 * m:128 * (m + 1)], hT[:, k, 0:512],
                                           start=(k == 0), stop=(k == KC - 1))
                        else:
                            mm = pe.matmul(PS[r][:, :], hT[:, k, 128 * m:128 * (m + 1)], w[:, k, :],
                                           start=(k == 0), stop=(k == KC - 1))
                    mm.then_inc(filled[r], 1)
                elif kind == "small":
                    b = item[1]
                    w = blkslot[BLOCKS.index(b) % 3]
                    before(pe, item, "t")
                    for m in range(4):
                        for k in range(KC):
                            mm = pe.matmul(PS["t"][:, N4 * m:N4 * (m + 1)], w[:, k, 128 * m:128 * (m + 1)],
                                           hT[:, k, 512:TOK], start=(k == 0), stop=(k == KC - 1))
                    mm.then_inc(filled["t"], 1)
                    pe.wait_ge(filled["t"], NTH[item, "t"] + 1)
                    pe.nop().then_inc(block_used, 1)
                elif kind == "tok":
                    name, j = item[1:]
                    n = nrows(j)
                    before(pe, item, "p")
                    blk = {"mq": "mqk", "mk": "mqk"}.get(name, name)
                    drained(pe, ("small", blk), "t")
                    if blk in FEATURE:
                        drained(pe, ("acc", blk, 2), "a0")
                        drained(pe, ("acc", blk, 3), "a1")
                        src = {"mq": mqkT[:, 0:2], "mk": mqkT[:, 2:4]}.get(name)
                        src = feat[blk] if src is None else src
                        src = src[:, :, col(j):col(j) + n]
                    else:
                        src = vT4[:, ("dv", "mv", "mo").index(name)]
                    for m in range(src.shape[1]):
                        mm = pe.transpose(PS["p"][0:n, 128 * m:128 * (m + 1)], src[:, m, :], ident[:, :])
                    mm.then_inc(filled["p"], 1)
                elif kind == "rows":
                    pe.wait_ge(rows_exp, 1)
                    pe.wait_ge(rows_scan, 3)
                    before(pe, item, "t")
                    for j in range(NTILES):
                        n = nrows(j)
                        c0 = N4 + 128 * j if j < NT else 0
                        mm = pe.transpose(PS["t"][0:n, 68 * j:68 * (j + 1)], R[0:68, c0:c0 + n], ident[0:68, 0:68])
                    mm.then_inc(filled["t"], 1)
                elif kind == "decscore":
                    pe.wait_ge(page_used, len(DEC))
                    before(pe, item, "t")
                    for p in range(NPAGES):
                        mm = pe.transpose(PS["t"][0:64, 128 * p:128 * (p + 1)], Sd[:, p, :], ident[:, :])
                    mm.then_inc(filled["t"], 1)
                elif kind == "decmix":
                    pe.wait_ge(dec_coef, 1)
                    before(pe, item, "p")
                    for p in range(NPAGES):
                        mm = pe.transpose(PS["p"][:, 64 * p:64 * (p + 1)], Sq[:, 128 * p:128 * (p + 1)], ident[0:64, 0:64])
                    mm.then_inc(filled["p"], 1)
                    drained(pe, item, "p")
                    before(pe, item, "t")
                    for b in range(NDEC):
                        for p in range(NPAGES):
                            n = 16 + b * NPAGES + p
                            pe.wait_ge(page_in[n % 4], 16 * (n // 4 + 1))
                        for h in range(H):
                            for p in range(NPAGES):
                                n = 16 + b * NPAGES + p
                                mm = pe.matmul(PS["t"][:, b * H + h:b * H + h + 1], kring[n % 4][:, DV * h:DV * (h + 1)],
                                               Wd[:, p, b * H + h:b * H + h + 1], start=(p == 0), stop=(p == NPAGES - 1))
                        if b < NDEC - 1:
                            mm.then_inc(vpage_used, 2)
                        else:
                            mm.then_inc(filled["t"], 1)
                    drained(pe, item, "t")
                    pe.nop().then_inc(vpage_used, 2)
                    before(pe, item, "p2")
                    for h in range(H):
                        mm = pe.transpose(PS["p"][0:N4, DV * h:DV * (h + 1)], padT[:, h, :], ident[:, :])
                    mm.then_inc(filled["p"], 1)
                elif kind == "qk":
                    j, h = item[1:]
                    n = 128 if j < NT else NMETA
                    c0 = col(j)
                    before(pe, item, "S")
                    if UIDX[j, h] == 0:
                        for b in ("dq", "dk"):
                            drained(pe, ("acc", b, 3), "a1")
                            drained(pe, ("small", b), "t")
                    for m in range(2):
                        r = slice(64 * m, 64 * m + 64)
                        at_ = 0
                        if j < NT:
                            at_ = 128 * (j + 1)
                            pe.matmul(Sps[0:n, m, 0:at_], dqT[r, h, c0:c0 + n], dkT[r, h, 0:at_], start=True, stop=True)
                        mm = pe.matmul(Sps[0:n, m, at_:at_ + NMETA], dqT[r, h, c0:c0 + n], dkT[r, h, 512:512 + NMETA],
                                       start=True, stop=True)
                    mm.then_inc(filled["S"], 1)
                elif kind == "tp":
                    j, h = item[1:]
                    n = 128 if j < NT else NMETA
                    P = P2[UIDX[j, h] % 2]
                    pe.wait_ge(mixed, UIDX[j, h] + 1)
                    before(pe, item, "p")
                    at_ = 128 * (j + 1) if j < NT else 0
                    pe.transpose(PS["p"][0:NMETA, 0:n], P[0:n, 0, at_:at_ + NMETA], ident[0:n, 0:n]).then_inc(filled["p"], 1)
                    if j < NT:
                        before(pe, item, "t")
                        for i in range(j + 1):
                            mm = pe.transpose(PS["t"][:, 128 * i:128 * (i + 1)], P[0:n, 0, 128 * i:128 * (i + 1)], ident[0:n, 0:n])
                        mm.then_inc(filled["t"], 1)
                elif kind == "pv":
                    j, h = item[1:]
                    n = 128 if j < NT else NMETA
                    drained(pe, ("tp", j, h), "p")
                    if UIDX[j, h] == 0:
                        drained(pe, ("acc", "dv", 3), "a1")
                        drained(pe, ("tok", "dv", T4), "p")
                    before(pe, item, "p")
                    mm = pe.matmul(PS["p"][0:n, 0:DV], AT[0:NMETA, 4, 0:n], DVt[0:NMETA, T4, DV * h:DV * (h + 1)],
                                   start=True, stop=(j == T4))
                    for i in range(j + 1) if j < NT else ():
                        mm = pe.matmul(PS["p"][0:n, 0:DV], AT[:, i, 0:n], DVt[:, i, DV * h:DV * (h + 1)],
                                       start=False, stop=(i == j))
                    mm.then_inc(filled["p"], 1)
                elif kind == "mqk_s":
                    h = item[1]
                    r = slice(64 * (h % 2), 64 * (h % 2) + 64)
                    if h == 0:
                        drained(pe, ("acc", "mqk", 3), "a1")
                        drained(pe, ("small", "mqk"), "t")
                    kT, qT = mqkT[r, 2 + h // 2, :], mqkT[r, h // 2, :]
                    for b in ("S", "t", "p"):
                        before(pe, item, b)
                    for i in range(NT):
                        mm = pe.matmul(Sps[:, i // 2, 512 * (i % 2):512 * (i % 2) + 512 - 128 * i],
                                       kT[:, 128 * i:128 * (i + 1)], qT[:, 128 * i:512], start=True, stop=True)
                    mm.then_inc(filled["S"], 1)
                    pe.matmul(PS["t"][0:NMETA, :], kT[:, 512:512 + NMETA], qT[:, 0:512], start=True, stop=True)\
                      .then_inc(filled["t"], 1)
                    pe.matmul(PS["p"][0:NMETA, 0:NMETA], kT[:, 512:512 + NMETA], qT[:, 512:512 + NMETA],
                              start=True, stop=True).then_inc(filled["p"], 1)
                elif kind == "mpv":
                    h = item[1]
                    for b in ("S", "t", "p"):
                        drained(pe, ("mqk_s", h), b)
                    if h == 0:
                        drained(pe, ("acc", "mv", 3), "a1")
                        drained(pe, ("tok", "mv", T4), "p")
                    before(pe, item, "a0")
                    before(pe, item, "a1")
                    for j in range(NTILES):
                        n = 128 if j < NT else NMETA
                        b, o = ("a0", 129 * j) if j < 3 else ("a1", 129 * (j - 3))
                        c0 = N4 + 128 * j if j < NT else 0
                        for i in range(j + 1) if j < NT else ():
                            pe.matmul(PS[b][0:n, o:o + 129], WT[:, OFF[i] + 128 * (j - i):OFF[i] + 128 * (j - i) + 128],
                                      MVA[:, i, h, :], start=(i == 0), stop=False)
                        mm = pe.matmul(PS[b][0:n, o:o + 129], WTm[:, c0:c0 + n], MVA[0:NMETA, T4, h, :],
                                       start=(j == T4), stop=True)
                        if j in (2, 4):
                            mm.then_inc(filled[b], 1)
                elif kind == "mdec":
                    pe.wait_ge(pad_ready, 1)
                    before(pe, item, "t")
                    for h in range(H):
                        mm = pe.transpose(PS["t"][0:N4, DV * h:DV * (h + 1)], padT[:, h, :], ident[:, :])
                    mm.then_inc(filled["t"], 1)
                elif kind == "cfin":
                    pe.wait_ge(wsk_ready, 1)
                    before(pe, item, "t")
                    for h in range(H):
                        for j in range(NTILES):
                            n = 128 if j < NT else NMETA
                            pe.matmul(PS["t"][:, DQ * h:DQ * (h + 1)], MVA[0:n, j, h, 0:DV], MK[0:n, j, DQ * h:DQ * (h + 1)],
                                      start=(j == 0), stop=(j == T4))
                    for j in range(NTILES):
                        n = 128 if j < NT else NMETA
                        mm = pe.matmul(PS["t"][0:1, 256:512], ones[0:n, 0:1], MK[0:n, j, :], start=(j == 0), stop=(j == T4))
                    mm.then_inc(filled["t"], 1)
                elif kind == "ot":
                    j = item[1]
                    pe.wait_ge(ho_ready, j + 1)
                    transpose_rows(HO[:, j, :], item, j)
                elif kind == "wo":
                    j, half = item[1:]
                    n = nrows(j)
                    bidx = 6 + half
                    if j == 0:
                        pe.wait_ge(block_in[bidx % 3], 16 * (bidx // 3 + 1))
                    drained(pe, ("ot", j), "S")
                    b = "a%d" % half
                    before(pe, item, b)
                    for k in range(KC):
                        mm = pe.matmul(PS[b][0:n, :], hT[:, k, col(j):col(j) + n], blkslot[bidx % 3][:, k, :],
                                       start=(k == 0), stop=(k == KC - 1))
                    mm.then_inc(filled[b], 1)
                    if j == T4:
                        pe.wait_ge(filled[b], NTH[item, b] + 1)
                        pe.nop().then_inc(block_used, 1)
                elif kind == "rt":
                    j = item[1]
                    pe.wait_ge(xn_ready, j + 1)
                    transpose_rows(HO[:, j, :], item, j)
                elif kind == "logit":
                    j = item[1]
                    n = nrows(j)
                    drained(pe, ("rt", j), "S")
                    before(pe, item, "t")
                    for k in range(KC):
                        mm = pe.matmul(PS["t"][0:n, 0:36], hT[:, k, col(j):col(j) + n], wr[:, k, :],
                                       start=(k == 0), stop=(k == KC - 1))
                    mm.then_inc(filled["t"], 1)
                elif kind == "rank":
                    pe.wait_ge(m_ready, 1)
                    before(pe, item, "p")
                    for j in range(NTILES + 1):
                        last = min(j, NTILES - 1)
                        for i in range(last + 1):
                            mm = pe.matmul(PS["p"][:, 32 * j:32 * (j + 1)], tri[:, :] if i == j else ones[:, :],
                                           MM[:, 32 * i:32 * (i + 1)], start=(i == 0), stop=(i == last))
                    mm.then_inc(filled["p"], 1)

            def pair(i, s):
                pe.wait_ge(xg_in[s], 16 * i + 16)
                reuse(pe, xt_evac[1 - s], i + s)
                for k in range(KC):
                    mm = pe.transpose(bank[k // 4][:, 128 * (k % 4):128 * (k % 4) + 128], XG[s][:, k:D:KC], ident[:, :])
                mm.then_inc(xt_filled[s], 1)
                pe.wait_ge(xt_evac[s], i + 1)
                reuse(pe, act_done[s], i)
                gu = PS["t" if s else "p"]
                for u in range(2):
                    pe.wait_ge(gu_in[2 * s + u], 32 * i + 32)
                for k in range(KC):
                    for u in range(2):
                        mm = pe.matmul(gu[64 * u:64 * u + 64, :], xT[s][:, k, 64 * u:64 * u + 64],
                                       Wgu[2 * s + u][:, :, k, :], start=(k == 0), stop=(k == KC - 1))
                mm.then_inc(gu_filled[s], 1)
                pe.wait_ge(act_done[s], i + 1)
                reuse(pe, at_evac[1 - s], i + s)
                for f in range(FC):
                    mm = pe.transpose(Sps[:, 1, 512 + 128 * f:640 + 128 * f], AB[s][:, f:DE:FC], ident[:, :])
                mm.then_inc(at_filled[s], 1)
                pe.wait_ge(at_evac[s], i + 1)
                reuse(pe, y0[1 - s], i + s)
                reuse(pe, y1[1 - s], i + s)
                for u in range(2):
                    pe.wait_ge(dn_in[2 * s + u], 16 * i + 16)
                for half in range(2):
                    for f in range(FC):
                        for u in range(2):
                            mm = pe.matmul(Sps[64 * u:64 * u + 64, 0, 512 * half:512 * half + 512],
                                           aT[s][:, f, 64 * u:64 * u + 64],
                                           Wdn[2 * s + u][:, f, 512 * half:512 * half + 512],
                                           start=(f == 0), stop=(f == FC - 1))
                mm.then_inc(dn_filled[s], 1)

            for b in ("a0", "a1", "S", "t", "p"):
                pe.wait_ge(freed[b], TOTAL[b])
            for s in range(2):
                pair(0, s)
            with pe.Fori(1, PAIRS // 2) as i:
                for s in range(2):
                    pair(i, s)
            pe.wait_ge(table_ready, 1)
            more = pe.value_load(TE[0:1, XBLOCKS:XBLOCKS + 1], min_val=0, max_val=XBLOCKS)
            with pe.If(more > 0):
                with pe.Fori(PAIRS // 2, (PAIRS + XPAIRS) // 2) as i:
                    for s in range(2):
                        pair(i, s)


_INS = ["x_prompt", "x_sample", "cache_k", "cache_v", "state_C", "state_n", "state_m", "page_table", "meta_tokens",
        "norm_mix", "w_in", "b_gates", "head_norm_m", "lambda_q1", "lambda_k1", "lambda_q2", "lambda_k2",
        "head_norm_da", "w_out", "norm_ffn", "w_group", "b_group", "w_router", "b_router", "w_gate_e", "w_up_e",
        "w_down_e", "norm_final"]
_OUTS = [(1, SEQ, D), (NDEC, 1, D), (1, 1, NMETA + SEQ, H, 2 * DQ), (1, 1, NMETA + SEQ, H, DV), (1, 1, H, DV, DQ),
         (1, 1, H, DQ), (1, 1, H), (1, NDEC, 1, H, 2 * DQ), (1, NDEC, 1, H, DV), (1, NDEC, H, DV, DQ),
         (1, NDEC, H, DQ), (1, NDEC, H)]


def kernel(**inputs):
    import numpy as _np
    import concourse.bacc as _bacc
    from concourse.bass_utils import run_bass_kernel_spmd as _run

    nc = _bacc.Bacc("TRN2", target_bir_lowering=False, num_devices=1)
    arrays, args = {}, []
    for name in _INS:
        a = _np.ascontiguousarray(inputs[name])
        arrays["in_" + name] = a
        args.append(nc.dram_tensor("in_" + name, a.shape, mybir.dt.from_np(a.dtype), kind="ExternalInput").ap())
    for i, shape in enumerate(_OUTS):
        args.append(nc.dram_tensor("out_%d" % i, shape, mybir.dt.float32, kind="ExternalOutput").ap())
    build(nc, *args)
    r = _run(nc, [arrays], core_ids=[0])
    return tuple(r.results[0]["out_%d" % i] for i in range(len(_OUTS)))
```

```python
import math
from contextlib import ExitStack

import concourse.bass as bass
from concourse import mybir

D = 1024
SEQ = 512
NMETA = 16
NDEC = 8
PAST = 256
PAGE = 128
NPAGES = PAST // PAGE
NPOOL = 20
H = 4
DQ = 64
DV = 128
NEXP = 32
NGRP = 4
EPG = NEXP // NGRP
DE = 256
KC = D // 128
FC = DE // 128
EPS = 1e-6
LAM_INIT = 0.8 - 0.6 * math.exp(-0.3 * 0)

NT = SEQ // 128
T4 = NT
S0 = 32
N4 = S0 + NDEC
TOK = SEQ + N4
NTILES = NT + 1

SLOTS = 64
PAIRS = NEXP // 2
ASSIGN = 2 * (SEQ + NMETA + NDEC)
XBLOCKS = (ASSIGN - 1) // SLOTS
XPAIRS = (XBLOCKS + 3) // 4 * 2
XBLOCKS = 2 * XPAIRS
XROW = NEXP * SLOTS
DUMP = XROW + XBLOCKS * SLOTS
GROWS = DUMP + 128
MAXQ = (SEQ + NMETA + NDEC) // SLOTS

W_COLS = dict(mqk=0, mv=512, mo=1024, gates=1536, dq=1544, dk=2056, dv=2568)
BLOCKS = ["dq", "dk", "dv", "mqk", "mv", "mo", "wo0", "wo1"]
PROJ = BLOCKS[:6]
FEATURE = ("dq", "dk", "mqk")
UNITS = [(j, h) for j in (4, 0, 1, 2, 3) for h in range(H)]


def nrows(j):
    return 128 if j < NT else N4


def col(j):
    return 128 * j


def schedule():
    order = [("xt", j) for j in range(NTILES)] + [("gates",)]

    def block(b):
        items = [("acc", b, m) for m in range(4)] + [("small", b)]
        if b != "dv" and b != "mo":
            items += [("ft", b)]
        if b == "dk":
            items += [("tok", "dk", j) for j in range(NT)]
        if b == "mqk":
            items += [("tok", "mk", j) for j in range(NT)]
        return items

    order += block("dq") + [("decscore",)] + block("dk") + [("rows",)] + block("dv") + [("decsm",)]
    back = block("mqk") + [("decmix",)] + block("mv") + block("mo")
    prev = None
    for n, u in enumerate(UNITS):
        order.append(("qk",) + u)
        take = math.ceil(len(back) / (len(UNITS) - n))
        order += back[:take]
        back = back[take:]
        if prev:
            order += [("tp",) + prev, ("pv",) + prev]
        prev = u
    order += [("mqk_s", 0), ("tp",) + prev, ("pv",) + prev, ("mdec1",)]
    order += [("mqk_s", 1), ("mpv", 0), ("mqk_s", 2), ("mpv", 1), ("mdec2",), ("mqk_s", 3), ("mpv", 2), ("sig",), ("mpv", 3)]
    order += [("ot", 0)]
    for j in range(NTILES):
        if j < T4:
            order += [("ot", j + 1)]
        order += [("wo", j, 0), ("wo", j, 1)] if j < T4 else [("wo", T4, 0)]
        order += {0: [("wsk",)], 1: [("cfin",)], 2: [("mdec3",)]}.get(j, [])
        if j:
            order += [("rt", j - 1), ("logit", j - 1)]
    order += [("rt", 4), ("logit", 4), ("rank",)]
    return order


ORDER = schedule()


def banks_of(item):
    kind = item[0]
    if kind == "xt":
        return ("a0", "a1") if item[1] % 2 == 0 else ("Sa",)
    if kind == "acc":
        return ("a%d" % (item[2] % 2),)
    if kind == "wo":
        return ("a%d" % item[2],)
    if kind == "tp":
        return ("t", "p") if item[1] < NT else ("p",)
    return {"ot": ("Sa",), "rt": ("Sb",), "gates": ("t", "p"), "small": ("t",), "ft": ("p",), "tok": ("p",),
            "rows": ("t",), "decsm": ("t",), "decmix": ("p", "t", "p2", "t2"), "qk": ("Sa", "Sb"), "pv": ("p",),
            "mqk_s": ("Sa", "Sb", "t", "p"), "mpv": ("a0", "a1"), "mdec2": ("t",), "cfin": ("t",),
            "logit": ("t",), "rank": ("p",)}.get(kind, ())


def fillings():
    count, nth = {}, {}
    for item in ORDER:
        for b in banks_of(item):
            region = b.rstrip("2")
            nth[item, b] = count.get(region, 0)
            count[region] = count.get(region, 0) + 1
    return nth, count


NTH, TOTAL = fillings()
NCONST = 17
NFIN = 5 + XPAIRS
RSQ8 = [6, 7, 9, 11, 13]
RSQF = [8, 10, 12, 14, 15]
OFF = [0, 512, 896, 1152]


def build(nc, x_prompt, x_sample, cache_k, cache_v, state_C, state_n, state_m, page_table, meta_tokens,
          norm_mix, w_in, b_gates, head_norm_m, lambda_q1, lambda_k1, lambda_q2, lambda_k2, head_norm_da,
          w_out, norm_ffn, w_group, b_group, w_router, b_router, w_gate_e, w_up_e, w_down_e, norm_final,
          y_prompt, y_sample, k_prompt, v_prompt, C_prompt, n_prompt, m_prompt, k_sample, v_sample,
          C_sample, n_sample, m_sample):
    f32, i32, u32 = mybir.dt.float32, mybir.dt.int32, mybir.dt.uint32
    ALU, ACT, AX = mybir.AluOpType, mybir.ActivationFunctionType, mybir.AxisListType
    ctx = ExitStack()
    with ctx:
        def sb(name, shape, dt=f32):
            return ctx.enter_context(nc.sbuf_tensor(name, shape, dt))

        def sem(name):
            return ctx.enter_context(nc.semaphore(name))

        def dram(name, shape):
            return nc.dram_tensor(name, shape, f32, kind="Internal").ap()

        tok_rows = dram("tok_rows", (TOK, D))
        slot_tok = nc.dram_tensor("slot_tok", (GROWS, 1), i32, kind="Internal").ap()
        slot_out = dram("slot_out", (DUMP, D))
        dec_q, dec_k = dram("dec_q", (NDEC, 512)), dram("dec_k", (NDEC, 512))
        dec_mq, dec_mk = dram("dec_mq", (NDEC, 256)), dram("dec_mk", (NDEC, 256))
        dec_w = dram("dec_w", (2, NDEC, H))
        dec_ps = dram("dec_ps", (NDEC * 8,))
        g_rows = dram("g_rows", (H, TOK))

        X = sb("X", [128, NTILES, D])
        HO = sb("HO", [128, NTILES, D])
        hT = sb("hT", [128, KC, TOK])
        WS = sb("WS", [128, 18432])
        FT = sb("FT", [128, 12 * TOK])
        DVt = sb("DVt", [128, NTILES, H * DV])
        MVA = sb("MVA", [128, NTILES, H, DV + 1])
        MO = sb("MO", [128, NTILES, H * DV])
        MK = sb("MK", [128, NTILES, H * DQ])
        ident, ones, tri = sb("ident", [128, 128]), sb("ones", [128, 128]), sb("tri", [128, 128])
        maskneg = sb("maskneg", [128, 128])
        gm, gda = sb("gm", [128, DV]), sb("gda", [128, DV])
        gmix, gffn = sb("gmix", [128, KC]), sb("gffn", [128, KC])
        wr = sb("wr", [128, KC, NGRP + NEXP])
        wg = sb("wg", [128, KC, 36])
        br = sb("br", [128, NGRP + NEXP])
        bgi, bgf = sb("bgi", [H, 1]), sb("bgf", [H, 1])
        lamv = sb("lamv", [128, 4, DQ])
        lam = sb("lam", [128, 6])
        neghalf = sb("neghalf", [128, 8])
        ss, rr = sb("ss", [128, 16]), sb("rr", [128, 16])
        ss8, rr8 = sb("ss8", [128, 8]), sb("rr8", [128, 8])
        RC = sb("RC", [128, NTILES, 68])
        sgn, sgi = sb("sgn", [64, 4]), sb("sgi", [64, 1], i32)
        rsum = sb("rsum", [128, NTILES * H])
        den = sb("den", [128, 3, 1])
        negG_t, c1 = sb("negG", [H, 1]), sb("c1", [128, 1])
        negG = negG_t[:, :]
        nold = sb("nold", [N4, H, DQ])
        cq, dwb = sb("cq", [128, NDEC * H]), sb("dwb", [128, 2, NDEC * H])
        Lt = sb("Lt", [128, NTILES, NGRP + NEXP])
        xf = sb("xf", [1, XBLOCKS])
        pidx = sb("pidx", [128, 1], i32)
        pfl = sb("pfl", [128, 1])
        vT4 = sb("vT4", [128, 4, N4])
        cfin_t = sb("cfin", [128, H, DQ])
        mask1, mask2 = sb("mask1", [128, H]), sb("mask2", [128, H])
        sel = sb("sel", [128, N4])
        tokid = sb("tokid", [128, NTILES], i32)
        zint = sb("zint", [128, GROWS // 128], i32)
        SL = [sb("SL%d" % n, [128, 1], i32) for n in range(2)]
        sums = sb("sums", [128, 8])
        pages = sb("pages", [128, NDEC * NPAGES], i32)
        Sd = sb("Sd", [128, NPAGES, 64])
        Sq = sb("Sq", [64, PAST + 4])
        Wd = sb("Wd", [128, NPAGES, 32])
        dcol = sb("dcol", [64, 8])
        padT = sb("padT", [128, H, N4])
        qk64 = sb("qk64", [64, 2, DQ])
        dr = sb("dr", [N4, 64])

        dqT = FT[:, 0:4 * TOK].rearrange("p (m t) -> p m t", t=TOK)
        dkT = FT[:, 4 * TOK:8 * TOK].rearrange("p (m t) -> p m t", t=TOK)
        mqkT = FT[:, 8 * TOK:12 * TOK].rearrange("p (m t) -> p m t", t=TOK)
        feat = {"dq": dqT, "dk": dkT, "mqk": mqkT}
        hn = [HO[:, 0, :], HO[:, 1, :]]
        tokst = [HO[:, n // 2, 512 * (n % 2):512 * (n % 2) + 512] for n in range(6)]
        blkslot = [WS[:, 4096 * s:4096 * (s + 1)].rearrange("p (k n) -> p k n", n=512) for s in range(3)]
        SC = WS[:, 12288:18432]
        GB = SC[:, 0:H * TOK].rearrange("p (h t) -> p h t", t=TOK)
        WTs = [(SC[:, o:o + 1280], SC[0:NMETA, o + 1280:o + 1280 + TOK]) for o in (2208, 4040)]
        P2 = [SC[:, o:o + 2 * 528].rearrange("p (m s) -> p m s", m=2) for o in (2208, 4040)]
        zeros = SC[:, 5888:6144]
        AT = SC[:, 5096:5096 + 640].rearrange("p (b t) -> p b t", t=128)
        R = SC[:, 4040:4040 + TOK]
        junk = SC[:, 0:D]
        hoflat = HO[:, 3:5, :].rearrange("p a b -> p (a b)")
        rB, rE, rF, rI = (SC[0:H, 1824 + TOK * n:1824 + TOK * (n + 1)] for n in range(4))
        rA, rG, rM = (hoflat[0:H, TOK * n:TOK * (n + 1)] for n in range(3))
        MQ4 = wg[:, :, :].rearrange("p a b -> p (a b)")[0:N4, 0:256]
        nnew = Sq[0:N4, 0:256].rearrange("p (h d) -> p h d", d=DQ)
        cfin = cfin_t[:, :, :]
        nfin = lamv[:, :, :].rearrange("p a b -> p (a b)")[0:1, 0:256]
        gfin = MK[:, :, :].rearrange("p a b -> p (a b)")[:, 0:D]
        kring = [MO[:, n, :] for n in range(5)]
        C0 = WS[:, 8192:8192 + 2048].rearrange("p (b d) -> p b d", d=DQ)
        QB = WS[:, 10240:10240 + 2048].rearrange("p (b d) -> p b d", d=DQ)
        dvflat = DVt[:, :, :].rearrange("p a b -> p (a b)")
        sqd, junk2 = dvflat[:, 0:D], dvflat[:, D:2 * D]

        bank = [ctx.enter_context(nc.psum_tensor("bank%d" % n, [128, 512], f32)) for n in (0, 1)]
        Sps = ctx.enter_context(nc.psum_tensor("scores", [128, 2, 1024], f32))
        pt_, pp_ = (ctx.enter_context(nc.psum_tensor(n, [128, 512], f32)) for n in ("bank_t", "bank_p"))
        PS = {"a0": bank[0], "a1": bank[1], "t": pt_, "p": pp_}

        filled = {b: sem("filled_" + b) for b in ("a0", "a1", "Sa", "Sb", "t", "p")}
        freed = {b: sem("freed_" + b) for b in ("a0", "a1", "Sa", "Sb", "t", "p")}
        x_in = [sem("x_in%d" % j) for j in range(NTILES)]
        const_in, const_made, pad_zeroed = sem("const_in"), sem("const_made"), sem("pad_zeroed")
        gmix_in, ident_made, dr_zeroed, wg_zeroed = sem("gmix_in"), sem("ident_made"), sem("dr_zeroed"), sem("wg_zeroed")
        gfin_in = sem("gfin_in")
        block_in = [sem("block_in%d" % s) for s in range(3)]
        block_used = sem("block_used")
        squares = sem("squares")
        rsq = sem("rsq")
        sums_ready = sem("sums_ready")
        hn_ready = sem("hn_ready")
        act_step, dve_step, pool_step, sp_step = (sem(n) for n in ("act_step", "dve_step", "pool_step", "sp_step"))
        rows_ln = sem("rows_ln")
        rows_scan = sem("rows_scan")
        rows_exp = sem("rows_exp")
        g_out, g_in, m_out = sem("g_out"), sem("g_in"), sem("m_out")
        tok_out = sem("tok_out")
        sel_made = sem("sel_made")
        dq_out, dk_out, dm_out = sem("dq_out"), sem("dk_out"), sem("dm_out")
        v_out = sem("v_out")
        fin_out = sem("fin_out")
        page_in = [sem("page_in%d" % n) for n in range(5)]
        page_used = sem("page_used")
        vpage_used = sem("vpage_used")
        pages_ready, ptab_in = sem("pages_ready"), sem("ptab_in")
        qk64_in = sem("qk64_in")
        dec_max, dec_exp, dec_coef, dec_mixed = sem("dec_max"), sem("dec_exp"), sem("dec_coef"), sem("dec_mixed")
        decps_out, decps_in = sem("decps_out"), sem("decps_in")
        pad_ready = sem("pad_ready")
        maxed, mixed = sem("maxed"), sem("mixed")
        lam_sum, lam_exp = sem("lam_sum"), sem("lam_exp")
        decay_made, decay_masked, decay_used, product = (sem(n) for n in (
            "decay_made", "decay_masked", "decay_used", "product"))
        st_in, dw_made, dw_out, dw_in, qb_in, qb_used, kb_in, cn_ready = (sem(n) for n in (
            "st_in", "dw_made", "dw_out", "dw_in", "qb_in", "qb_used", "kb_in", "cn_ready"))
        dm_ready, dm_exp = sem("dm_ready"), sem("dm_exp")
        wsk_ready = sem("wsk_ready")
        cfin_ready = sem("cfin_ready")
        ho_ready = sem("ho_ready")
        x2_ready, xn_ready = sem("x2_ready"), sem("xn_ready")
        zero_made = sem("zero_made")
        zero_out, xrow_out = sem("zero_out"), sem("xrow_out")
        ids_in = [sem("ids_in%d" % n) for n in range(2)]
        gexp_in, gexp = sem("gexp_in"), sem("gexp")
        m_ready, pos_ready, table_ready = sem("m_ready"), sem("pos_ready"), sem("table_ready")
        scattered = sem("scattered")
        two = lambda n: [sem("%s%d" % (n, s)) for s in range(2)]
        xg_in, xt_filled, xt_evac, gu_filled, silu_done, act_done, at_filled, at_evac, dn_filled, y0, y1, y_out = (
            two(n) for n in ("xg_in", "xt_filled", "xt_evac", "gu_filled", "silu_done", "act_done", "at_filled",
                             "at_evac", "dn_filled", "y_first", "y_second", "y_out"))
        gu_in = [sem("gu_in%d" % n) for n in range(4)]
        dn_in = [sem("dn_in%d" % n) for n in range(4)]
        y_in = [sem("y_in%d" % n) for n in range(4)]
        y_free = sem("y_free")
        fsq, yfin = sem("final_squares"), sem("y_final")

        eslot = [WS[:, 12288:18432], FT[:, 0:6144], WS[:, 0:6144], WS[:, 6144:12288]]
        Wgu = [e[:, 0:4096].rearrange("p (g k n) -> p g k n", g=2, n=DE) for e in eslot]
        Wdn = [e[:, 4096:6144].rearrange("p (f n) -> p f n", n=D) for e in eslot]
        XG = [DVt[:, 0:2, :].rearrange("p a b -> p (a b)"), DVt[:, 2:4, :].rearrange("p a b -> p (a b)")]
        mvflat = MVA[:, :, :, :].rearrange("p a b c -> p (a b c)")
        YO = [mvflat[:, 0:D], mvflat[:, D:2 * D]]
        hflat = hT[:, :, :].rearrange("p k t -> p (k t)")
        xT = [hflat[:, 1024 * s:1024 * (s + 1)].rearrange("p (k t) -> p k t", t=128) for s in range(2)]
        SG = [hflat[:, 2048 + 256 * s:2304 + 256 * s] for s in range(2)]
        AB = [hflat[:, 2560 + 256 * s:2816 + 256 * s] for s in range(2)]
        aT = [hflat[:, 3072 + 256 * s:3328 + 256 * s].rearrange("p (f t) -> p f t", t=128) for s in range(2)]
        moflat = MO[:, :, :].rearrange("p a b -> p (a b)")
        at = [0]

        def piece(n):
            at[0] += n
            return moflat[:, at[0] - n:at[0]]

        L = Lt[:, :, :]
        Gx = piece(20).rearrange("p (j g) -> p j g", g=4)
        Go = piece(20).rearrange("p (j g) -> p j g", g=4)
        Gk = piece(20).rearrange("p (j g) -> p j g", g=4)
        E8 = [piece(40).rearrange("p (j e) -> p j e", e=8) for _ in range(5)]
        T160 = piece(160)
        M1, M2, MM = (piece(160) for _ in range(3))
        c5 = [piece(5) for _ in range(12)]
        PREF = piece(192)
        CX = piece(32 * MAXQ)
        e32 = [piece(32) for _ in range(6)]
        XT32 = piece(XBLOCKS * 32)
        kiota = sb("kiota", [128, 8])
        qiota = sb("qiota", [128, MAXQ])
        eiota = sb("eiota", [128, 32])
        xiota = sb("xiota", [1, XBLOCKS])
        iscr = sb("iscr", [128, 32], i32)
        valid = sb("valid", [128, NTILES])
        dump = sb("dump", [128, 2, NTILES])
        POS = sb("POS", [128, 2, NTILES], u32)
        POSG = sb("POSG", [128, 2, NTILES], u32)
        TE = sb("TE", [1, XBLOCKS + 1], i32)
        pw = sb("pw", [128, 2, NTILES])
        YG = [WS[:, 2048 * n:2048 * n + 1024] for n in range(2)], [WS[:, 2048 * n + 1024:2048 * n + 2048] for n in range(2)]

        def before(eng, item, b):
            if NTH[item, b]:
                eng.wait_ge(freed[b.rstrip("2")], NTH[item, b])

        def after(eng, item, b):
            eng.wait_ge(filled[b.rstrip("2")], NTH[item, b] + 1)

        def drained(eng, item, b):
            eng.wait_ge(freed[b.rstrip("2")], NTH[item, b] + 1)

        def reuse(eng, done, turns):
            if not (isinstance(turns, int) and turns == 0):
                eng.wait_ge(done, turns)

        def count(kind, *rest):
            n = 0
            for item in ORDER:
                if item[0] == kind:
                    n += 1
                    if item[1:] == rest:
                        return n

        def further_blocks(eng):
            return eng.value_load(TE[0:1, XBLOCKS:XBLOCKS + 1], min_val=0, max_val=XBLOCKS)

        def loop_further(eng, more, pair):
            with eng.If(more > 0):
                with eng.Fori(PAIRS // 2, (PAIRS + XPAIRS) // 2) as i:
                    for s in range(2):
                        with eng.If(more > 4 * i + 2 * s - 2 * PAIRS):
                            pair(i, s)

        DEC = [(b, p) for b in range(NDEC) for p in range(NPAGES)]
        UIDX = {u: n for n, u in enumerate(UNITS)}
        block = ctx.enter_context(nc.Block())

        @block.sync
        def _(sp):
            for j in range(NT):
                sp.dma_start(X[:, j, :], x_prompt[0, 128 * j:128 * (j + 1), :]).then_inc(x_in[j], 16)
            sp.wait_ge(pad_zeroed, 1)
            sp.dma_start(X[0:NMETA, T4, :], meta_tokens).then_inc(x_in[T4], 16)
            sp.dma_start(X[S0:N4, T4, :], x_sample[:, 0, :]).then_inc(x_in[T4], 16)

            def load_block(n):
                b = BLOCKS[n]
                if n >= 3:
                    sp.wait_ge(block_used, n - 2)
                src = (w_out[0].rearrange("(p k) n -> p k n", k=KC)[:, :, 512 * int(b[2]):512 * int(b[2]) + 512]
                       if b[:2] == "wo" else
                       w_in[0].rearrange("(p k) n -> p k n", k=KC)[:, :, W_COLS[b]:W_COLS[b] + 512])
                sp.dma_start(blkslot[n % 3], src).then_inc(block_in[n % 3], 16)

            def expert_weights(i, s, u, e):
                w = 2 * s + u
                for g, src in enumerate((w_gate_e, w_up_e)):
                    sp.dma_start(Wgu[w][:, g], src[0, e].rearrange("(p k) n -> p k n", k=KC)).then_inc(gu_in[w], 16)
                sp.dma_start(Wdn[w], w_down_e[0, e].rearrange("(p f) n -> p f n", f=FC)).then_inc(dn_in[w], 16)

            for n in range(3):
                load_block(n)
            for item in ORDER:
                kind = item[0]
                if kind == "small" and PROJ.index(item[1]) + 3 < len(BLOCKS):
                    load_block(PROJ.index(item[1]) + 3)
                if kind == "small":
                    drained(sp, item, "t")
                    if item[1] == "dq":
                        sp.dma_start(dec_q, tokst[0][S0:N4]).then_inc(dq_out, 16)
                    elif item[1] == "dk":
                        s = tokst[1]
                        sp.dma_start(k_prompt[0, 0, 0:NMETA].rearrange("t h d -> t (h d)"),
                                     s[0:NMETA]).then_inc(tok_out, 16)
                        sp.dma_start(k_sample[0, :, 0].rearrange("t h d -> t (h d)"), s[S0:N4]).then_inc(tok_out, 16)
                        sp.dma_start(dec_k, s[S0:N4]).then_inc(dk_out, 16)
                        sp.wait_ge(dk_out, 16)
                        sp.wait_ge(dq_out, 16)
                        sp.dma_start(qk64[:, 0, :], dec_q.rearrange("b (u d) -> (b u) d", d=DQ)).then_inc(qk64_in, 16)
                        sp.dma_start(qk64[:, 1, :], dec_k.rearrange("b (u d) -> (b u) d", d=DQ)).then_inc(qk64_in, 16)
                    elif item[1] == "dv":
                        for i in range(NT):
                            sp.dma_start(v_prompt[0, 0, NMETA + 128 * i:NMETA + 128 * (i + 1)]
                                         .rearrange("t h d -> t (h d)"), DVt[:, i, :]).then_inc(v_out, 16)
                        sp.dma_start(v_prompt[0, 0, 0:NMETA].rearrange("t h d -> t (h d)"),
                                     DVt[0:NMETA, T4, :]).then_inc(v_out, 16)
                        sp.dma_start(v_sample[0, :, 0].rearrange("t h d -> t (h d)"),
                                     DVt[S0:N4, T4, :]).then_inc(v_out, 16)
                    elif item[1] == "mqk":
                        sp.dma_start(dec_mq, MQ4[S0:N4]).then_inc(dm_out, 16)
                        sp.dma_start(dec_mk, MK[S0:N4, T4, :]).then_inc(dm_out, 16)
                elif kind == "tok":
                    name, j = item[1:]
                    if name == "dk":
                        drained(sp, item, "p")
                        sp.dma_start(k_prompt[0, 0, NMETA + 128 * j:NMETA + 128 * (j + 1)]
                                     .rearrange("t h d -> t (h d)"), tokst[2 + j]).then_inc(tok_out, 16)
                elif kind == "rows":
                    sp.wait_ge(rows_scan, 2)
                    sp.dma_start(g_rows, rG).then_inc(g_out, 16)
                    sp.dma_start(m_prompt[0, 0, :].rearrange("(h a) -> h a", a=1), rM[:, TOK - 1:TOK],
                                 allow_slow_non_contiguous=True).then_inc(m_out, 16)
                    sp.wait_ge(g_out, 16)
                    sp.wait_ge(squares, NTILES)
                    sp.dma_start(GB, g_rows.rearrange("h t -> (h t)").partition_broadcast(128)
                                 .rearrange("p (h t) -> p h t", t=TOK)).then_inc(g_in, 16)
                elif kind == "decsm":
                    sp.wait_ge(zero_made, 1)
                    for n in range(XPAIRS):
                        sp.dma_start(slot_out[XROW + 128 * n:XROW + 128 * (n + 1)].rearrange("p (c n) -> p c n", n=256),
                                     zeros[:, None, :].to_broadcast([128, 4, 256])).then_inc(fin_out, 16)
                elif kind == "decmix":
                    sp.wait_ge(dec_coef, 1)
                    sp.dma_start(dec_ps.rearrange("(r a) -> r a", a=1), Sq[:, PAST:PAST + 1],
                                 allow_slow_non_contiguous=True).then_inc(decps_out, 16)
                    sp.wait_ge(decps_out, 16)
                    sp.dma_start(dr[S0:N4, 40:48], dec_ps.rearrange("(b u) -> b u", u=8)).then_inc(decps_in, 16)
                elif kind == "mdec1":
                    sp.wait_ge(block_used, 6)
                    sp.dma_start(C0, state_C[0].rearrange("b h v d -> v (b h) d")).then_inc(st_in, 16)
                    sp.wait_ge(dm_out, 32)
                    sp.dma_start(QB, dec_mq.rearrange("b n -> (b n)").partition_broadcast(128)
                                 .rearrange("p (b d) -> p b d", d=DQ)).then_inc(qb_in, 16)
                    sp.wait_ge(dw_made, 1)
                    sp.dma_start(dec_w[0], dr[S0:N4, 8:12]).then_inc(dw_out, 16)
                    sp.dma_start(dec_w[1], dr[S0:N4, 12:16]).then_inc(dw_out, 16)
                    sp.wait_ge(dw_out, 32)
                    sp.dma_start(dwb[:, :, :], dec_w.rearrange("a b h -> (a b h)").partition_broadcast(128)
                                 .rearrange("p (a b) -> p a b", a=2)).then_inc(dw_in, 16)
                    sp.dma_start(m_sample[0], dr[S0:N4, 4:8]).then_inc(fin_out, 16)
                    sp.wait_ge(qb_used, 1)
                    sp.dma_start(QB, dec_mk.rearrange("b n -> (b n)").partition_broadcast(128)
                                 .rearrange("p (b d) -> p b d", d=DQ)).then_inc(kb_in, 16)
                elif kind == "mdec3":
                    sp.wait_ge(cn_ready, 2)
                    sp.dma_start(C_sample[0].rearrange("b h v d -> v (b h) d"), C0).then_inc(fin_out, 16)
                    sp.dma_start(n_sample[0], nnew[S0:N4]).then_inc(fin_out, 16)
                elif kind == "rt":
                    j = item[1]
                    sp.wait_ge(xn_ready, j + 1)
                    sp.dma_start(tok_rows[128 * j:128 * j + nrows(j)], HO[0:nrows(j), j, :]).then_inc(xrow_out, 16)
                elif kind == "ot" and item[1] == 0:
                    sp.wait_ge(filled["a1"], NTH[("mpv", H - 1), "a1"] + 1)
                    for u in range(2):
                        expert_weights(0, 0, u, u)
                elif kind == "cfin":
                    drained(sp, item, "t")
                    sp.dma_start(C_prompt[0, 0].rearrange("h v d -> v h d"), cfin).then_inc(fin_out, 16)
                    sp.dma_start(n_prompt[0, 0].rearrange("h d -> (h d)").rearrange("(a n) -> a n", a=1),
                                 nfin).then_inc(fin_out, 16)
                    sp.dma_start(gfin, norm_final.partition_broadcast(128)).then_inc(gfin_in, 16)

            def pair_loads(i, s, experts):
                sp.wait_ge(dn_filled[s], i)
                for u in range(2):
                    expert_weights(i, s, u, experts[u])

            sp.wait_ge(fin_out, 16 * NFIN)
            sp.wait_ge(block_used, len(BLOCKS))
            for u in range(2):
                expert_weights(0, 1, u, 2 + u)
            with sp.Fori(1, PAIRS // 2) as i:
                for s in range(2):
                    pair_loads(i, s, [4 * i + 2 * s, 4 * i + 2 * s + 1])
            sp.wait_ge(table_ready, 1)

            def further_pair(i, s):
                ids = [sp.value_load(TE[0:1, bass.DynSlice(4 * i + 2 * s + u - 2 * PAIRS, 1)],
                                     min_val=0, max_val=NEXP - 1) for u in range(2)]
                pair_loads(i, s, ids)

            loop_further(sp, further_blocks(sp), further_pair)

            for n, j in enumerate((0, 1, 2, 3, 4)):
                sp.wait_ge(yfin, n + 1)
                if j < NT:
                    sp.dma_start(y_prompt[0, 128 * j:128 * (j + 1), :], X[:, j, :]).then_inc(fin_out, 16)
                else:
                    sp.dma_start(y_sample[:, 0, :], X[S0:N4, T4, :]).then_inc(fin_out, 16)
            sp.wait_ge(fin_out, 16 * (NFIN + NTILES))
            sp.wait_ge(tok_out, 16 * 6)
            sp.wait_ge(v_out, 16 * 6)

        @block.gpsimd
        def _(pool):
            steps = [0]

            def link(ins):
                steps[0] += 1
                ins.then_inc(pool_step, 1)
                pool.wait_ge(pool_step, steps[0])

            pool.dma_start(pages[:, :], page_table.rearrange("b p -> (b p)").partition_broadcast(128)).then_inc(ptab_in, 16)
            link(pool.memset(dr[:, :], 0.0))
            pool.nop().then_inc(dr_zeroed, 1)
            link(pool.memset(ident[:, :], 0.0))
            link(pool.affine_select(out=ident[:, :], in_=ident[:, :], compare_op=ALU.not_equal, fill=1.0,
                                    base=0, pattern=[[-1, 128]], channel_multiplier=1))
            pool.nop().then_inc(ident_made, 1)
            link(pool.memset(maskneg[:, :], 0.0))
            link(pool.memset(ones[:, :], 1.0))
            link(pool.affine_select(out=maskneg[:, :], in_=maskneg[:, :], compare_op=ALU.is_ge, fill=-1e30,
                                    base=0, pattern=[[-1, 128]], channel_multiplier=1))
            link(pool.affine_select(out=tri[:, :], in_=ones[:, :], compare_op=ALU.is_gt, fill=0.0,
                                    base=0, pattern=[[1, 128]], channel_multiplier=-1))
            link(pool.memset(neghalf[:, :], -0.5))
            link(pool.iota(pidx[:, :], [[0, 1]], base=0, channel_multiplier=1))
            link(pool.iota(iscr[:, 0:8], [[-1, 8]], base=8, channel_multiplier=0))
            link(pool.tensor_copy(kiota[:, :], iscr[:, 0:8]))
            link(pool.iota(iscr[:, 0:MAXQ], [[SLOTS, MAXQ]], base=SLOTS, channel_multiplier=0))
            link(pool.tensor_copy(qiota[:, :], iscr[:, 0:MAXQ]))
            link(pool.iota(iscr[:, 0:32], [[SLOTS, 32]], base=0, channel_multiplier=0))
            link(pool.tensor_copy(eiota[:, :], iscr[:, 0:32]))
            link(pool.iota(iscr[:, 0:XBLOCKS], [[1, XBLOCKS]], base=0, channel_multiplier=0))
            link(pool.tensor_copy(xiota[:, :], iscr[0:1, 0:XBLOCKS]))
            link(pool.memset(zint[:, :], 0))
            pool.dma_start(slot_tok.rearrange("(p a) o -> p (a o)", p=128), zint[:, :]).then_inc(zero_out, 16)
            link(pool.iota(tokid[:, :], [[128, NTILES]], base=0, channel_multiplier=1))
            link(pool.memset(valid[:, 0:NT], 1.0))
            link(pool.memset(valid[:, NT:], 0.0))
            link(pool.memset(valid[0:NMETA, NT:], 1.0))
            link(pool.memset(valid[S0:N4, NT:], 1.0))
            pool.nop().then_inc(const_made, 1)

            roots = [0]

            def decode_masks():
                for m, o in ((mask1, 0), (mask2, 16)):
                    link(pool.memset(m[:, :], 0.0))
                    for g in range(4):
                        link(pool.affine_select(out=m[:, :], in_=m[:, :], compare_op=ALU.not_equal, fill=1.0,
                                                base=-(36 * g + o), pattern=[[-1, H]], channel_multiplier=1))
                link(pool.memset(sel[:, :], 0.0))
                for g in range(4):
                    for h in range(H):
                        link(pool.affine_select(out=sel[:, S0:N4], in_=sel[:, S0:N4], compare_op=ALU.not_equal, fill=1.0,
                                                base=-(32 * g + h), pattern=[[-H, NDEC]], channel_multiplier=1))
                pool.nop().then_inc(sel_made, 1)

            def rsqrt(dst, src, width, wait_sem, wait_val):
                pool.wait_ge(wait_sem, wait_val)
                link(pool.tensor_scalar(dst, src, 1.0 / width, EPS, ALU.mult, ALU.add))
                n = dst.shape[1]
                pool.tensor_tensor(dst, dst, neghalf[0:dst.shape[0], 0:n], ALU.pow).then_inc(rsq, 1)
                roots[0] += 1
                pool.wait_ge(rsq, roots[0])

            for j in range(NTILES):
                n = nrows(j)
                rsqrt(rr[0:n, j:j + 1], ss[0:n, j:j + 1], D, squares, j + 1)

            ring = [0]

            def gather(cache, b, p):
                n = ring[0]
                slot = n % 4
                if n >= 4:
                    if n < 16 + 4:
                        pool.wait_ge(page_used, min(n - 3, 16))
                    if n >= 20:
                        pool.wait_ge(vpage_used, n - 19)
                pool.indirect_dma_start(
                    kring[slot], None, cache[0].rearrange("n t h d -> (n t) (h d)"),
                    bass.IndirectOffsetOnAxis(ap=pages[:, b * NPAGES + p:b * NPAGES + p + 1].bitcast(u32), axis=0))\
                    .then_inc(page_in[slot], 16)
                ring[0] += 1

            pool.wait_ge(pages_ready, 1)
            for n, (b, p) in enumerate(DEC):
                gather(cache_k, b, p)
                if p == 0:
                    if n == 0:
                        pool.wait_ge(dq_out, 16)
                    if b:
                        pool.wait_ge(page_used, 2 * b)
                    pool.dma_start(kring[4], dec_q[b].partition_broadcast(128)).then_inc(page_in[4], 16)
                if n == 3:
                    decode_masks()
            for b, p in DEC:
                gather(cache_v, b, p)

            for h in range(H):
                WT, WTm = WTs[h % 2]
                pool.wait_ge(decay_made, h + 1)
                for i in range(NT):
                    blk = WT[:, OFF[i]:OFF[i] + 128]
                    link(pool.affine_select(out=blk, in_=blk, compare_op=ALU.is_ge, fill=0.0, base=0,
                                            pattern=[[1, 128]], channel_multiplier=-1))
                pool.affine_select(out=WTm[:, 0:NMETA], in_=WTm[:, 0:NMETA], compare_op=ALU.is_ge, fill=0.0, base=0,
                                   pattern=[[1, NMETA]], channel_multiplier=-1).then_inc(decay_masked, 1)
                pool.wait_ge(decay_masked, h + 1)

            k = 0
            for j in (0, 1, 2, 3, 4):
                n = nrows(j)
                k += 1
                rsqrt(rr8[0:n, :], ss8[0:n, :], DV, sums_ready, k)
                if j:
                    m = nrows(j - 1)
                    rsqrt(rr[0:m, 5 + j - 1:5 + j], ss[0:m, 5 + j - 1:5 + j], D, squares, NTILES + j)
            rsqrt(rr[0:N4, 9:10], ss[0:N4, 9:10], D, squares, 2 * NTILES)

            pool.wait_ge(pos_ready, 1)
            pool.wait_ge(zero_out, 16)
            for j in range(NTILES):
                n = nrows(j)
                for c in range(2):
                    pool.indirect_dma_start(slot_tok, bass.IndirectOffsetOnAxis(ap=POS[0:n, c, j:j + 1], axis=0),
                                            tokid[0:n, j:j + 1], None).then_inc(scattered, 16)
            pool.wait_ge(scattered, 16 * 2 * NTILES)
            pool.wait_ge(xrow_out, 16 * NTILES)

            def fetch_rows(i, s):
                reuse(pool, xt_filled[s], i)
                pool.dma_start(SL[s][:, :], slot_tok[bass.DynSlice((2 * i + s) * 128, 128), :]).then_inc(ids_in[s], 16)
                pool.wait_ge(ids_in[s], ids_due[s])
                pool.reg_add(ids_due[s], ids_due[s], 16)
                pool.indirect_dma_start(XG[s], None, tok_rows,
                                        bass.IndirectOffsetOnAxis(ap=SL[s][:, :].bitcast(u32), axis=0)).then_inc(xg_in[s], 16)

            def store(i, s):
                pool.wait_ge(y0[s], i + 1)
                pool.wait_ge(y1[s], i + 1)
                pool.dma_start(slot_out[bass.DynSlice((2 * i + s) * 128, 128), :], YO[s]).then_inc(y_out[s], 16)

            ids_due = [pool.alloc_register("ids_due%d" % s) for s in range(2)]
            for s in range(2):
                pool.reg_mov(ids_due[s], 16)
            for s in range(2):
                fetch_rows(0, s)
            with pool.Fori(1, PAIRS // 2) as i:
                for s in range(2):
                    fetch_rows(i, s)
                    store(i - 1, s)
            for s in range(2):
                store(PAIRS // 2 - 1, s)
            for s in range(2):
                pool.wait_ge(y_out[s], 16 * (PAIRS // 2))
            further = further_blocks(pool)
            def further_pair(i, s):
                fetch_rows(i, s)
                store(i, s)
                pool.wait_ge(y_out[s], 16 * i + 16)
            loop_further(pool, further, further_pair)
            def fetch(j):
                n = nrows(j)
                for c in range(2):
                    if j >= 2:
                        pool.wait_ge(y_free, j - 1)
                    pool.indirect_dma_start(YG[c][j % 2][0:n], None, slot_out,
                                            bass.IndirectOffsetOnAxis(ap=POSG[0:n, c, j:j + 1], axis=0))\
                        .then_inc(y_in[2 * (j % 2) + c], 16)
            fetch(0)
            fetch(1)
            for j in range(NTILES):
                if j + 2 < NTILES:
                    fetch(j + 2)
                n = nrows(j)
                rsqrt(rr[0:n, 10 + j:11 + j], ss[0:n, 10 + j:11 + j], D, fsq, j + 1)

        @block.scalar
        def _(act):
            steps = [0]

            def link(ins):
                steps[0] += 1
                ins.then_inc(act_step, 1)
                act.wait_ge(act_step, steps[0])

            act.dma_start(gmix[:, :], norm_mix[0].rearrange("(p k) -> p k", k=KC)).then_inc(gmix_in, 16)
            small = [(gffn[:, :], norm_ffn[0].rearrange("(p k) -> p k", k=KC)),
                     (bgi[:, :], b_gates[0, 0:H].rearrange("(h a) -> h a", a=1)),
                     (bgf[:, :], b_gates[0, H:2 * H].rearrange("(h a) -> h a", a=1)),
                     (wr[:, :, 0:NGRP], w_group[0].rearrange("(p k) n -> p k n", k=KC)),
                     (wr[:, :, NGRP:], w_router[0].rearrange("(p k) n -> p k n", k=KC)),
                     (br[:, 0:NGRP], b_group[0].partition_broadcast(128)),
                     (br[:, NGRP:], b_router[0].partition_broadcast(128)),
                     (gm[:, :], head_norm_m[0].partition_broadcast(128)),
                     (gda[:, :], head_norm_da[0].partition_broadcast(128)),
                     (nold[S0:N4], state_n[0]),
                     (dr[S0:N4, 0:4], state_m[0])]
            small += [(lamv[:, n, :], v[0].partition_broadcast(128))
                      for n, v in enumerate((lambda_q1, lambda_k1, lambda_q2, lambda_k2))]
            g = w_in[0].rearrange("(p k) n -> p k n", k=KC)[:, :, W_COLS["gates"]:W_COLS["gates"] + 8]
            act.wait_ge(wg_zeroed, 1)
            act.dma_start(wg[:, :, 0:H], g[:, :, 0:H]).then_inc(const_in, 16)
            act.dma_start(wg[:, :, 32:32 + H], g[:, :, H:2 * H]).then_inc(const_in, 16)
            act.wait_ge(dr_zeroed, 1)
            assert len(small) + 2 == NCONST
            for dst, src in small:
                act.dma_start(dst, src, allow_slow_non_contiguous=True).then_inc(const_in, 16)

            for j in range(NTILES):
                n = nrows(j)
                act.wait_ge(x_in[j], 16 if j < NT else 32)
                if j:
                    act.wait_ge(squares, j)
                act.activation(junk[0:n, :], X[0:n, j, :], ACT.Square, accum_out=ss[0:n, j:j + 1]).then_inc(squares, 1)
            act.wait_ge(const_in, 16 * NCONST)

            def copy(dst, src, scale=1.0):
                return act.activation(dst, src, ACT.Copy, scale=scale)

            for item in ORDER:
                kind = item[0]
                if kind == "gates":
                    after(act, item, "t")
                    after(act, item, "p")
                    act.activation(rI[:, 0:N4], PS["p"][0:H, 0:N4], ACT.Identity, bias=bgi[:, :])
                    act.activation(rI[:, N4:TOK], PS["t"][0:H, :], ACT.Identity, bias=bgi[:, :])
                    act.activation(rF[:, 0:N4], PS["p"][32:32 + H, 0:N4], ACT.Identity, bias=bgf[:, :]).then_inc(freed["p"], 1)
                    act.activation(rF[:, N4:TOK], PS["t"][32:32 + H, :], ACT.Identity, bias=bgf[:, :]).then_inc(freed["t"], 1)
                    drained(act, item, "t")
                    link(act.activation(rE[:, :], rF[:, :], ACT.Abs))
                    link(act.activation(rE[:, :], rE[:, :], ACT.Exp, scale=-1.0))
                    act.activation(rE[:, :], rE[:, :], ACT.Ln, bias=1.0).then_inc(rows_ln, 1)
                elif kind == "acc":
                    b, m = item[1:]
                    after(act, item, "a%d" % (m % 2))
                    src = PS["a%d" % (m % 2)]
                    if b in FEATURE:
                        scale = DQ ** -0.5 if b == "dq" or (b == "mqk" and m >= 2) else 1.0
                        ins = copy(feat[b][:, m, 0:512], src[:, :], scale)
                    elif b == "dv":
                        ins = copy(DVt[:, m, :], src[:, :])
                    elif b == "mv":
                        ins = copy(MVA[:, m, :, 0:DV], src[:, :].rearrange("p (h d) -> p h d", d=DV))
                    else:
                        if m == 0:
                            after(act, ("decmix",), "t2")
                        ins = act.activation(MO[:, m, :], src[:, :], ACT.Exp, scale=-1.0)
                    ins.then_inc(freed["a%d" % (m % 2)], 1)
                elif kind == "small":
                    b = item[1]
                    after(act, item, "t")
                    for u in range(2):
                        src = PS["t"][64 * u:64 * u + N4, 0:256]
                        cols = slice(256 * u, 256 * u + 256)
                        if b == "dq":
                            ins = copy(tokst[0][0:N4, cols], src, DQ ** -0.5)
                        elif b == "dk":
                            ins = copy(tokst[1][0:N4, cols], src)
                        elif b == "mqk":
                            ins = copy(MK[0:N4, T4, :], src, DQ ** -0.5) if u else copy(MQ4, src)
                        elif b == "dv":
                            ins = copy(DVt[0:N4, T4, cols], src)
                        elif b == "mv":
                            ins = copy(MVA[0:N4, T4, 2 * u:2 * u + 2, 0:DV], src.rearrange("p (h d) -> p h d", d=DV))
                        else:
                            ins = act.activation(MO[0:N4, T4, cols], src, ACT.Exp, scale=-1.0)
                    ins.then_inc(freed["t"], 1)
                elif kind == "ft":
                    b = item[1]
                    after(act, item, "p")
                    src = PS["p"][:, 0:4 * N4].rearrange("p (m t) -> p m t", t=N4)
                    copy(vT4[:, :, :] if b == "mv" else feat[b][:, :, 512:TOK], src).then_inc(freed["p"], 1)
                elif kind == "tok":
                    name, j = item[1:]
                    after(act, item, "p")
                    if name == "dk":
                        ins = copy(tokst[2 + j], PS["p"][:, :])
                    else:
                        ins = copy(MK[:, j, :], PS["p"][:, 0:256])
                    ins.then_inc(freed["p"], 1)
                elif kind == "rows":
                    act.wait_ge(rows_scan, 3)
                    link(act.activation(R[32:32 + H, :], rA[:, :], ACT.Exp, bias=negG))
                    link(copy(R[32:32 + H, S0:N4], rF[:, S0:N4]))
                    act.activation(R[64:64 + H, :], rM[:, :], ACT.Exp, scale=-1.0).then_inc(rows_exp, 1)
                    after(act, item, "t")
                    copy(RC[:, 0:NT, :], PS["t"][:, 0:NT * 68].rearrange("p (j r) -> p j r", r=68))
                    copy(RC[0:N4, T4, :], PS["t"][0:N4, NT * 68:NTILES * 68]).then_inc(freed["t"], 1)
                    act.wait_ge(lam_sum, 1)
                    act.activation(lam[:, 2:4], lam[:, 0:2], ACT.Exp).then_inc(lam_exp, 1)
                elif kind == "decsm":
                    act.wait_ge(dec_max, 1)
                    act.activation(Sq[:, 0:PAST + 1], Sq[:, 0:PAST + 1], ACT.Exp, bias=dcol[:, 1:2],
                                   accum_out=dcol[:, 2:3]).then_inc(dec_exp, 1)
                elif kind == "qk":
                    j, h = item[1:]
                    n = 128 if j < NT else NMETA
                    w = 128 * (j + 1) + NMETA if j < NT else NMETA
                    u = UIDX[j, h]
                    act.wait_ge(maxed, u + 1)
                    P = P2[u % 2]
                    act.activation(P[0:n, 0, 0:w], Sps[0:n, 0, 0:w], ACT.Exp, bias=sums[0:n, 0:1],
                                   accum_out=sums[0:n, 2:3]).then_inc(freed["Sa"], 1)
                    act.activation(P[0:n, 1, 0:w], Sps[0:n, 1, 0:w], ACT.Exp, bias=sums[0:n, 1:2],
                                   accum_out=sums[0:n, 3:4]).then_inc(freed["Sb"], 1)
                elif kind == "tp":
                    j, h = item[1:]
                    n = 128 if j < NT else NMETA
                    after(act, item, "p")
                    if j < NT:
                        after(act, item, "t")
                        copy(AT[:, 0:j + 1, 0:n], PS["t"][:, 0:128 * (j + 1)].rearrange("p (b t) -> p b t", t=128))\
                            .then_inc(freed["t"], 1)
                    copy(AT[0:NMETA, 4, 0:n], PS["p"][0:NMETA, 0:n]).then_inc(freed["p"], 1)
                elif kind == "pv":
                    j, h = item[1:]
                    n = 128 if j < NT else NMETA
                    after(act, item, "p")
                    if UIDX[j, h] == 0:
                        act.wait_ge(tok_out, 16 * 6)
                    act.activation(HO[0:n, j, 512 + DV * h:512 + DV * (h + 1)], PS["p"][0:n, 0:DV], ACT.Copy,
                                   scale=rsum[0:n, UIDX[j, h]:UIDX[j, h] + 1]).then_inc(freed["p"], 1)
                elif kind == "mqk_s":
                    h = item[1]
                    WT, WTm = WTs[h % 2]
                    if h == 0:
                        act.wait_ge(g_in, 16)
                    if h >= 2:
                        after(act, ("mpv", h - 2), "a1")
                    for i in range(NT):
                        act.activation(WT[:, OFF[i]:OFF[i] + 512 - 128 * i], GB[:, h, N4 + 128 * i:TOK], ACT.Exp,
                                       scale=-1.0, bias=RC[:, i, h:h + 1])
                    act.activation(WTm[:, 0:NMETA], GB[0:NMETA, h, 0:NMETA], ACT.Exp, scale=-1.0, bias=RC[0:NMETA, T4, h:h + 1])
                    act.activation(WTm[:, N4:TOK], GB[0:NMETA, h, N4:TOK], ACT.Exp, scale=-1.0,
                                   bias=RC[0:NMETA, T4, h:h + 1]).then_inc(decay_made, 1)
                elif kind == "mdec1":
                    act.wait_ge(dm_ready, 1)
                    act.activation(dr[S0:N4, 8:16], dr[S0:N4, 16:24], ACT.Exp).then_inc(dm_exp, 1)
                    act.activation(dr[S0:N4, 24:28], dr[S0:N4, 4:8], ACT.Exp, scale=-1.0).then_inc(dm_exp, 1)
                elif kind == "cfin":
                    after(act, item, "t")
                    copy(cfin, PS["t"][:, 0:H * DQ].rearrange("p (h d) -> p h d", d=DQ))
                    copy(nfin, PS["t"][0:1, 256:512]).then_inc(freed["t"], 1)
                elif kind == "wo" and (item[2] == 1 or item[1] == T4):
                    j = item[1]
                    n = nrows(j)
                    drained(act, item, "a%d" % item[2])
                    act.wait_ge(squares, NTILES + j)
                    act.activation(junk2[0:n, :], X[0:n, j, :], ACT.Square,
                                   accum_out=ss[0:n, 5 + j:6 + j]).then_inc(squares, 1)
                elif kind == "rank":
                    act.wait_ge(gexp_in, 1)
                    act.activation(Gx, Gx, ACT.Exp).then_inc(gexp, 1)
                    act.wait_ge(gexp_in, 2)
                    act.activation(c5[5], c5[4], ACT.Exp).then_inc(gexp, 1)

            def silu(i, s):
                act.wait_ge(gu_filled[s], i + 1)
                reuse(act, act_done[s], i)
                act.activation(SG[s], PS["t" if s else "p"][:, 0:DE], ACT.Silu).then_inc(silu_done[s], 1)

            def pair(i, s):
                silu(i, s)
                act.wait_ge(at_filled[s], i + 1)
                reuse(act, dn_filled[s], i)
                copy(aT[s], Sps[:, 1, 512:768].rearrange("p (f t) -> p f t", t=128)).then_inc(at_evac[s], 1)
                act.wait_ge(dn_filled[s], i + 1)
                reuse(act, y_out[s], 16 * i)
                copy(YO[s][:, 0:512], Sps[:, 0, 0:512]).then_inc(y0[s], 1)

            for s in range(2):
                pair(0, s)
            with act.Fori(1, PAIRS // 2) as i:
                for s in range(2):
                    pair(i, s)
            act.wait_ge(table_ready, 1)
            loop_further(act, further_blocks(act), pair)
            for j in range(NTILES):
                n = nrows(j)
                act.wait_ge(x2_ready, j + 1)
                if j:
                    act.wait_ge(fsq, j)
                act.activation(junk2[0:n, :], X[0:n, j, :], ACT.Square,
                               accum_out=ss[0:n, 10 + j:11 + j]).then_inc(fsq, 1)

        @block.vector
        def _(dve):
            v = nc.vector
            steps = [0]

            def link(ins):
                steps[0] += 1
                ins.then_inc(dve_step, 1)
                dve.wait_ge(dve_step, steps[0])

            v.memset(X[0:N4, T4, :], 0.0).then_inc(pad_zeroed, 1)
            v.memset(wg[:, :, :], 0.0).then_inc(wg_zeroed, 1)
            link(v.memset(R[:, :], 0.0))
            v.memset(zeros, 0.0).then_inc(zero_made, 1)
            link(v.memset(padT[:, :, :], 0.0))
            link(v.memset(MVA[:, :, :, DV:DV + 1], 1.0))
            dve.wait_ge(const_made, 1)
            dve.wait_ge(ptab_in, 16)
            link(v.tensor_copy(pfl[:, :], pidx[:, :]))
            v.tensor_scalar(pages[:, :], pages[:, :], float(PAGE), pfl[:, :], ALU.mult, ALU.add).then_inc(pages_ready, 1)
            for c in range(2):
                link(v.tensor_scalar(dump[:, c, :], valid[:, :], -1.0, 1.0, ALU.mult, ALU.add))
                link(v.tensor_scalar(c1[:, :], pfl[:, :], float(DUMP + 64 * c), None, ALU.add))
                link(v.tensor_scalar(dump[:, c, :], dump[:, c, :], c1[:, :], None, ALU.mult))

            def transposed(item, src_banks, g, j):
                n = nrows(j)
                for half in range(2):
                    b, src = src_banks[half]
                    if b is not None:
                        after(dve, item, b)
                    o = hT[:, 4 * half:4 * half + 4, col(j):col(j) + n]
                    s_ = src[:, :].rearrange("p (k t) -> p k t", t=128)[:, :, 0:n]
                    if g is None:
                        ins = v.tensor_copy(o, s_)
                    else:
                        ins = v.tensor_tensor(o, s_, g[:, 4 * half:4 * half + 4, None].to_broadcast([128, 4, n]), ALU.mult)
                    if b in ("a0", "a1"):
                        ins.then_inc(freed[b], 1)
                    elif half == 1:
                        ins.then_inc(freed[src_banks[0][0]], 1)

            def tbanks(item):
                if banks_of(item) == ("a0", "a1"):
                    return [("a0", bank[0]), ("a1", bank[1])]
                b = banks_of(item)[0]
                return [(b, Sps[:, b == "Sb", 0:512]), (None, Sps[:, b == "Sb", 512:1024])]

            def decode_state(kind, item):
                r8 = slice(S0, N4)
                ig, lf = RC[r8, T4, 0:4], RC[r8, T4, 32:36]
                if kind == "mdec1":
                    dve.wait_ge(const_in, 16 * NCONST)
                    link(v.tensor_tensor(dr[r8, 28:32], dr[r8, 0:4], lf, ALU.add))
                    link(v.tensor_tensor(dr[r8, 4:8], dr[r8, 28:32], ig, ALU.max))
                    link(v.tensor_tensor(dr[r8, 16:20], dr[r8, 28:32], dr[r8, 4:8], ALU.subtract))
                    v.tensor_tensor(dr[r8, 20:24], ig, dr[r8, 4:8], ALU.subtract).then_inc(dm_ready, 1)
                    dve.wait_ge(dm_exp, 2)
                    v.nop().then_inc(dw_made, 1)
                    drained(dve, ("small", "mqk"), "t")
                    q = MQ4[r8].rearrange("p (h d) -> p h d", d=DQ)
                    k = MK[r8, T4, :].rearrange("p (h d) -> p h d", d=DQ)
                    link(v.tensor_tensor(nnew[r8], q, k, ALU.mult))
                    link(v.tensor_reduce(dr[r8, 32:36], nnew[r8], AX.X, ALU.add))
                    link(v.tensor_tensor(nnew[r8], q, nold[r8], ALU.mult))
                    link(v.tensor_reduce(dr[r8, 36:40], nnew[r8], AX.X, ALU.add))
                    link(v.tensor_tensor(dr[r8, 32:36], dr[r8, 32:36], dr[r8, 12:16], ALU.mult))
                    link(v.tensor_tensor(dr[r8, 36:40], dr[r8, 36:40], dr[r8, 8:12], ALU.mult))
                    link(v.tensor_tensor(dr[r8, 36:40], dr[r8, 36:40], dr[r8, 32:36], ALU.add))
                    link(v.scalar_tensor_tensor(dr[r8, 60:64], dr[r8, 36:40], -1.0, dr[r8, 24:28], ALU.mult, ALU.max))
                    link(v.tensor_tensor(dr[r8, 36:40], dr[r8, 36:40], dr[r8, 60:64], ALU.max))
                    link(v.reciprocal(dr[r8, 36:40], dr[r8, 36:40]))
                    link(v.tensor_tensor(dr[r8, 52:56], dr[r8, 32:36], dr[r8, 36:40], ALU.mult))
                    link(v.tensor_tensor(dr[r8, 56:60], dr[r8, 8:12], dr[r8, 36:40], ALU.mult))
                    link(v.tensor_tensor(nold[r8], nold[r8], dr[r8, 8:12, None].to_broadcast([NDEC, H, DQ]), ALU.mult))
                    link(v.tensor_tensor(nnew[r8], k, dr[r8, 12:16, None].to_broadcast([NDEC, H, DQ]), ALU.mult))
                    v.tensor_tensor(nnew[r8], nnew[r8], nold[r8], ALU.add).then_inc(cn_ready, 1)
                    dve.wait_ge(st_in, 16)
                    dve.wait_ge(qb_in, 16)
                    link(v.tensor_tensor(QB, QB, C0, ALU.mult))
                    v.tensor_reduce(cq[:, :], QB, AX.X, ALU.add).then_inc(qb_used, 1)
                    dve.wait_ge(qb_used, 1)
                    v.tensor_copy(padT[:, :, S0:N4], cq[:, :].rearrange("p (b h) -> p h b", h=H)).then_inc(pad_ready, 1)
                elif kind == "mdec2":
                    after(dve, item, "t")
                    for h in range(H):
                        link(v.tensor_scalar(HO[r8, T4, DV * h:DV * (h + 1)], PS["t"][r8, DV * h:DV * (h + 1)],
                                             dr[r8, 56 + h:57 + h], None, ALU.mult))
                    v.nop().then_inc(freed["t"], 1)
                    for h in range(H):
                        link(v.scalar_tensor_tensor(HO[r8, T4, DV * h:DV * (h + 1)], MVA[r8, T4, h, 0:DV], dr[r8, 52 + h:53 + h],
                                                    HO[r8, T4, DV * h:DV * (h + 1)], ALU.mult, ALU.add))
                elif kind == "mdec3":
                    dve.wait_ge(dw_in, 16)
                    dve.wait_ge(kb_in, 16)
                    dve.wait_ge(pad_ready, 1)
                    drained(dve, ("ft", "mv"), "p")
                    link(v.tensor_tensor(cq[:, :].rearrange("p (b h) -> p b h", h=H),
                                         vT4[:, :, S0:N4].rearrange("p h b -> p b h"),
                                         dwb[:, 1, :].rearrange("p (b h) -> p b h", h=H), ALU.mult))
                    link(v.tensor_tensor(QB, QB, cq[:, :, None].to_broadcast([128, 32, DQ]), ALU.mult))
                    link(v.tensor_tensor(C0, C0, dwb[:, 0, :, None].to_broadcast([128, 32, DQ]), ALU.mult))
                    v.tensor_tensor(C0, C0, QB, ALU.add).then_inc(cn_ready, 1)
                elif kind == "wsk":
                    drained(dve, ("tok", "mk", NT - 1), "p")
                    for j in range(NTILES):
                        n = 128 if j < NT else NMETA
                        link(v.tensor_tensor(MK[0:n, j, :].rearrange("p (h d) -> p h d", d=DQ),
                                             MK[0:n, j, :].rearrange("p (h d) -> p h d", d=DQ),
                                             RC[0:n, j, 32:36, None].to_broadcast([n, H, DQ]), ALU.mult))
                    v.nop().then_inc(wsk_ready, 1)
                else:
                    drained(dve, ("acc", "mo", 3), "a1")
                    drained(dve, ("small", "mo"), "t")
                    for ap in (MO[:, 0:NT, :], MO[0:N4, T4, :]):
                        link(v.tensor_scalar(ap, ap, 1.0, None, ALU.add))
                        link(v.reciprocal(ap, ap))

            for item in ORDER:
                kind = item[0]
                if kind == "xt":
                    j = item[1]
                    n = nrows(j)
                    dve.wait_ge(rsq, j + 1)
                    if j == 0:
                        dve.wait_ge(gmix_in, 16)
                    v.tensor_scalar(hn[j % 2][0:n], X[0:n, j, :], rr[0:n, j:j + 1], None, ALU.mult).then_inc(hn_ready, 1)
                    transposed(item, tbanks(item), gmix, j)
                elif kind == "gates":
                    dve.wait_ge(const_in, 16 * NCONST)
                    link(v.tensor_tensor(lamv[:, 0, :], lamv[:, 0, :], lamv[:, 1, :], ALU.mult))
                    link(v.tensor_tensor(lamv[:, 1, :], lamv[:, 2, :], lamv[:, 3, :], ALU.mult))
                    v.tensor_reduce(lam[:, 0:2], lamv[:, 0:2, :], AX.X, ALU.add).then_inc(lam_sum, 1)
                    dve.wait_ge(rows_ln, 1)
                    link(v.scalar_tensor_tensor(rF, rF, 0.0, rE, ALU.min, ALU.subtract))
                    link(v.memset(rE, 1.0))
                    link(v.tensor_copy(rB, rF))
                    link(v.memset(rB[:, NMETA:N4], 0.0))
                    link(v.tensor_tensor_scan(rB, rE, rB, 0.0, ALU.mult, ALU.add))
                    link(v.tensor_tensor(rA, rI, rB, ALU.subtract))
                    link(v.memset(rA[:, NMETA:N4], -1e30))
                    v.tensor_tensor_scan(rG, rE, rA, 0.0, ALU.mult, ALU.max).then_inc(rows_scan, 1)
                    dve.wait_ge(rows_scan, 1)
                    v.tensor_tensor(rM, rB, rG, ALU.add).then_inc(rows_scan, 1)
                    link(v.tensor_scalar(negG, rG[:, TOK - 1:TOK], -1.0, None, ALU.mult))
                    dve.wait_ge(rows_scan, 2)
                    link(v.tensor_copy(R[0:H, :], rA))
                    v.tensor_copy(R[0:H, S0:N4], rI[:, S0:N4]).then_inc(rows_scan, 1)
                elif kind == "rows":
                    dve.wait_ge(lam_exp, 1)
                    dve.wait_ge(g_out, 16)
                    dve.wait_ge(m_out, 16)
                    dve.wait_ge(rows_exp, 1)
                    link(v.tensor_tensor(lam[:, 4:5], lam[:, 3:4], lam[:, 2:3], ALU.subtract))
                    link(v.tensor_scalar(lam[:, 4:5], lam[:, 4:5], -LAM_INIT, None, ALU.add))
                    link(v.tensor_scalar(sgi[:, :], pidx[0:64, :], 1, None, ALU.bitwise_and))
                    link(v.tensor_copy(sgn[:, 0:1], sgi[:, :]))
                    link(v.tensor_scalar(sgn[:, 1:2], lam[0:64, 4:5], -1.0, None, ALU.add))
                    link(v.tensor_tensor(sgn[:, 2:3], sgn[:, 0:1], sgn[:, 1:2], ALU.mult))
                    link(v.tensor_scalar(sgn[:, 3:4], sgn[:, 2:3], 1.0, None, ALU.add))
                    link(v.tensor_scalar(gda[:, :], gda[:, :], 1.0 - LAM_INIT, None, ALU.mult))
                    link(v.memset(HO[0:S0, T4, :], 0.0))
                elif kind == "decscore":
                    for n, (b, p) in enumerate(DEC):
                        dve.wait_ge(page_in[n % 4], 16 * (n // 4 + 1))
                        if p == 0:
                            dve.wait_ge(page_in[4], 16 * (b + 1))
                        link(v.tensor_tensor(kring[n % 4], kring[n % 4], kring[4], ALU.mult))
                        v.tensor_reduce(Sd[:, p, 8 * b:8 * b + 8], kring[n % 4].rearrange("p (u d) -> p u d", d=DQ),
                                        AX.X, ALU.add).then_inc(page_used, 1)
                elif kind == "decsm":
                    dve.wait_ge(qk64_in, 32)
                    link(v.tensor_tensor(qk64[:, 0, :], qk64[:, 0, :], qk64[:, 1, :], ALU.mult))
                    link(v.tensor_reduce(Sq[:, PAST:PAST + 1], qk64[:, 0, :], AX.X, ALU.add))
                    after(dve, item, "t")
                    v.tensor_copy(Sq[:, 0:PAST], PS["t"][0:64, 0:PAST]).then_inc(freed["t"], 1)
                    drained(dve, item, "t")
                    v.tensor_reduce(dcol[:, 1:2], Sq[:, 0:PAST + 1], AX.X, ALU.max, negate=True).then_inc(dec_max, 1)
                    dve.wait_ge(dec_exp, 1)
                    link(v.reciprocal(dcol[:, 3:4], dcol[:, 2:3]))
                    link(v.tensor_tensor(dcol[:, 3:4], dcol[:, 3:4], sgn[:, 3:4], ALU.mult))
                    v.tensor_scalar(Sq[:, 0:PAST + 1], Sq[:, 0:PAST + 1], dcol[:, 3:4], None, ALU.mult).then_inc(dec_coef, 1)
                elif kind == "decmix":
                    after(dve, item, "p")
                    v.tensor_reduce(Wd[:, :, :], PS["p"][:, 0:128].rearrange("p (a r m) -> p a r m", a=NPAGES, m=2),
                                    AX.X, ALU.add).then_inc(freed["p"], 1)
                    dve.wait_ge(sel_made, 1)
                    for b, m, dst in (("t", mask1, kring[4]), ("p2", mask2, kring[0])):
                        after(dve, item, b)
                        v.tensor_tensor(dst.rearrange("p (h d) -> p h d", d=DV),
                                        PS[b[0]][:, :].rearrange("p (h d) -> p h d", d=DV),
                                        m[:, :, None].to_broadcast([128, H, DV]), ALU.mult).then_inc(freed[b[0]], 1)
                    dve.wait_ge(decps_in, 16)
                    link(v.tensor_reduce(dr[S0:N4, 48:52], dr[S0:N4, 40:48].rearrange("p (h m) -> p h m", m=2), AX.X, ALU.add))
                    drained(dve, ("small", "dv"), "t")
                    dve.wait_ge(tok_out, 16 * 6)
                    after(dve, item, "t2")
                    for h in range(H):
                        ins = v.scalar_tensor_tensor(HO[S0:N4, T4, 512 + DV * h:512 + DV * (h + 1)],
                                                     DVt[S0:N4, T4, DV * h:DV * (h + 1)], dr[S0:N4, 48 + h:49 + h],
                                                     PS["t"][S0:N4, DV * h:DV * (h + 1)], ALU.mult, ALU.add)
                    ins.then_inc(freed["t"], 1)
                elif kind == "qk":
                    j, h = item[1:]
                    u = UIDX[j, h]
                    n = 128 if j < NT else NMETA
                    w = 128 * (j + 1) + NMETA if j < NT else NMETA
                    d0 = 128 * j if j < NT else 0
                    P = P2[u % 2]
                    after(dve, item, "Sa")
                    after(dve, item, "Sb")
                    diag = Sps[0:n, :, d0:d0 + n]
                    link(v.tensor_tensor(diag, diag, maskneg[0:n, None, 0:n].to_broadcast([n, 2, n]), ALU.add))
                    v.tensor_reduce(sums[0:n, 0:2], Sps[0:n, :, 0:w], AX.X, ALU.max, negate=True).then_inc(maxed, 1)
                    drained(dve, item, "Sa")
                    drained(dve, item, "Sb")
                    link(v.reciprocal(sums[0:n, 4:6], sums[0:n, 2:4]))
                    link(v.tensor_copy(rsum[0:n, u:u + 1], sums[0:n, 4:5]))
                    link(v.scalar_tensor_tensor(sums[0:n, 6:7], sums[0:n, 2:3], lam[0:n, 4:5], sums[0:n, 5:6], ALU.mult, ALU.mult))
                    v.scalar_tensor_tensor(P[0:n, 0, 0:w], P[0:n, 1, 0:w], sums[0:n, 6:7], P[0:n, 0, 0:w],
                                           ALU.mult, ALU.add).then_inc(mixed, 1)
                elif kind == "mqk_s":
                    h = item[1]
                    WT, WTm = WTs[h % 2]
                    dve.wait_ge(decay_masked, h + 1)
                    for i in range(NT):
                        if i % 2 == 0:
                            after(dve, item, "Sb" if i else "Sa")
                        ins = v.tensor_tensor(WT[:, OFF[i]:OFF[i] + 512 - 128 * i], WT[:, OFF[i]:OFF[i] + 512 - 128 * i],
                                              Sps[:, i // 2, 512 * (i % 2):512 * (i % 2) + 512 - 128 * i], ALU.mult)
                        if i % 2:
                            ins.then_inc(freed["Sb" if i > 1 else "Sa"], 1)
                    after(dve, item, "t")
                    v.tensor_tensor(WTm[:, N4:TOK], WTm[:, N4:TOK], PS["t"][0:NMETA, :], ALU.mult).then_inc(freed["t"], 1)
                    after(dve, item, "p")
                    v.tensor_tensor(WTm[:, 0:NMETA], WTm[:, 0:NMETA], PS["p"][0:NMETA, 0:NMETA], ALU.mult).then_inc(freed["p"], 1)
                elif kind == "mpv":
                    h = item[1]
                    for b, jj, n in (("a0", (0, 3), 128), ("a1", (3, 4), 128), ("a1", (4, 5), NMETA)):
                        after(dve, item, b)
                        o = 129 * (jj[0] - (3 if b == "a1" else 0))
                        k = jj[1] - jj[0]
                        src = PS[b][0:n, o:o + 129 * k].rearrange("p (j d) -> p j d", d=129)
                        dd = src[:, :, DV:DV + 1]
                        link(v.scalar_tensor_tensor(den[0:n, 0:k, :], dd, -1.0, RC[0:n, jj[0]:jj[1], 64 + h:65 + h],
                                                    ALU.mult, ALU.max))
                        link(v.tensor_tensor(den[0:n, 0:k, :], den[0:n, 0:k, :], dd, ALU.max))
                        link(v.reciprocal(den[0:n, 0:k, :], den[0:n, 0:k, :]))
                        ins = v.tensor_tensor(HO[0:n, jj[0]:jj[1], DV * h:DV * (h + 1)], src[:, :, 0:DV],
                                              den[0:n, 0:k, :].to_broadcast([n, k, DV]), ALU.mult)
                        if b == "a0" or jj[0] == 4:
                            ins.then_inc(freed[b], 1)
                            drained(dve, item, b)
                        else:
                            link(ins)
                elif kind in ("mdec1", "mdec2", "mdec3", "wsk", "sig"):
                    decode_state(kind, item)
                elif kind == "ot":
                    j = item[1]
                    n = nrows(j)
                    if j == 0:
                        drained(dve, ("pv",) + UNITS[-1], "p")
                        dve.wait_ge(v_out, 16 * 6)
                    sq = sqd[0:n, :]
                    link(v.tensor_tensor(sq, HO[0:n, j, :], HO[0:n, j, :], ALU.mult))
                    v.tensor_reduce(ss8[0:n, :], sq.rearrange("p (u d) -> p u d", d=DV), AX.X, ALU.add).then_inc(sums_ready, 1)
                    dve.wait_ge(rsq, RSQ8[j])
                    ho = HO[0:n, j, :].rearrange("p (u d) -> p u d", d=DV)
                    link(v.tensor_tensor(ho, ho, rr8[0:n, :, None].to_broadcast([n, 8, DV]), ALU.mult))
                    link(v.tensor_tensor(ho[:, 0:4], ho[:, 0:4], gm[0:n, None, :].to_broadcast([n, 4, DV]), ALU.mult))
                    link(v.tensor_tensor(ho[:, 4:8], ho[:, 4:8], gda[0:n, None, :].to_broadcast([n, 4, DV]), ALU.mult))
                    v.tensor_tensor(HO[0:n, j, 0:512], HO[0:n, j, 0:512], MO[0:n, j, :], ALU.mult).then_inc(ho_ready, 1)
                    transposed(item, tbanks(item), None, j)
                elif kind == "wo":
                    j, half = item[1:]
                    n = nrows(j)
                    b = "a%d" % half
                    after(dve, item, b)
                    xs = X[0:n, j, 512 * half:512 * half + 512]
                    ins = v.tensor_tensor(xs, xs, PS[b][0:n, :], ALU.add)
                    if j == T4:
                        xs = X[0:n, j, 512:1024]
                        ins = v.tensor_tensor(xs, xs, PS[b][64:64 + n, :], ALU.add)
                    ins.then_inc(freed[b], 1)
                elif kind == "rt":
                    j = item[1]
                    n = nrows(j)
                    dve.wait_ge(rsq, RSQF[j])
                    v.tensor_scalar(HO[0:n, j, :], X[0:n, j, :], rr[0:n, 5 + j:6 + j], None, ALU.mult).then_inc(xn_ready, 1)
                    transposed(item, tbanks(item), gffn, j)
                elif kind == "logit":
                    j = item[1]
                    n = nrows(j)
                    if j == 0:
                        link(v.memset(Lt[:, :, :], 0.0))
                    after(dve, item, "t")
                    v.tensor_tensor(Lt[0:n, j, :], PS["t"][0:n, 0:36], br[0:n, :], ALU.add).then_inc(freed["t"], 1)
                elif kind == "rank":
                    drained(dve, ("logit", T4), "t")
                    b4 = lambda a: a[:, :, None].to_broadcast([128, NTILES, 4])
                    b8 = lambda a: a[:, :, None].to_broadcast([128, NTILES, 8])
                    gl = L[:, :, 0:4]
                    gmax, gsum, v1, v2, dlt, ex, key, p1 = c5[0], c5[1], c5[2], c5[3], c5[4], c5[5], c5[6], c5[7]

                    def first(onehot, vals, best, width, tmp):
                        bw = lambda a: a[:, :, None].to_broadcast([128, NTILES, width])
                        link(v.tensor_tensor(tmp, vals, bw(best), ALU.is_equal))
                        link(v.tensor_tensor(tmp, tmp, kiota[:, None, 0:width].to_broadcast([128, NTILES, width]), ALU.mult))
                        link(v.tensor_reduce(key, tmp, AX.X, ALU.max))
                        link(v.tensor_tensor(onehot, tmp, bw(key), ALU.is_equal))

                    link(v.tensor_reduce(gmax, gl, AX.X, ALU.max))
                    v.tensor_tensor(Gx, gl, b4(gmax), ALU.subtract).then_inc(gexp_in, 1)
                    first(Go, gl, gmax, 4, Gk)
                    t4 = T160.rearrange("p (j g e) -> p j g e", g=4, e=8)
                    link(v.tensor_tensor(t4[:, :, 0], L[:, :, 4:12], b8(Go[:, :, 0]), ALU.mult))
                    for g_ in range(1, 4):
                        link(v.tensor_tensor(t4[:, :, g_], L[:, :, 4 + 8 * g_:12 + 8 * g_], b8(Go[:, :, g_]), ALU.mult))
                    ein, o1, o2, tmp, rest = E8
                    link(v.tensor_tensor(ein, t4[:, :, 0], t4[:, :, 1], ALU.add))
                    link(v.tensor_tensor(ein, ein, t4[:, :, 2], ALU.add))
                    link(v.tensor_tensor(ein, ein, t4[:, :, 3], ALU.add))
                    link(v.tensor_reduce(v1, ein, AX.X, ALU.max))
                    first(o1, ein, v1, 8, tmp)
                    link(v.scalar_tensor_tensor(rest, o1, -3e38, ein, ALU.mult, ALU.add))
                    link(v.tensor_reduce(v2, rest, AX.X, ALU.max))
                    first(o2, rest, v2, 8, tmp)
                    v.tensor_tensor(dlt, v2, v1, ALU.subtract).then_inc(gexp_in, 1)
                    for dst, o in ((M1, o1), (M2, o2)):
                        d4 = dst.rearrange("p (j g e) -> p j g e", g=4, e=8)
                        for g_ in range(4):
                            link(v.tensor_tensor(d4[:, :, g_], o, b8(Go[:, :, g_]), ALU.mult))
                        d3 = dst.rearrange("p (j e) -> p j e", e=32)
                        link(v.tensor_tensor(d3, d3, valid[:, :, None].to_broadcast([128, NTILES, 32]), ALU.mult))
                    v.tensor_tensor(MM, M1, M2, ALU.add).then_inc(m_ready, 1)
                    dve.wait_ge(gexp, 2)
                    link(v.tensor_reduce(gsum, Gx, AX.X, ALU.add))
                    link(v.tensor_scalar(p1, ex, 1.0, None, ALU.add))
                    link(v.tensor_tensor(p1, p1, gsum, ALU.mult))
                    link(v.reciprocal(pw[:, 0, :], p1))
                    link(v.tensor_tensor(pw[:, 1, :], pw[:, 0, :], ex, ALU.mult))
                    after(dve, item, "p")
                    v.tensor_copy(PREF, PS["p"][:, 0:192]).then_inc(freed["p"], 1)
                    drained(dve, item, "p")
                    rank = PREF[:, 0:160].rearrange("p (j e) -> p j e", e=32)
                    cnt = PREF[:, 160:192]
                    extra, xend, dd, one32 = e32[0], e32[1], e32[2], e32[3]
                    cx = CX.rearrange("p (e q) -> p e q", q=MAXQ)
                    link(v.tensor_tensor(cx, cnt[:, :, None].to_broadcast([128, 32, MAXQ]),
                                         qiota[:, None, :].to_broadcast([128, 32, MAXQ]), ALU.is_gt))
                    link(v.tensor_reduce(extra, cx, AX.X, ALU.add))
                    link(v.memset(one32, 1.0))
                    link(v.tensor_tensor_scan(xend, one32, extra, 0.0, ALU.mult, ALU.add))
                    link(v.tensor_tensor(dd, xend, extra, ALU.subtract))
                    link(v.tensor_scalar(dd, dd, float(SLOTS), float(XROW - SLOTS), ALU.mult, ALU.add))
                    link(v.tensor_tensor(dd, dd, eiota[:, :], ALU.subtract))
                    t3 = T160.rearrange("p (j e) -> p j e", e=32)
                    link(v.tensor_scalar(t3, rank, float(SLOTS), None, ALU.is_ge))
                    link(v.tensor_tensor(t3, t3, dd[:, None, :].to_broadcast([128, NTILES, 32]), ALU.mult))
                    link(v.tensor_tensor(t3, t3, rank, ALU.add))
                    link(v.tensor_tensor(t3, t3, eiota[:, None, :].to_broadcast([128, NTILES, 32]), ALU.add))
                    for c, m_ in enumerate((M1, M2)):
                        link(v.tensor_tensor(m_, m_, T160, ALU.mult))
                        link(v.tensor_reduce(c5[8 + c], m_.rearrange("p (j e) -> p j e", e=32), AX.X, ALU.add))
                        link(v.tensor_tensor(POS[:, c, :], c5[8 + c], dump[:, c, :], ALU.add))
                        link(v.tensor_copy(POSG[:, c, :], c5[8 + c]))
                    v.nop().then_inc(pos_ready, 1)
                    x3 = XT32[0:1, :].rearrange("p (x e) -> p x e", e=32)
                    link(v.tensor_tensor(x3, xend[0:1, None, :].to_broadcast([1, XBLOCKS, 32]),
                                         xiota[:, :, None].to_broadcast([1, XBLOCKS, 32]), ALU.is_le))
                    link(v.tensor_reduce(xf[0:1, 0:XBLOCKS], x3, AX.X, ALU.add))
                    link(v.tensor_scalar(TE[0:1, 0:XBLOCKS], xf[0:1, 0:XBLOCKS], float(NEXP - 1), None, ALU.min))
                    link(v.tensor_copy(TE[0:1, XBLOCKS:XBLOCKS + 1], xend[0:1, 31:32]))
                    v.nop().then_inc(table_ready, 1)

            def pair(i, s):
                dve.wait_ge(xt_filled[s], i + 1)
                reuse(dve, gu_filled[s], i)
                for half in range(2):
                    ins = v.tensor_tensor(xT[s][:, 4 * half:4 * half + 4, :],
                                          bank[half][:, :].rearrange("p (k t) -> p k t", t=128),
                                          gffn[:, 4 * half:4 * half + 4, None].to_broadcast([128, 4, 128]), ALU.mult)
                ins.then_inc(xt_evac[s], 1)
                dve.wait_ge(silu_done[s], i + 1)
                reuse(dve, at_filled[s], i)
                v.tensor_tensor(AB[s], SG[s], PS["t" if s else "p"][:, DE:2 * DE], ALU.mult).then_inc(act_done[s], 1)
                dve.wait_ge(dn_filled[s], i + 1)
                reuse(dve, y_out[s], 16 * i)
                v.tensor_copy(YO[s][:, 512:1024], Sps[:, 0, 512:1024]).then_inc(y1[s], 1)

            def finish(j):
                n = nrows(j)
                dve.wait_ge(rsq, 3 * NTILES + j + 1)
                if j == 0:
                    dve.wait_ge(gfin_in, 16)
                link(v.tensor_scalar(X[0:n, j, :], X[0:n, j, :], rr[0:n, 10 + j:11 + j], None, ALU.mult))
                v.tensor_tensor(X[0:n, j, :], X[0:n, j, :], gfin[0:n], ALU.mult).then_inc(yfin, 1)

            for s in range(2):
                pair(0, s)
            with dve.Fori(1, PAIRS // 2) as i:
                for s in range(2):
                    pair(i, s)
            loop_further(dve, further_blocks(dve), pair)
            for j in range(NTILES):
                n = nrows(j)
                for c in range(2):
                    dve.wait_ge(y_in[2 * (j % 2) + c], 16 * (j // 2 + 1))
                    ins = v.scalar_tensor_tensor(X[0:n, j, :], YG[c][j % 2][0:n], pw[0:n, c, j:j + 1], X[0:n, j, :],
                                                 ALU.mult, ALU.add)
                    if c == 0:
                        link(ins)
                    else:
                        ins.then_inc(x2_ready, 1)
                dve.wait_ge(x2_ready, j + 1)
                v.nop().then_inc(y_free, 1)
                if j:
                    finish(j - 1)
            finish(T4)

        @block.tensor
        def _(pe):
            def transpose_rows(rows, item, j):
                n = nrows(j)
                names = banks_of(item)
                for half in range(2):
                    b = names[min(half, len(names) - 1)]
                    if half == 0 or len(names) == 2:
                        before(pe, item, b)
                    dst = bank[half][:, :] if len(names) == 2 else Sps[:, b == "Sb", 512 * half:512 * half + 512]
                    for k in range(4):
                        mm = pe.transpose(dst[:, 128 * k:128 * k + n], rows[0:n, 4 * half + k:D:KC], ident[0:n, 0:n])
                    if len(names) == 2 or half == 1:
                        mm.then_inc(filled[b], 1)

            for item in ORDER:
                kind = item[0]
                if kind == "xt":
                    j = item[1]
                    if j == 0:
                        pe.wait_ge(ident_made, 1)
                    pe.wait_ge(hn_ready, j + 1)
                    transpose_rows(hn[j % 2], item, j)
                elif kind == "gates":
                    for j in range(NTILES):
                        drained(pe, ("xt", j), banks_of(("xt", j))[-1])
                    pe.wait_ge(const_in, 16 * NCONST)
                    before(pe, item, "t")
                    before(pe, item, "p")
                    for b, c0, c1_ in (("t", 0, 512), ("p", 512, TOK)):
                        for k in range(KC):
                            mm = pe.matmul(PS[b][0:36, 0:c1_ - c0], wg[:, k, :], hT[:, k, c0:c1_],
                                           start=(k == 0), stop=(k == KC - 1))
                        mm.then_inc(filled[b], 1)
                elif kind == "acc":
                    b, m = item[1:]
                    r = "a%d" % (m % 2)
                    n = BLOCKS.index(b)
                    w = blkslot[n % 3]
                    if m == 0:
                        pe.wait_ge(block_in[n % 3], 16 * (n // 3 + 1))
                    before(pe, item, r)
                    for k in range(KC):
                        if b in FEATURE:
                            mm = pe.matmul(PS[r][:, :], w[:, k, 128 * m:128 * (m + 1)], hT[:, k, 0:512],
                                           start=(k == 0), stop=(k == KC - 1))
                        else:
                            mm = pe.matmul(PS[r][:, :], hT[:, k, 128 * m:128 * (m + 1)], w[:, k, :],
                                           start=(k == 0), stop=(k == KC - 1))
                    mm.then_inc(filled[r], 1)
                elif kind == "small":
                    b = item[1]
                    w = blkslot[BLOCKS.index(b) % 3]
                    before(pe, item, "t")
                    for k in range(KC):
                        for u in range(2):
                            mm = pe.matmul(PS["t"][64 * u:64 * u + N4, 0:256], hT[:, k, 512:TOK],
                                           w[:, k, 256 * u:256 * u + 256], start=(k == 0), stop=(k == KC - 1))
                    mm.then_inc(filled["t"], 1)
                    pe.wait_ge(filled["t"], NTH[item, "t"] + 1)
                    pe.nop().then_inc(block_used, 1)
                elif kind == "ft":
                    b = item[1]
                    drained(pe, ("small", b), "t")
                    before(pe, item, "p")
                    for m in range(4):
                        cols = slice(128 * m, 128 * m + 128)
                        src = (MVA[0:N4, T4, m, 0:DV] if b == "mv" else tokst[0][0:N4, cols] if b == "dq" else
                               tokst[1][0:N4, cols] if b == "dk" else MQ4[:, cols] if m < 2 else
                               MK[0:N4, T4, 128 * (m - 2):128 * (m - 1)])
                        mm = pe.transpose(PS["p"][:, N4 * m:N4 * (m + 1)], src, ident[0:N4, 0:N4])
                    mm.then_inc(filled["p"], 1)
                elif kind == "tok":
                    name, j = item[1:]
                    b, m0 = ("dk", 0) if name == "dk" else ("mqk", 2)
                    if j == 0:
                        drained(pe, ("acc", b, 2), "a0")
                        drained(pe, ("acc", b, 3), "a1")
                    before(pe, item, "p")
                    for m in range(m0, 4):
                        mm = pe.transpose(PS["p"][:, 128 * (m - m0):128 * (m - m0 + 1)], feat[b][:, m, col(j):col(j) + 128],
                                          ident[:, :])
                    mm.then_inc(filled["p"], 1)
                elif kind == "rows":
                    pe.wait_ge(rows_exp, 1)
                    pe.wait_ge(rows_scan, 3)
                    before(pe, item, "t")
                    for j in range(NTILES):
                        n = nrows(j)
                        c0 = N4 + 128 * j if j < NT else 0
                        mm = pe.transpose(PS["t"][0:n, 68 * j:68 * (j + 1)], R[0:68, c0:c0 + n], ident[0:68, 0:68])
                    mm.then_inc(filled["t"], 1)
                elif kind == "decsm":
                    pe.wait_ge(page_used, len(DEC))
                    before(pe, item, "t")
                    for p in range(NPAGES):
                        mm = pe.transpose(PS["t"][0:64, 128 * p:128 * (p + 1)], Sd[:, p, :], ident[:, :])
                    mm.then_inc(filled["t"], 1)
                elif kind == "decmix":
                    pe.wait_ge(dec_coef, 1)
                    before(pe, item, "p")
                    for p in range(NPAGES):
                        mm = pe.transpose(PS["p"][:, 64 * p:64 * (p + 1)], Sq[:, 128 * p:128 * (p + 1)], ident[0:64, 0:64])
                    mm.then_inc(filled["p"], 1)
                    drained(pe, item, "p")
                    before(pe, item, "t")
                    for b in range(NDEC):
                        dst = "t" if b < 4 else "p"
                        for p in range(NPAGES):
                            n = 16 + b * NPAGES + p
                            pe.wait_ge(page_in[n % 4], 16 * (n // 4 + 1))
                            mm = pe.matmul(PS[dst][32 * (b % 4):32 * (b % 4) + 32, :], Wd[:, p, :], kring[n % 4],
                                           start=(p == 0), stop=(p == NPAGES - 1))
                        if b % 4 < 3:
                            mm.then_inc(vpage_used, 2)
                        else:
                            region = dst if dst == "t" else "p2"
                            mm.then_inc(filled[dst], 1)
                            after(pe, item, region)
                            pe.nop().then_inc(vpage_used, 2)
                    drained(pe, item, "p2")
                    before(pe, item, "t2")
                    for n, part in enumerate((kring[4], kring[0])):
                        mm = pe.matmul(PS["t"][0:N4, :], sel[:, :], part, start=(n == 0), stop=(n == 1))
                    mm.then_inc(filled["t"], 1)
                elif kind == "qk":
                    j, h = item[1:]
                    n = 128 if j < NT else NMETA
                    c0 = col(j)
                    if UIDX[j, h] == 0:
                        for b in ("dq", "dk"):
                            drained(pe, ("acc", b, 3), "a1")
                            drained(pe, ("ft", b), "p")
                    for m in range(2):
                        before(pe, item, ("Sa", "Sb")[m])
                        r = slice(64 * m, 64 * m + 64)
                        at_ = 0
                        if j < NT:
                            at_ = 128 * (j + 1)
                            pe.matmul(Sps[0:n, m, 0:at_], dqT[r, h, c0:c0 + n], dkT[r, h, 0:at_], start=True, stop=True)
                        mm = pe.matmul(Sps[0:n, m, at_:at_ + NMETA], dqT[r, h, c0:c0 + n], dkT[r, h, 512:512 + NMETA],
                                       start=True, stop=True)
                        mm.then_inc(filled[("Sa", "Sb")[m]], 1)
                elif kind == "tp":
                    j, h = item[1:]
                    n = 128 if j < NT else NMETA
                    P = P2[UIDX[j, h] % 2]
                    pe.wait_ge(mixed, UIDX[j, h] + 1)
                    before(pe, item, "p")
                    at_ = 128 * (j + 1) if j < NT else 0
                    pe.transpose(PS["p"][0:NMETA, 0:n], P[0:n, 0, at_:at_ + NMETA], ident[0:n, 0:n]).then_inc(filled["p"], 1)
                    if j < NT:
                        before(pe, item, "t")
                        for i in range(j + 1):
                            mm = pe.transpose(PS["t"][:, 128 * i:128 * (i + 1)], P[0:n, 0, 128 * i:128 * (i + 1)], ident[0:n, 0:n])
                        mm.then_inc(filled["t"], 1)
                elif kind == "pv":
                    j, h = item[1:]
                    n = 128 if j < NT else NMETA
                    drained(pe, ("tp", j, h), "p")
                    if UIDX[j, h] == 0:
                        drained(pe, ("acc", "dv", 3), "a1")
                        drained(pe, ("small", "dv"), "t")
                    before(pe, item, "p")
                    mm = pe.matmul(PS["p"][0:n, 0:DV], AT[0:NMETA, 4, 0:n], DVt[0:NMETA, T4, DV * h:DV * (h + 1)],
                                   start=True, stop=(j == T4))
                    for i in range(j + 1) if j < NT else ():
                        mm = pe.matmul(PS["p"][0:n, 0:DV], AT[:, i, 0:n], DVt[:, i, DV * h:DV * (h + 1)],
                                       start=False, stop=(i == j))
                    mm.then_inc(filled["p"], 1)
                elif kind == "mqk_s":
                    h = item[1]
                    r = slice(64 * (h % 2), 64 * (h % 2) + 64)
                    if h == 0:
                        drained(pe, ("acc", "mqk", 3), "a1")
                        drained(pe, ("ft", "mqk"), "p")
                    kT, qT = mqkT[r, 2 + h // 2, :], mqkT[r, h // 2, :]
                    for b in ("Sa", "Sb", "t", "p"):
                        before(pe, item, b)
                    for i in range(NT):
                        mm = pe.matmul(Sps[:, i // 2, 512 * (i % 2):512 * (i % 2) + 512 - 128 * i],
                                       kT[:, 128 * i:128 * (i + 1)], qT[:, 128 * i:512], start=True, stop=True)
                        if i % 2:
                            mm.then_inc(filled["Sb" if i > 1 else "Sa"], 1)
                    pe.matmul(PS["t"][0:NMETA, :], kT[:, 512:512 + NMETA], qT[:, 0:512], start=True, stop=True)\
                      .then_inc(filled["t"], 1)
                    pe.matmul(PS["p"][0:NMETA, 0:NMETA], kT[:, 512:512 + NMETA], qT[:, 512:512 + NMETA],
                              start=True, stop=True).then_inc(filled["p"], 1)
                elif kind == "mpv":
                    h = item[1]
                    WT, WTm = WTs[h % 2]
                    for b in ("Sa", "Sb", "t", "p"):
                        drained(pe, ("mqk_s", h), b)
                    if h == 0:
                        drained(pe, ("acc", "mv", 3), "a1")
                        drained(pe, ("small", "mv"), "t")
                    before(pe, item, "a0")
                    before(pe, item, "a1")
                    for j in range(NTILES):
                        n = 128 if j < NT else NMETA
                        b, o = ("a0", 129 * j) if j < 3 else ("a1", 129 * (j - 3))
                        c0 = N4 + 128 * j if j < NT else 0
                        for i in range(j + 1) if j < NT else ():
                            pe.matmul(PS[b][0:n, o:o + 129], WT[:, OFF[i] + 128 * (j - i):OFF[i] + 128 * (j - i) + 128],
                                      MVA[:, i, h, :], start=(i == 0), stop=False)
                        mm = pe.matmul(PS[b][0:n, o:o + 129], WTm[:, c0:c0 + n], MVA[0:NMETA, T4, h, :],
                                       start=(j == T4), stop=True)
                        if j in (2, 4):
                            mm.then_inc(filled[b], 1)
                elif kind == "mdec2":
                    pe.wait_ge(pad_ready, 1)
                    before(pe, item, "t")
                    for h in range(H):
                        mm = pe.transpose(PS["t"][0:N4, DV * h:DV * (h + 1)], padT[:, h, :], ident[:, :])
                    mm.then_inc(filled["t"], 1)
                elif kind == "cfin":
                    pe.wait_ge(wsk_ready, 1)
                    before(pe, item, "t")
                    for h in range(H):
                        for j in range(NTILES):
                            n = 128 if j < NT else NMETA
                            pe.matmul(PS["t"][:, DQ * h:DQ * (h + 1)], MVA[0:n, j, h, 0:DV], MK[0:n, j, DQ * h:DQ * (h + 1)],
                                      start=(j == 0), stop=(j == T4))
                    for j in range(NTILES):
                        n = 128 if j < NT else NMETA
                        mm = pe.matmul(PS["t"][0:1, 256:512], ones[0:n, 0:1], MK[0:n, j, :], start=(j == 0), stop=(j == T4))
                    mm.then_inc(filled["t"], 1)
                elif kind == "ot":
                    j = item[1]
                    pe.wait_ge(ho_ready, j + 1)
                    transpose_rows(HO[:, j, :], item, j)
                elif kind == "wo":
                    j, half = item[1:]
                    n = nrows(j)
                    bidx = 6 + half
                    if j == 0:
                        pe.wait_ge(block_in[bidx % 3], 16 * (bidx // 3 + 1))
                    drained(pe, ("ot", j), "Sa")
                    b = "a%d" % half
                    before(pe, item, b)
                    for k in range(KC):
                        if j < T4:
                            mm = pe.matmul(PS[b][0:n, :], hT[:, k, col(j):col(j) + n], blkslot[bidx % 3][:, k, :],
                                           start=(k == 0), stop=(k == KC - 1))
                            continue
                        for u in range(2):
                            mm = pe.matmul(PS[b][64 * u:64 * u + n, :], hT[:, k, 512:TOK], blkslot[(6 + u) % 3][:, k, :],
                                           start=(k == 0), stop=(k == KC - 1))
                    mm.then_inc(filled[b], 1)
                    if j == T4:
                        after(pe, item, b)
                        pe.nop().then_inc(block_used, 2)
                elif kind == "rt":
                    j = item[1]
                    pe.wait_ge(xn_ready, j + 1)
                    transpose_rows(HO[:, j, :], item, j)
                elif kind == "logit":
                    j = item[1]
                    n = nrows(j)
                    drained(pe, ("rt", j), "Sb")
                    before(pe, item, "t")
                    for k in range(KC):
                        mm = pe.matmul(PS["t"][0:n, 0:36], hT[:, k, col(j):col(j) + n], wr[:, k, :],
                                       start=(k == 0), stop=(k == KC - 1))
                    mm.then_inc(filled["t"], 1)
                elif kind == "rank":
                    pe.wait_ge(m_ready, 1)
                    before(pe, item, "p")
                    for j in range(NTILES + 1):
                        last = min(j, NTILES - 1)
                        for i in range(last + 1):
                            mm = pe.matmul(PS["p"][:, 32 * j:32 * (j + 1)], tri[:, :] if i == j else ones[:, :],
                                           MM[:, 32 * i:32 * (i + 1)], start=(i == 0), stop=(i == last))
                    mm.then_inc(filled["p"], 1)

            def pair(i, s):
                pe.wait_ge(xg_in[s], 16 * i + 16)
                reuse(pe, xt_evac[1 - s], i + s)
                for k in range(KC):
                    mm = pe.transpose(bank[k // 4][:, 128 * (k % 4):128 * (k % 4) + 128], XG[s][:, k:D:KC], ident[:, :])
                mm.then_inc(xt_filled[s], 1)
                pe.wait_ge(xt_evac[s], i + 1)
                reuse(pe, act_done[s], i)
                gu = PS["t" if s else "p"]
                for u in range(2):
                    pe.wait_ge(gu_in[2 * s + u], 32 * i + 32)
                for k in range(KC):
                    for u in range(2):
                        mm = pe.matmul(gu[64 * u:64 * u + 64, :], xT[s][:, k, 64 * u:64 * u + 64],
                                       Wgu[2 * s + u][:, :, k, :], start=(k == 0), stop=(k == KC - 1))
                mm.then_inc(gu_filled[s], 1)
                pe.wait_ge(act_done[s], i + 1)
                reuse(pe, at_evac[1 - s], i + s)
                for f in range(FC):
                    mm = pe.transpose(Sps[:, 1, 512 + 128 * f:640 + 128 * f], AB[s][:, f:DE:FC], ident[:, :])
                mm.then_inc(at_filled[s], 1)
                pe.wait_ge(at_evac[s], i + 1)
                reuse(pe, y0[1 - s], i + s)
                reuse(pe, y1[1 - s], i + s)
                for u in range(2):
                    pe.wait_ge(dn_in[2 * s + u], 16 * i + 16)
                for half in range(2):
                    for f in range(FC):
                        for u in range(2):
                            mm = pe.matmul(Sps[64 * u:64 * u + 64, 0, 512 * half:512 * half + 512],
                                           aT[s][:, f, 64 * u:64 * u + 64],
                                           Wdn[2 * s + u][:, f, 512 * half:512 * half + 512],
                                           start=(f == 0), stop=(f == FC - 1))
                mm.then_inc(dn_filled[s], 1)

            for b in ("a0", "a1", "Sa", "Sb", "t", "p"):
                pe.wait_ge(freed[b], TOTAL[b])
            for s in range(2):
                pair(0, s)
            with pe.Fori(1, PAIRS // 2) as i:
                for s in range(2):
                    pair(i, s)
            pe.wait_ge(table_ready, 1)
            loop_further(pe, further_blocks(pe), pair)


_INS = ["x_prompt", "x_sample", "cache_k", "cache_v", "state_C", "state_n", "state_m", "page_table", "meta_tokens",
        "norm_mix", "w_in", "b_gates", "head_norm_m", "lambda_q1", "lambda_k1", "lambda_q2", "lambda_k2",
        "head_norm_da", "w_out", "norm_ffn", "w_group", "b_group", "w_router", "b_router", "w_gate_e", "w_up_e",
        "w_down_e", "norm_final"]
_OUTS = [(1, SEQ, D), (NDEC, 1, D), (1, 1, NMETA + SEQ, H, 2 * DQ), (1, 1, NMETA + SEQ, H, DV), (1, 1, H, DV, DQ),
         (1, 1, H, DQ), (1, 1, H), (1, NDEC, 1, H, 2 * DQ), (1, NDEC, 1, H, DV), (1, NDEC, H, DV, DQ),
         (1, NDEC, H, DQ), (1, NDEC, H)]


def kernel(**inputs):
    import numpy as _np
    import concourse.bacc as _bacc
    from concourse.bass_utils import run_bass_kernel_spmd as _run

    nc = _bacc.Bacc("TRN2", target_bir_lowering=False, num_devices=1)
    arrays, args = {}, []
    for name in _INS:
        a = _np.ascontiguousarray(inputs[name])
        arrays["in_" + name] = a
        args.append(nc.dram_tensor("in_" + name, a.shape, mybir.dt.from_np(a.dtype), kind="ExternalInput").ap())
    for i, shape in enumerate(_OUTS):
        args.append(nc.dram_tensor("out_%d" % i, shape, mybir.dt.float32, kind="ExternalOutput").ap())
    build(nc, *args)
    r = _run(nc, [arrays], core_ids=[0])
    return tuple(r.results[0]["out_%d" % i] for i in range(len(_OUTS)))
```

```python
import math
from contextlib import ExitStack

import concourse.bass as bass
from concourse import mybir

D = 1024
SEQ = 512
NMETA = 16
NDEC = 8
PAST = 256
PAGE = 128
NPAGES = PAST // PAGE
NPOOL = 20
H = 4
DQ = 64
DV = 128
NEXP = 32
NGRP = 4
EPG = NEXP // NGRP
DE = 256
KC = D // 128
FC = DE // 128
EPS = 1e-6
LAM_INIT = 0.8 - 0.6 * math.exp(-0.3 * 0)

NT = SEQ // 128
T4 = NT
S0 = 32
N4 = S0 + NDEC
TOK = SEQ + N4
NTILES = NT + 1

SLOTS = 64
PAIRS = NEXP // 2
ASSIGN = 2 * (SEQ + NMETA + NDEC)
XBLOCKS = (ASSIGN - 1) // SLOTS
XPAIRS = (XBLOCKS + 3) // 4 * 2
XBLOCKS = 2 * XPAIRS
XROW = NEXP * SLOTS
DUMP = XROW + XBLOCKS * SLOTS
GROWS = DUMP + 256
SECOND = 1024
assert TOK <= SECOND
NPAIRS = GROWS // 128
NOROW = 1 << 20
MAXQ = (SEQ + NMETA + NDEC) // SLOTS

W_COLS = dict(mqk=0, mv=512, mo=1024, gates=1536, dq=1544, dk=2056, dv=2568)
BLOCKS = ["dq", "dk", "dv", "mqk", "mv", "mo", "wo0", "wo1"]
PROJ = BLOCKS[:6]
FEATURE = ("dq", "dk", "mqk")
FILL = {4: .7, 0: .8, 1: 1, 2: 1.1, 3: 1.3}
UNITS = [(j, h) for j in (4, 0, 1, 2, 3) for h in range(H)]


def nrows(j):
    return 128 if j < NT else N4


def col(j):
    return 128 * j


def schedule():
    order = [("xt", j) for j in range(NTILES)] + [("gates",)]

    def block(b):
        items = [("acc", b, m) for m in range(4)] + [("small", b)]
        if b == "mo":
            items = [items[0], items[1], ("sig", 0), items[2], ("sig", 1), items[3], ("sig", 2), items[4], ("sig", 3), ("sig", 4)]
        if b != "dv" and b != "mo":
            items += [("ft", b)]
        if b == "dk":
            items += [("tok", "dk", j) for j in range(NT)]
        if b == "mqk":
            items += [("tok", "mk", j) for j in range(NT)]
        return items

    order += block("dq") + [("decscore",)] + block("dk") + [("rows",)] + block("dv") + [("decsm",)]
    mv = block("mv")
    back = block("mqk") + [("decmix",)] + mv[:4] + [("decmix2",)] + mv[4:] + block("mo")
    work = {"acc": 14, "small": 8, "decmix": 14, "decmix2": 16, "sig": 0}
    done, shares = 0, 0
    total = sum(work.get(i[0], 1) for i in back)
    prev = None
    for n, u in enumerate(UNITS):
        order.append(("qk",) + u)
        shares += FILL[u[0]]
        while back and (n == len(UNITS) - 1 or
                        done + work.get(back[0][0], 1) / 2 < total * shares / sum(FILL[v[0]] for v in UNITS)):
            done += work.get(back[0][0], 1)
            order.append(back.pop(0))
        if prev:
            order += [("tp",) + prev, ("pv",) + prev]
        prev = u
    order += [("mqk_s", 0), ("tp",) + prev, ("pv",) + prev, ("mdec1",)]
    order += [("mqk_s", 1), ("mpv", 0), ("mqk_s", 2), ("mpv", 1), ("mqk_s", 3), ("mpv", 2), ("mdec2",), ("wsk",),
              ("mpv", 3)]
    order += [("hs", 0), ("hs", 1), ("on", 0), ("hs", 2), ("on", 1), ("cfin",), ("ot", 0)]
    for j in range(NTILES):
        order += [(k, j + d) for k, d in (("hs", 3), ("on", 2), ("ot", 1)) if j + d < NTILES]
        order += [("wo", j, 0)]
        order += [("logit", j - 2)] if j >= 2 else []
        order += [("xn", j - 1)] if j else []
        order += [("wo", j, 1)] if j < T4 else []
        order += [("mdec3",)] if j == 2 else []
        order += [("rt", j - 1)] if j else []
    order += [("logit", 3), ("xn", 4), ("rt", 4), ("logit", 4), ("rank",), ("invert",)]
    return order


ORDER = schedule()


def banks_of(item):
    kind = item[0]
    if kind == "xt":
        return ("a0", "a1") if item[1] % 2 == 0 else ("Sa",)
    if kind == "acc":
        return ("a%d" % (item[2] % 2),)
    if kind == "wo":
        return ("a%d" % item[2],)
    if kind == "tp":
        return ("t", "p") if item[1] < NT else ("p",)
    if kind == "tok":
        return ("pt"[item[2] % 2],)
    return {"ot": ("Sa",), "rt": ("Sb",), "gates": ("t", "p"), "small": ("t",), "ft": ("p",),
            "rows": ("t",), "decsm": ("t",), "decmix": ("p", "t"), "decmix2": ("p", "t"), "qk": ("Sa", "Sb"), "pv": ("p",),
            "mqk_s": ("Sa", "Sb", "t", "p"), "mpv": ("a0", "a1"), "mdec2": ("t",), "cfin": ("t",),
            "logit": ("t",), "rank": ("p",), "invert": ("p",)}.get(kind, ())


def fillings():
    count, nth = {}, {}
    for item in ORDER:
        for b in banks_of(item):
            region = b.rstrip("2")
            nth[item, b] = count.get(region, 0)
            count[region] = count.get(region, 0) + 1
    return nth, count


NTH, TOTAL = fillings()
NCONST = 15
NFIN = 5
RSQ8 = [6, 7, 8, 9, 11]
RSQF = [10, 12, 13, 14, 15]
OFF = [0, 512, 896, 1152]


def build(nc, x_prompt, x_sample, cache_k, cache_v, state_C, state_n, state_m, page_table, meta_tokens,
          norm_mix, w_in, b_gates, head_norm_m, lambda_q1, lambda_k1, lambda_q2, lambda_k2, head_norm_da,
          w_out, norm_ffn, w_group, b_group, w_router, b_router, w_gate_e, w_up_e, w_down_e, norm_final,
          y_prompt, y_sample, k_prompt, v_prompt, C_prompt, n_prompt, m_prompt, k_sample, v_sample,
          C_sample, n_sample, m_sample):
    f32, i32, u32 = mybir.dt.float32, mybir.dt.int32, mybir.dt.uint32
    ALU, ACT, AX = mybir.AluOpType, mybir.ActivationFunctionType, mybir.AxisListType
    ctx = ExitStack()
    with ctx:
        def sb(name, shape, dt=f32):
            return ctx.enter_context(nc.sbuf_tensor(name, shape, dt))

        def sem(name):
            return ctx.enter_context(nc.semaphore(name))

        def dram(name, shape):
            return nc.dram_tensor(name, shape, f32, kind="Internal").ap()

        tok_rows = dram("tok_rows", (TOK, D))
        out_rows = dram("out_rows", (2 * SECOND, D))
        dec_q, dec_k = dram("dec_q", (NDEC, 512)), dram("dec_k", (NDEC, 512))
        dec_mq, dec_mk = dram("dec_mq", (NDEC, 256)), dram("dec_mk", (NDEC, 256))
        dec_w = dram("dec_w", (2, NDEC, H))
        dec_ps = dram("dec_ps", (NDEC * 8,))
        g_rows = dram("g_rows", (H, TOK))

        X = sb("X", [128, NTILES, D])
        HO = sb("HO", [128, NTILES, D])
        hT = sb("hT", [128, KC, TOK])
        WS = sb("WS", [128, 18432])
        FT = sb("FT", [128, 12 * TOK])
        DVt = sb("DVt", [128, NTILES, H * DV])
        MVA = sb("MVA", [128, NTILES, H, DV + 1])
        MO = sb("MO", [128, NTILES, H * DV])
        MK = sb("MK", [128, NTILES, H * DQ])
        ident, ones, tri = sb("ident", [128, 128]), sb("ones", [128, 128]), sb("tri", [128, 128])
        maskneg = sb("maskneg", [128, 128])
        gm, gda = sb("gm", [128, DV]), sb("gda", [128, DV])
        gmix, gffn = sb("gmix", [128, KC]), sb("gffn", [128, KC])
        wr = sb("wr", [128, KC, NGRP + NEXP])
        wg = sb("wg", [128, KC, 36])
        br = sb("br", [128, NGRP + NEXP])
        bgi, bgf = sb("bgi", [H, 1]), sb("bgf", [H, 1])
        lamv = sb("lamv", [128, 4, DQ])
        lam = sb("lam", [128, 6])
        neghalf = sb("neghalf", [128, 8])
        ss, rr = sb("ss", [128, 16]), sb("rr", [128, 16])
        ss8, rr8 = sb("ss8", [128, NTILES, 8]), sb("rr8", [128, NTILES, 8])
        RC = sb("RC", [128, NTILES, 68])
        sgn, sgi = sb("sgn", [64, 4]), sb("sgi", [64, 1], i32)
        rsum = sb("rsum", [128, NTILES * H])
        den = sb("den", [128, 3, 1])
        negG_t, c1 = sb("negG", [H, 1]), sb("c1", [128, 1])
        negG = negG_t[:, :]
        nold = sb("nold", [N4, H, DQ])
        cq, dwb = sb("cq", [128, NDEC * H]), sb("dwb", [128, 2, NDEC * H])
        Lt = sb("Lt", [128, NTILES, NGRP + NEXP])
        xf = sb("xf", [1, XBLOCKS])
        pidx = sb("pidx", [128, 1], i32)
        pfl = sb("pfl", [128, 1])
        vT4 = sb("vT4", [128, 4, N4])
        cfin_t = sb("cfin", [128, H, DQ])
        mask1, mask2 = sb("mask1", [128, H]), sb("mask2", [128, H])
        sel = sb("sel", [128, N4])
        tokf = sb("tokf", [128, 2 * NTILES])
        slot_ids = sb("slot_ids", [128, NPAIRS, 2], i32)
        row_ids, out_ids = ([sb("%s%d" % (m, n), [128, 1], i32) for n in range(2)] for m in ("row_ids", "out_ids"))
        sums = sb("sums", [128, 8])
        pages = sb("pages", [128, NDEC * NPAGES], i32)
        Sd = sb("Sd", [128, NPAGES, 64])
        Sq = sb("Sq", [64, PAST + 4])
        Wd = sb("Wd", [128, NPAGES, 32])
        dcol = sb("dcol", [64, 8])
        padT = sb("padT", [128, H, N4])
        qk64 = sb("qk64", [64, 2, DQ])
        dr = sb("dr", [N4, 64])

        dqT = FT[:, 0:4 * TOK].rearrange("p (m t) -> p m t", t=TOK)
        dkT = FT[:, 4 * TOK:8 * TOK].rearrange("p (m t) -> p m t", t=TOK)
        mqkT = FT[:, 8 * TOK:12 * TOK].rearrange("p (m t) -> p m t", t=TOK)
        feat = {"dq": dqT, "dk": dkT, "mqk": mqkT}
        hn = [HO[:, 0, :], HO[:, 1, :]]
        tokst = [HO[:, n // 2, 512 * (n % 2):512 * (n % 2) + 512] for n in range(6)]
        blkslot = [WS[:, 4096 * s:4096 * (s + 1)].rearrange("p (k n) -> p k n", n=512) for s in range(3)]
        SC = WS[:, 12288:18432]
        GB = SC[:, 0:H * TOK].rearrange("p (h t) -> p h t", t=TOK)
        WTs = [(SC[:, o:o + 1280], SC[0:NMETA, o + 1280:o + 1280 + TOK]) for o in (2208, 4040)]
        P2 = [SC[:, o:o + 2 * 528].rearrange("p (m s) -> p m s", m=2) for o in (2208, 4040)]
        AT = SC[:, 5096:5096 + 640].rearrange("p (b t) -> p b t", t=128)
        R = SC[:, 4040:4040 + TOK]
        junk = SC[:, 0:D]
        hoflat = HO[:, 3:5, :].rearrange("p a b -> p (a b)")
        rB, rE, rF, rI = (SC[0:H, 1824 + TOK * n:1824 + TOK * (n + 1)] for n in range(4))
        rA, rG, rM = (hoflat[0:H, TOK * n:TOK * (n + 1)] for n in range(3))
        MQ4 = wg[:, :, :].rearrange("p a b -> p (a b)")[0:N4, 0:256]
        nnew = Sq[0:N4, 0:256].rearrange("p (h d) -> p h d", d=DQ)
        cfin = cfin_t[:, :, :]
        nfin = lamv[:, :, :].rearrange("p a b -> p (a b)")[0:1, 0:256]
        gfin = MK[:, :, :].rearrange("p a b -> p (a b)")[:, 0:D]
        kring = [MO[:, n, :] for n in range(5)]
        vring = kring[:4] + [HO[:, n, 0:512] for n in range(4)]
        C0 = WS[:, 8192:8192 + 2048].rearrange("p (b d) -> p b d", d=DQ)
        QB = WS[:, 10240:10240 + 2048].rearrange("p (b d) -> p b d", d=DQ)
        dvflat = DVt[:, :, :].rearrange("p a b -> p (a b)")
        sqd, junk2 = dvflat[:, 0:D], dvflat[:, D:2 * D]

        bank = [ctx.enter_context(nc.psum_tensor("bank%d" % n, [128, 512], f32)) for n in (0, 1)]
        Sps = ctx.enter_context(nc.psum_tensor("scores", [128, 2, 1024], f32))
        pt_, pp_ = (ctx.enter_context(nc.psum_tensor(n, [128, 512], f32)) for n in ("bank_t", "bank_p"))
        PS = {"a0": bank[0], "a1": bank[1], "t": pt_, "p": pp_}

        filled = {b: sem("filled_" + b) for b in ("a0", "a1", "Sa", "Sb", "t", "p")}
        freed = {b: sem("freed_" + b) for b in ("a0", "a1", "Sa", "Sb", "t", "p")}
        x_in = [sem("x_in%d" % j) for j in range(NTILES)]
        wg_in = sem("wg_in")
        const_in, const_made, pad_zeroed = sem("const_in"), sem("const_made"), sem("pad_zeroed")
        gmix_in, ident_made, dr_zeroed, wg_zeroed = sem("gmix_in"), sem("ident_made"), sem("dr_zeroed"), sem("wg_zeroed")
        gfin_in = sem("gfin_in")
        block_in = [sem("block_in%d" % s) for s in range(3)]
        block_used = sem("block_used")
        squares = sem("squares")
        rsq = sem("rsq")
        sums_ready = sem("sums_ready")
        hn_ready = sem("hn_ready")
        act_step, dve_step, pool_step, sp_step = (sem(n) for n in ("act_step", "dve_step", "pool_step", "sp_step"))
        rows_ln = sem("rows_ln")
        rows_scan = sem("rows_scan")
        rows_exp = sem("rows_exp")
        g_out, g_in, m_out = sem("g_out"), sem("g_in"), sem("m_out")
        tok_out = sem("tok_out")
        sel_made = sem("sel_made")
        dq_out, dk_out, dm_out = sem("dq_out"), sem("dk_out"), sem("dm_out")
        v_out = sem("v_out")
        fin_out = sem("fin_out")
        page_in = [sem("page_in%d" % n) for n in range(5)]
        vpage_in = [sem("vpage_in%d" % n) for n in range(8)]
        page_used = sem("page_used")
        vpage_used = sem("vpage_used")
        pages_ready, ptab_in = sem("pages_ready"), sem("ptab_in")
        qk64_in = sem("qk64_in")
        dec_max, dec_exp, dec_coef = sem("dec_max"), sem("dec_exp"), sem("dec_coef")
        decps_out, decps_in = sem("decps_out"), sem("decps_in")
        pad_ready = sem("pad_ready")
        maxed, mixed = sem("maxed"), sem("mixed")
        lam_sum, lam_exp = sem("lam_sum"), sem("lam_exp")
        decay_made, decay_masked, decay_used, product = (sem(n) for n in (
            "decay_made", "decay_masked", "decay_used", "product"))
        st_in, dw_made, dw_out, dw_in, qb_in, qb_used, kb_in, cn_ready = (sem(n) for n in (
            "st_in", "dw_made", "dw_out", "dw_in", "qb_in", "qb_used", "kb_in", "cn_ready"))
        dm_ready, dm_exp = sem("dm_ready"), sem("dm_exp")
        wsk_ready = sem("wsk_ready")
        ho_ready = sem("ho_ready")
        x2_ready, xn_ready = sem("x2_ready"), sem("xn_ready")
        all_out = sem("all_out")
        xrow_out = sem("xrow_out")
        onehots_ready, ids_ready = sem("onehots_ready"), sem("ids_ready")
        row_ids_made, out_ids_made = ([sem("%s%d" % (m, n)) for n in range(2)] for m in ("row_ids_made", "out_ids_made"))
        gexp_in, gexp = sem("gexp_in"), sem("gexp")
        m_ready, table_ready = sem("m_ready"), sem("table_ready")
        two = lambda n: [sem("%s%d" % (n, s)) for s in range(2)]
        xg_in, xt_filled, xt_evac, gu_filled, silu_done, act_done, at_filled, at_evac, dn_filled, y0, y1, y_out = (
            two(n) for n in ("xg_in", "xt_filled", "xt_evac", "gu_filled", "silu_done", "act_done", "at_filled",
                             "at_evac", "dn_filled", "y_first", "y_second", "y_out"))
        gu_in = [sem("gu_in%d" % n) for n in range(4)]
        dn_in = [sem("dn_in%d" % n) for n in range(4)]
        y_in = [sem("y_in%d" % n) for n in range(NTILES)]
        fsq, yfin = sem("final_squares"), sem("y_final")

        eslot = [WS[:, 12288:18432], FT[:, 0:6144], WS[:, 0:6144], WS[:, 6144:12288]]
        Wgu = [e[:, 0:4096].rearrange("p (g k n) -> p g k n", g=2, n=DE) for e in eslot]
        Wdn = [e[:, 4096:6144].rearrange("p (f n) -> p f n", n=D) for e in eslot]
        XG = [DVt[:, 0:2, :].rearrange("p a b -> p (a b)"), DVt[:, 2:4, :].rearrange("p a b -> p (a b)")]
        mvflat = MVA[:, :, :, :].rearrange("p a b c -> p (a b c)")
        YO = [mvflat[:, 0:D], mvflat[:, D:2 * D]]
        hflat = hT[:, :, :].rearrange("p k t -> p (k t)")
        xT = [hflat[:, 1024 * s:1024 * (s + 1)].rearrange("p (k t) -> p k t", t=128) for s in range(2)]
        SG = [hflat[:, 2048 + 256 * s:2304 + 256 * s] for s in range(2)]
        AB = [hflat[:, 2560 + 256 * s:2816 + 256 * s] for s in range(2)]
        aT = [hflat[:, 3072 + 256 * s:3328 + 256 * s].rearrange("p (f t) -> p f t", t=128) for s in range(2)]
        moflat = MO[:, :, :].rearrange("p a b -> p (a b)")
        at = [0]

        def piece(n):
            at[0] += n
            return moflat[:, at[0] - n:at[0]]

        L = Lt[:, :, :]
        Gx = piece(20).rearrange("p (j g) -> p j g", g=4)
        Go = piece(20).rearrange("p (j g) -> p j g", g=4)
        Gk = piece(20).rearrange("p (j g) -> p j g", g=4)
        E8 = [piece(40).rearrange("p (j e) -> p j e", e=8) for _ in range(5)]
        T160 = piece(160)
        M1, M2, MM = (piece(160) for _ in range(3))
        c5 = [piece(5) for _ in range(12)]
        slot_of, in_pair = (piece(10).rearrange("p (c j) -> p c j", c=2) for _ in range(2))
        slot_int = sb("slot_int", [128, 2, NTILES], i32)
        GONE = piece(NPAIRS)
        PREF, CUM = piece(192), piece(192)
        CX = piece(32 * MAXQ)
        e32 = [piece(32) for _ in range(6)]
        XT32 = piece(XBLOCKS * 32)
        kiota = sb("kiota", [128, 8])
        qiota = sb("qiota", [128, MAXQ])
        eiota = sb("eiota", [128, 32])
        xiota = sb("xiota", [1, XBLOCKS])
        riota = sb("riota", [128, 128])
        piota = sb("piota", [128, NPAIRS])
        iscr = moflat[:, 0:128].bitcast(i32)
        valid = sb("valid", [128, NTILES])
        dump = sb("dump", [128, 2, NTILES])
        in_onehot = hflat[:, 0:1280].rearrange("p (n r) -> p n r", r=128)
        pair_onehot = hflat[:, 1280:1280 + 20 * NPAIRS].rearrange("p (n o a) -> p n o a", n=10, o=2)
        TE = sb("TE", [1, XBLOCKS + 1], i32)
        pw = sb("pw", [128, 2, NTILES])
        YG = [WS[:, 2 * D * j:2 * D * (j + 1)].rearrange("p (c d) -> p c d", c=2) for j in range(NTILES)]

        def before(eng, item, b):
            if NTH[item, b]:
                eng.wait_ge(freed[b.rstrip("2")], NTH[item, b])

        def after(eng, item, b):
            eng.wait_ge(filled[b.rstrip("2")], NTH[item, b] + 1)

        def drained(eng, item, b):
            eng.wait_ge(freed[b.rstrip("2")], NTH[item, b] + 1)

        def reuse(eng, done, turns):
            if not (isinstance(turns, int) and turns == 0):
                eng.wait_ge(done, turns)

        def count(kind, *rest):
            n = 0
            for item in ORDER:
                if item[0] == kind:
                    n += 1
                    if item[1:] == rest:
                        return n

        def further_blocks(eng):
            return eng.value_load(TE[0:1, XBLOCKS:XBLOCKS + 1], min_val=0, max_val=XBLOCKS)

        def loop_further(eng, more, pair):
            with eng.If(more > 0):
                with eng.Fori(PAIRS // 2, (PAIRS + XPAIRS) // 2) as i:
                    for s in range(2):
                        with eng.If(more > 4 * i + 2 * s - 2 * PAIRS):
                            pair(i, s)

        DEC = [(b, p) for b in range(NDEC) for p in range(NPAGES)]
        UIDX = {u: n for n, u in enumerate(UNITS)}
        block = ctx.enter_context(nc.Block())

        @block.sync
        def _(sp):
            for j in range(NT):
                sp.dma_start(X[:, j, :], x_prompt[0, 128 * j:128 * (j + 1), :]).then_inc(x_in[j], 16)
            sp.wait_ge(pad_zeroed, 1)
            sp.dma_start(X[0:NMETA, T4, :], meta_tokens).then_inc(x_in[T4], 16)
            sp.dma_start(X[S0:N4, T4, :], x_sample[:, 0, :]).then_inc(x_in[T4], 16)

            def load_block(n):
                b = BLOCKS[n]
                if n >= 3:
                    sp.wait_ge(block_used, n - 2)
                src = (w_out[0].rearrange("(p k) n -> p k n", k=KC)[:, :, 512 * int(b[2]):512 * int(b[2]) + 512]
                       if b[:2] == "wo" else
                       w_in[0].rearrange("(p k) n -> p k n", k=KC)[:, :, W_COLS[b]:W_COLS[b] + 512])
                sp.dma_start(blkslot[n % 3], src).then_inc(block_in[n % 3], 16)

            def gate_up(s, u, e):
                w = 2 * s + u
                for g, src in enumerate((w_gate_e, w_up_e)):
                    sp.dma_start(Wgu[w][:, g], src[0, e].rearrange("(p k) n -> p k n", k=KC)).then_inc(gu_in[w], 16)

            def down(s, u, e):
                w = 2 * s + u
                sp.dma_start(Wdn[w], w_down_e[0, e].rearrange("(p f) n -> p f n", f=FC)).then_inc(dn_in[w], 16)

            for n in range(3):
                load_block(n)
            for item in ORDER:
                kind = item[0]
                if kind == "small" and PROJ.index(item[1]) + 3 < len(BLOCKS):
                    load_block(PROJ.index(item[1]) + 3)
                if kind == "small":
                    drained(sp, item, "t")
                    if item[1] == "dq":
                        sp.dma_start(dec_q, tokst[0][S0:N4]).then_inc(dq_out, 16)
                    elif item[1] == "dk":
                        s = tokst[1]
                        sp.dma_start(k_prompt[0, 0, 0:NMETA].rearrange("t h d -> t (h d)"),
                                     s[0:NMETA]).then_inc(tok_out, 16)
                        sp.dma_start(k_sample[0, :, 0].rearrange("t h d -> t (h d)"), s[S0:N4]).then_inc(tok_out, 16)
                        sp.dma_start(dec_k, s[S0:N4]).then_inc(dk_out, 16)
                        sp.wait_ge(dk_out, 16)
                        sp.wait_ge(dq_out, 16)
                        sp.dma_start(qk64[:, 0, :], dec_q.rearrange("b (u d) -> (b u) d", d=DQ)).then_inc(qk64_in, 16)
                        sp.dma_start(qk64[:, 1, :], dec_k.rearrange("b (u d) -> (b u) d", d=DQ)).then_inc(qk64_in, 16)
                    elif item[1] == "dv":
                        for i in range(NT):
                            sp.dma_start(v_prompt[0, 0, NMETA + 128 * i:NMETA + 128 * (i + 1)]
                                         .rearrange("t h d -> t (h d)"), DVt[:, i, :]).then_inc(v_out, 16)
                        sp.dma_start(v_prompt[0, 0, 0:NMETA].rearrange("t h d -> t (h d)"),
                                     DVt[0:NMETA, T4, :]).then_inc(v_out, 16)
                        sp.dma_start(v_sample[0, :, 0].rearrange("t h d -> t (h d)"),
                                     DVt[S0:N4, T4, :]).then_inc(v_out, 16)
                    elif item[1] == "mqk":
                        sp.dma_start(dec_mq, MQ4[S0:N4]).then_inc(dm_out, 16)
                        sp.dma_start(dec_mk, MK[S0:N4, T4, :]).then_inc(dm_out, 16)
                elif kind == "tok":
                    name, j = item[1:]
                    if name == "dk":
                        drained(sp, item, "pt"[j % 2])
                        sp.dma_start(k_prompt[0, 0, NMETA + 128 * j:NMETA + 128 * (j + 1)]
                                     .rearrange("t h d -> t (h d)"), tokst[2 + j]).then_inc(tok_out, 16)
                elif kind == "rows":
                    sp.wait_ge(rows_scan, 2)
                    sp.dma_start(g_rows, rG).then_inc(g_out, 16)
                    sp.dma_start(m_prompt[0, 0, :].rearrange("(h a) -> h a", a=1), rM[:, TOK - 1:TOK],
                                 allow_slow_non_contiguous=True).then_inc(m_out, 16)
                    sp.wait_ge(g_out, 16)
                    sp.wait_ge(squares, NTILES)
                    sp.dma_start(GB, g_rows.rearrange("h t -> (h t)").partition_broadcast(128)
                                 .rearrange("p (h t) -> p h t", t=TOK)).then_inc(g_in, 16)
                elif kind == "decmix":
                    sp.wait_ge(dec_coef, 1)
                    sp.dma_start(dec_ps.rearrange("(r a) -> r a", a=1), Sq[:, PAST:PAST + 1],
                                 allow_slow_non_contiguous=True).then_inc(decps_out, 16)
                    sp.wait_ge(decps_out, 16)
                    sp.dma_start(dr[S0:N4, 40:48], dec_ps.rearrange("(b u) -> b u", u=8)).then_inc(decps_in, 16)
                elif kind == "mdec1":
                    sp.wait_ge(block_used, 6)
                    sp.dma_start(C0, state_C[0].rearrange("b h v d -> v (b h) d")).then_inc(st_in, 16)
                    sp.wait_ge(dm_out, 32)
                    sp.dma_start(QB, dec_mq.rearrange("b n -> (b n)").partition_broadcast(128)
                                 .rearrange("p (b d) -> p b d", d=DQ)).then_inc(qb_in, 16)
                    sp.wait_ge(dw_made, 1)
                    sp.dma_start(dec_w[0], dr[S0:N4, 8:12]).then_inc(dw_out, 16)
                    sp.dma_start(dec_w[1], dr[S0:N4, 12:16]).then_inc(dw_out, 16)
                    sp.wait_ge(dw_out, 32)
                    sp.dma_start(dwb[:, :, :], dec_w.rearrange("a b h -> (a b h)").partition_broadcast(128)
                                 .rearrange("p (a b) -> p a b", a=2)).then_inc(dw_in, 16)
                    sp.dma_start(m_sample[0], dr[S0:N4, 4:8]).then_inc(fin_out, 16)
                    sp.wait_ge(qb_used, 1)
                    sp.dma_start(QB, dec_mk.rearrange("b n -> (b n)").partition_broadcast(128)
                                 .rearrange("p (b d) -> p b d", d=DQ)).then_inc(kb_in, 16)
                elif kind == "mdec3":
                    sp.wait_ge(cn_ready, 2)
                    sp.dma_start(C_sample[0].rearrange("b h v d -> v (b h) d"), C0).then_inc(fin_out, 16)
                    sp.dma_start(n_sample[0], nnew[S0:N4]).then_inc(fin_out, 16)
                elif kind == "rt":
                    j = item[1]
                    sp.wait_ge(xn_ready, j + 1)
                    sp.dma_start(tok_rows[128 * j:128 * j + nrows(j)], HO[0:nrows(j), j, :]).then_inc(xrow_out, 16)
                elif kind == "ot" and item[1] == 0:
                    sp.wait_ge(filled["a1"], NTH[("mpv", H - 1), "a1"] + 1)
                    for u in range(2):
                        gate_up(0, u, u)
                    for u in range(2):
                        down(0, u, u)
                elif kind == "cfin":
                    drained(sp, item, "t")
                    sp.dma_start(C_prompt[0, 0].rearrange("h v d -> v h d"), cfin).then_inc(fin_out, 16)
                    sp.dma_start(n_prompt[0, 0].rearrange("h d -> (h d)").rearrange("(a n) -> a n", a=1),
                                 nfin).then_inc(fin_out, 16)
                    sp.dma_start(gfin, norm_final.partition_broadcast(128)).then_inc(gfin_in, 16)

            def pair_loads(i, s, experts, second=None):
                def both(load):
                    load(s, 0, experts[0])
                    if second is None:
                        load(s, 1, experts[1])
                    else:
                        with sp.If(second > 0):
                            load(s, 1, experts[1])
                        with sp.If(second < 1):
                            w = 2 * s + 1
                            sp.nop().then_inc(*((gu_in[w], 32) if load is gate_up else (dn_in[w], 16)))
                sp.wait_ge(gu_filled[s], i)
                both(gate_up)
                sp.wait_ge(dn_filled[s], i)
                both(down)

            sp.wait_ge(fin_out, 16 * NFIN)
            sp.wait_ge(block_used, len(BLOCKS))
            for u in range(2):
                gate_up(1, u, 2 + u)
            for u in range(2):
                down(1, u, 2 + u)
            with sp.Fori(1, PAIRS // 2) as i:
                for s in range(2):
                    pair_loads(i, s, [4 * i + 2 * s, 4 * i + 2 * s + 1])
            sp.wait_ge(table_ready, 1)

            def further_pair(i, s):
                ids = [sp.value_load(TE[0:1, bass.DynSlice(4 * i + 2 * s + u - 2 * PAIRS, 1)],
                                     min_val=0, max_val=NEXP - 1) for u in range(2)]
                pair_loads(i, s, ids, more - (4 * i + 2 * s + 1 - 2 * PAIRS))

            more = further_blocks(sp)
            loop_further(sp, more, further_pair)

            sp.wait_ge(all_out, 1)
            src = out_rows.rearrange("(c t) d -> t c d", c=2)
            for j in range(NT):
                sp.dma_start(YG[j], src[128 * j:128 * (j + 1)]).then_inc(y_in[j], 16)
            sp.dma_start(YG[T4][0:NMETA], src[SEQ:SEQ + NMETA]).then_inc(y_in[T4], 16)
            sp.dma_start(YG[T4][S0:N4], src[SEQ + S0:SEQ + N4]).then_inc(y_in[T4], 16)
            for n, j in enumerate((0, 1, 2, 3, 4)):
                sp.wait_ge(yfin, n + 1)
                if j < NT:
                    sp.dma_start(y_prompt[0, 128 * j:128 * (j + 1), :], X[:, j, :]).then_inc(fin_out, 16)
                else:
                    sp.dma_start(y_sample[:, 0, :], X[S0:N4, T4, :]).then_inc(fin_out, 16)
            sp.wait_ge(fin_out, 16 * (NFIN + NTILES))
            sp.wait_ge(tok_out, 16 * 6)
            sp.wait_ge(v_out, 16 * 6)

        @block.gpsimd
        def _(pool):
            steps = [0]

            def link(ins):
                steps[0] += 1
                ins.then_inc(pool_step, 1)
                pool.wait_ge(pool_step, steps[0])

            pool.dma_start(pages[:, :], page_table.rearrange("b p -> (b p)").partition_broadcast(128)).then_inc(ptab_in, 16)
            link(pool.memset(dr[:, :], 0.0))
            pool.nop().then_inc(dr_zeroed, 1)
            link(pool.memset(ident[:, :], 0.0))
            link(pool.affine_select(out=ident[:, :], in_=ident[:, :], compare_op=ALU.not_equal, fill=1.0,
                                    base=0, pattern=[[-1, 128]], channel_multiplier=1))
            pool.nop().then_inc(ident_made, 1)
            link(pool.memset(maskneg[:, :], 0.0))
            link(pool.memset(ones[:, :], 1.0))
            link(pool.affine_select(out=maskneg[:, :], in_=maskneg[:, :], compare_op=ALU.is_ge, fill=-1e30,
                                    base=0, pattern=[[-1, 128]], channel_multiplier=1))
            link(pool.affine_select(out=tri[:, :], in_=ones[:, :], compare_op=ALU.is_gt, fill=0.0,
                                    base=0, pattern=[[1, 128]], channel_multiplier=-1))
            link(pool.memset(neghalf[:, :], -0.5))
            link(pool.iota(pidx[:, :], [[0, 1]], base=0, channel_multiplier=1))
            link(pool.iota(iscr[:, 0:8], [[-1, 8]], base=8, channel_multiplier=0))
            link(pool.tensor_copy(kiota[:, :], iscr[:, 0:8]))
            link(pool.iota(iscr[:, 0:MAXQ], [[SLOTS, MAXQ]], base=SLOTS, channel_multiplier=0))
            link(pool.tensor_copy(qiota[:, :], iscr[:, 0:MAXQ]))
            link(pool.iota(iscr[:, 0:32], [[SLOTS, 32]], base=0, channel_multiplier=0))
            link(pool.tensor_copy(eiota[:, :], iscr[:, 0:32]))
            link(pool.iota(iscr[:, 0:XBLOCKS], [[1, XBLOCKS]], base=0, channel_multiplier=0))
            link(pool.tensor_copy(xiota[:, :], iscr[0:1, 0:XBLOCKS]))
            link(pool.iota(iscr[:, :], [[1, 128]], base=0, channel_multiplier=0))
            link(pool.tensor_copy(riota[:, :], iscr[:, :]))
            link(pool.iota(iscr[:, 0:NPAIRS], [[128, NPAIRS]], base=0, channel_multiplier=0))
            link(pool.tensor_copy(piota[:, :], iscr[:, 0:NPAIRS]))
            link(pool.iota(iscr[:, 0:2 * NTILES], [[SECOND, 2], [128, NTILES]], base=0, channel_multiplier=1))
            link(pool.tensor_copy(tokf[:, :], iscr[:, 0:2 * NTILES]))
            link(pool.memset(valid[:, 0:NT], 1.0))
            link(pool.memset(valid[:, NT:], 0.0))
            link(pool.memset(valid[0:NMETA, NT:], 1.0))
            link(pool.memset(valid[S0:N4, NT:], 1.0))
            pool.nop().then_inc(const_made, 1)

            roots = [0]

            def decode_masks():
                for m, o in ((mask1, 0), (mask2, 16)):
                    link(pool.memset(m[:, :], 0.0))
                    for g in range(4):
                        link(pool.affine_select(out=m[:, :], in_=m[:, :], compare_op=ALU.not_equal, fill=1.0,
                                                base=-(36 * g + o), pattern=[[-1, H]], channel_multiplier=1))
                link(pool.memset(sel[:, :], 0.0))
                for g in range(4):
                    for h in range(H):
                        link(pool.affine_select(out=sel[:, S0:N4], in_=sel[:, S0:N4], compare_op=ALU.not_equal, fill=1.0,
                                                base=-(32 * g + h), pattern=[[-H, NDEC]], channel_multiplier=1))
                pool.nop().then_inc(sel_made, 1)

            def rsqrt(dst, src, width, wait_sem, wait_val):
                pool.wait_ge(wait_sem, wait_val)
                link(pool.tensor_scalar(dst, src, 1.0 / width, EPS, ALU.mult, ALU.add))
                n = dst.shape[1]
                pool.tensor_tensor(dst, dst, neghalf[0:dst.shape[0], 0:n], ALU.pow).then_inc(rsq, 1)
                roots[0] += 1
                pool.wait_ge(rsq, roots[0])

            for j in range(NTILES):
                n = nrows(j)
                rsqrt(rr[0:n, j:j + 1], ss[0:n, j:j + 1], D, squares, j + 1)

            def gather(dst, cache, b, p, signal):
                pool.indirect_dma_start(
                    dst, None, cache[0].rearrange("n t h d -> (n t) (h d)"),
                    bass.IndirectOffsetOnAxis(ap=pages[:, b * NPAGES + p:b * NPAGES + p + 1].bitcast(u32), axis=0))\
                    .then_inc(signal, 16)

            pool.wait_ge(pages_ready, 1)
            for n, (b, p) in enumerate(DEC):
                if n >= 4:
                    pool.wait_ge(page_used, n - 3)
                gather(kring[n % 4], cache_k, b, p, page_in[n % 4])
                if p == 0:
                    if n == 0:
                        pool.wait_ge(dq_out, 16)
                    if b:
                        pool.wait_ge(page_used, 2 * b)
                    pool.dma_start(kring[4], dec_q[b].partition_broadcast(128)).then_inc(page_in[4], 16)
                if n == 3:
                    decode_masks()
            for n, (b, p) in enumerate(DEC):
                if n < 4:
                    pool.wait_ge(page_used, n + 13)
                elif n == 4:
                    pool.wait_ge(tok_out, 16 * 6)
                    pool.wait_ge(rows_exp, 1)
                elif n >= 8:
                    pool.wait_ge(vpage_used, n - 7)
                gather(vring[n % 8], cache_v, b, p, vpage_in[n % 8])

            for h in range(H):
                WT, WTm = WTs[h % 2]
                pool.wait_ge(decay_made, h + 1)
                for i in range(NT):
                    blk = WT[:, OFF[i]:OFF[i] + 128]
                    link(pool.affine_select(out=blk, in_=blk, compare_op=ALU.is_ge, fill=0.0, base=0,
                                            pattern=[[1, 128]], channel_multiplier=-1))
                pool.affine_select(out=WTm[:, 0:NMETA], in_=WTm[:, 0:NMETA], compare_op=ALU.is_ge, fill=0.0, base=0,
                                   pattern=[[1, NMETA]], channel_multiplier=-1).then_inc(decay_masked, 1)
                pool.wait_ge(decay_masked, h + 1)

            for j in range(NTILES + 3):
                if j < NTILES:
                    n = nrows(j)
                    rsqrt(rr8[0:n, j, :], ss8[0:n, j, :], DV, sums_ready, j + 1)
                if j >= 3:
                    n = nrows(j - 3)
                    rsqrt(rr[0:n, 2 + j:3 + j], ss[0:n, 2 + j:3 + j], D, squares, NTILES + j - 2)

            pool.wait_ge(ids_ready, 1)
            pool.wait_ge(xrow_out, 16 * NTILES)

            xt_due, row_ids_due, y_due, out_ids_due, out_due = (
                [pool.alloc_register("%s%d" % (n, s)) for s in range(2)]
                for n in ("xt_due", "row_ids_due", "y_due", "out_ids_due", "out_due"))
            for s in range(2):
                for due, first in ((xt_due, 1), (row_ids_due, 1), (y_due, 1), (out_ids_due, 1), (out_due, 0)):
                    pool.reg_mov(due[s], first)

            def await_due(semaphore, due, step=1):
                pool.wait_ge(semaphore, due)
                pool.reg_add(due, due, step)

            def fetch(i, s):
                if not isinstance(i, int) or i:
                    await_due(xt_filled[s], xt_due[s])
                pool.tensor_copy(row_ids[s][:, :], slot_ids[:, bass.DynSlice(2 * i + s, 1), 0])\
                    .then_inc(row_ids_made[s], 1)
                await_due(row_ids_made[s], row_ids_due[s])
                pool.indirect_dma_start(XG[s], None, tok_rows,
                                        bass.IndirectOffsetOnAxis(ap=row_ids[s][:, :].bitcast(u32), axis=0),
                                        bounds_check=TOK - 1, oob_is_err=False).then_inc(xg_in[s], 16)

            def store(i, s):
                pool.wait_ge(y0[s], y_due[s])
                await_due(y1[s], y_due[s])
                pool.tensor_copy(out_ids[s][:, :], slot_ids[:, bass.DynSlice(2 * i + s, 1), 1])\
                    .then_inc(out_ids_made[s], 1)
                await_due(out_ids_made[s], out_ids_due[s])
                pool.reg_add(out_due[s], out_due[s], 16)
                pool.indirect_dma_start(out_rows, bass.IndirectOffsetOnAxis(ap=out_ids[s][:, :].bitcast(u32), axis=0),
                                        YO[s], None, bounds_check=2 * SECOND - 1, oob_is_err=False).then_inc(y_out[s], 16)

            for s in range(2):
                fetch(0, s)
            with pool.Fori(1, PAIRS // 2) as i:
                for s in range(2):
                    fetch(i, s)
                    store(i - 1, s)
            more = further_blocks(pool)
            for s in range(2):
                with pool.If(more > 2 * s):
                    fetch(PAIRS // 2, s)
                store(PAIRS // 2 - 1, s)
            with pool.If(more > 0):
                with pool.Fori(PAIRS // 2, (PAIRS + XPAIRS) // 2) as i:
                    for s in range(2):
                        with pool.If(more > 4 * i + 2 * s - 2 * PAIRS):
                            with pool.If(more > 4 * i + 4 + 2 * s - 2 * PAIRS):
                                fetch(i + 1, s)
                            store(i, s)
            for s in range(2):
                pool.wait_ge(y_out[s], out_due[s])
            pool.nop().then_inc(all_out, 1)
            for j in range(NTILES):
                n = nrows(j)
                rsqrt(rr[0:n, 10 + j:11 + j], ss[0:n, 10 + j:11 + j], D, fsq, j + 1)

        @block.scalar
        def _(act):
            steps = [0]

            def link(ins):
                steps[0] += 1
                ins.then_inc(act_step, 1)
                act.wait_ge(act_step, steps[0])

            act.dma_start(gmix[:, :], norm_mix[0].rearrange("(p k) -> p k", k=KC)).then_inc(gmix_in, 16)
            small = [(gffn[:, :], norm_ffn[0].rearrange("(p k) -> p k", k=KC)),
                     (bgi[:, :], b_gates[0, 0:H].rearrange("(h a) -> h a", a=1)),
                     (bgf[:, :], b_gates[0, H:2 * H].rearrange("(h a) -> h a", a=1)),
                     (wr[:, :, 0:NGRP], w_group[0].rearrange("(p k) n -> p k n", k=KC)),
                     (wr[:, :, NGRP:], w_router[0].rearrange("(p k) n -> p k n", k=KC)),
                     (br[:, 0:NGRP], b_group[0].partition_broadcast(128)),
                     (br[:, NGRP:], b_router[0].partition_broadcast(128)),
                     (gm[:, :], head_norm_m[0].partition_broadcast(128)),
                     (gda[:, :], head_norm_da[0].partition_broadcast(128)),
                     (nold[S0:N4], state_n[0]),
                     (dr[S0:N4, 0:4], state_m[0])]
            small += [(lamv[:, n, :], v[0].partition_broadcast(128))
                      for n, v in enumerate((lambda_q1, lambda_k1, lambda_q2, lambda_k2))]
            g = w_in[0].rearrange("(p k) n -> p k n", k=KC)[:, :, W_COLS["gates"]:W_COLS["gates"] + 8]
            act.wait_ge(wg_zeroed, 1)
            act.dma_start(wg[:, :, 0:H], g[:, :, 0:H]).then_inc(wg_in, 16)
            act.dma_start(wg[:, :, 32:32 + H], g[:, :, H:2 * H]).then_inc(wg_in, 16)
            act.wait_ge(ident_made, 1)
            link(act.activation(lam[:, 5:6], ident[:, 0:1], ACT.Square))
            for j in range(NTILES):
                n = nrows(j)
                act.wait_ge(x_in[j], 16 if j < NT else 32)
                if j:
                    act.wait_ge(squares, j)
                act.activation(junk[0:n, :], X[0:n, j, :], ACT.Square, accum_out=ss[0:n, j:j + 1]).then_inc(squares, 1)
            act.wait_ge(dr_zeroed, 1)
            assert len(small) == NCONST
            for dst, src in small:
                act.dma_start(dst, src, allow_slow_non_contiguous=True).then_inc(const_in, 16)

            act.wait_ge(const_in, 16 * NCONST)

            def copy(dst, src, scale=1.0):
                return act.activation(dst, src, ACT.Copy, scale=scale)

            for item in ORDER:
                kind = item[0]
                if kind == "gates":
                    after(act, item, "t")
                    after(act, item, "p")
                    act.activation(rI[:, 0:N4], PS["p"][0:H, 0:N4], ACT.Identity, bias=bgi[:, :])
                    act.activation(rI[:, N4:TOK], PS["t"][0:H, :], ACT.Identity, bias=bgi[:, :])
                    act.activation(rF[:, 0:N4], PS["p"][32:32 + H, 0:N4], ACT.Identity, bias=bgf[:, :]).then_inc(freed["p"], 1)
                    act.activation(rF[:, N4:TOK], PS["t"][32:32 + H, :], ACT.Identity, bias=bgf[:, :]).then_inc(freed["t"], 1)
                    drained(act, item, "t")
                    link(act.activation(rE[:, :], rF[:, :], ACT.Abs))
                    link(act.activation(rE[:, :], rE[:, :], ACT.Exp, scale=-1.0))
                    act.activation(rE[:, :], rE[:, :], ACT.Ln, bias=1.0).then_inc(rows_ln, 1)
                elif kind == "acc":
                    b, m = item[1:]
                    after(act, item, "a%d" % (m % 2))
                    src = PS["a%d" % (m % 2)]
                    if b in FEATURE:
                        scale = DQ ** -0.5 if b == "dq" or (b == "mqk" and m >= 2) else 1.0
                        ins = copy(feat[b][:, m, 0:512], src[:, :], scale)
                    elif b == "dv":
                        ins = copy(DVt[:, m, :], src[:, :])
                    elif b == "mv":
                        ins = copy(MVA[:, m, :, 0:DV], src[:, :].rearrange("p (h d) -> p h d", d=DV))
                    else:
                        if m == 0:
                            after(act, ("decmix2",), "t")
                        ins = act.activation(MO[:, m, :], src[:, :], ACT.Exp, scale=-1.0)
                    ins.then_inc(freed["a%d" % (m % 2)], 1)
                elif kind == "small":
                    b = item[1]
                    after(act, item, "t")
                    for u in range(2):
                        src = PS["t"][64 * u:64 * u + N4, 0:256]
                        cols = slice(256 * u, 256 * u + 256)
                        if b == "dq":
                            ins = copy(tokst[0][0:N4, cols], src, DQ ** -0.5)
                        elif b == "dk":
                            ins = copy(tokst[1][0:N4, cols], src)
                        elif b == "mqk":
                            ins = copy(MK[0:N4, T4, :], src, DQ ** -0.5) if u else copy(MQ4, src)
                        elif b == "dv":
                            ins = copy(DVt[0:N4, T4, cols], src)
                        elif b == "mv":
                            ins = copy(MVA[0:N4, T4, 2 * u:2 * u + 2, 0:DV], src.rearrange("p (h d) -> p h d", d=DV))
                        else:
                            ins = act.activation(MO[0:N4, T4, cols], src, ACT.Exp, scale=-1.0)
                    ins.then_inc(freed["t"], 1)
                elif kind == "ft":
                    b = item[1]
                    after(act, item, "p")
                    src = PS["p"][:, 0:4 * N4].rearrange("p (m t) -> p m t", t=N4)
                    copy(vT4[:, :, :] if b == "mv" else feat[b][:, :, 512:TOK], src).then_inc(freed["p"], 1)
                elif kind == "tok":
                    name, j = item[1:]
                    r = "pt"[j % 2]
                    after(act, item, r)
                    if name == "dk":
                        ins = copy(tokst[2 + j], PS[r][:, :])
                    else:
                        ins = copy(MK[:, j, :], PS[r][:, 0:256])
                    ins.then_inc(freed[r], 1)
                elif kind == "rows":
                    act.wait_ge(rows_scan, 3)
                    link(act.activation(R[32:32 + H, :], rA[:, :], ACT.Exp, bias=negG))
                    link(copy(R[32:32 + H, S0:N4], rF[:, S0:N4]))
                    act.activation(R[64:64 + H, :], rM[:, :], ACT.Exp, scale=-1.0).then_inc(rows_exp, 1)
                    after(act, item, "t")
                    copy(RC[:, 0:NT, :], PS["t"][:, 0:NT * 68].rearrange("p (j r) -> p j r", r=68))
                    copy(RC[0:N4, T4, :], PS["t"][0:N4, NT * 68:NTILES * 68]).then_inc(freed["t"], 1)
                    act.wait_ge(lam_sum, 1)
                    act.activation(lam[:, 2:4], lam[:, 0:2], ACT.Exp).then_inc(lam_exp, 1)
                elif kind == "decsm":
                    act.wait_ge(dec_max, 1)
                    act.activation(Sq[:, 0:PAST + 1], Sq[:, 0:PAST + 1], ACT.Exp, bias=dcol[:, 1:2],
                                   accum_out=dcol[:, 2:3]).then_inc(dec_exp, 1)
                elif kind == "qk":
                    j, h = item[1:]
                    n = 128 if j < NT else NMETA
                    w = 128 * (j + 1) + NMETA if j < NT else NMETA
                    u = UIDX[j, h]
                    act.wait_ge(maxed, u + 1)
                    P = P2[u % 2]
                    act.activation(P[0:n, 0, 0:w], Sps[0:n, 0, 0:w], ACT.Exp, bias=sums[0:n, 0:1],
                                   accum_out=sums[0:n, 2:3]).then_inc(freed["Sa"], 1)
                    act.activation(P[0:n, 1, 0:w], Sps[0:n, 1, 0:w], ACT.Exp, bias=sums[0:n, 1:2],
                                   accum_out=sums[0:n, 3:4]).then_inc(freed["Sb"], 1)
                elif kind == "tp":
                    j, h = item[1:]
                    n = 128 if j < NT else NMETA
                    after(act, item, "p")
                    if j < NT:
                        after(act, item, "t")
                        copy(AT[:, 0:j + 1, 0:n], PS["t"][:, 0:128 * (j + 1)].rearrange("p (b t) -> p b t", t=128))\
                            .then_inc(freed["t"], 1)
                    copy(AT[0:NMETA, 4, 0:n], PS["p"][0:NMETA, 0:n]).then_inc(freed["p"], 1)
                elif kind == "pv":
                    j, h = item[1:]
                    n = 128 if j < NT else NMETA
                    after(act, item, "p")
                    if UIDX[j, h] == 0:
                        act.wait_ge(tok_out, 16 * 6)
                    act.activation(HO[0:n, j, 512 + DV * h:512 + DV * (h + 1)], PS["p"][0:n, 0:DV], ACT.Copy,
                                   scale=rsum[0:n, UIDX[j, h]:UIDX[j, h] + 1]).then_inc(freed["p"], 1)
                elif kind == "mqk_s":
                    h = item[1]
                    WT, WTm = WTs[h % 2]
                    if h == 0:
                        act.wait_ge(g_in, 16)
                    if h >= 2:
                        after(act, ("mpv", h - 2), "a1")
                    for i in range(NT):
                        act.activation(WT[:, OFF[i]:OFF[i] + 512 - 128 * i], GB[:, h, N4 + 128 * i:TOK], ACT.Exp,
                                       scale=-1.0, bias=RC[:, i, h:h + 1])
                    act.activation(WTm[:, 0:NMETA], GB[0:NMETA, h, 0:NMETA], ACT.Exp, scale=-1.0, bias=RC[0:NMETA, T4, h:h + 1])
                    act.activation(WTm[:, N4:TOK], GB[0:NMETA, h, N4:TOK], ACT.Exp, scale=-1.0,
                                   bias=RC[0:NMETA, T4, h:h + 1]).then_inc(decay_made, 1)
                elif kind == "mdec1":
                    act.wait_ge(dm_ready, 1)
                    act.activation(dr[S0:N4, 8:16], dr[S0:N4, 16:24], ACT.Exp).then_inc(dm_exp, 1)
                    act.activation(dr[S0:N4, 24:28], dr[S0:N4, 4:8], ACT.Exp, scale=-1.0).then_inc(dm_exp, 1)
                elif kind == "cfin":
                    after(act, item, "t")
                    copy(cfin, PS["t"][:, 0:H * DQ].rearrange("p (h d) -> p h d", d=DQ))
                    copy(nfin, PS["t"][0:1, 256:512]).then_inc(freed["t"], 1)
                elif kind == "hs":
                    j = item[1]
                    n = nrows(j)
                    if j == 0:
                        drained(act, ("mpv", H - 1), "a1")
                        drained(act, ("pv",) + UNITS[-1], "p")
                        act.wait_ge(v_out, 16 * 6)
                    else:
                        act.wait_ge(sums_ready, j)
                    for u in range(8):
                        c = slice(DV * u, DV * (u + 1))
                        ins = act.activation(sqd[0:n, c], HO[0:n, j, c], ACT.Square, accum_out=ss8[0:n, j, u:u + 1])
                    ins.then_inc(sums_ready, 1)
                elif kind == "ot":
                    j = item[1]
                    n = nrows(j)
                    after(act, item, "Sa")
                    for half in range(2):
                        ins = copy(hT[:, 4 * half:4 * half + 4, col(j):col(j) + n],
                                   Sps[:, 0, 512 * half:512 * half + 512].rearrange("p (k t) -> p k t", t=128)[:, :, 0:n])
                    ins.then_inc(freed["Sa"], 1)
                elif kind == "wo" and (item[2] == 1 or item[1] == T4):
                    j = item[1]
                    n = nrows(j)
                    drained(act, item, "a%d" % item[2])
                    act.wait_ge(squares, NTILES + j)
                    act.activation(junk2[0:n, :], X[0:n, j, :], ACT.Square,
                                   accum_out=ss[0:n, 5 + j:6 + j]).then_inc(squares, 1)
                elif kind == "rank":
                    act.wait_ge(gexp_in, 1)
                    act.activation(Gx, Gx, ACT.Exp).then_inc(gexp, 1)
                    act.wait_ge(gexp_in, 2)
                    act.activation(c5[5], c5[4], ACT.Exp).then_inc(gexp, 1)

            def silu(i, s):
                act.wait_ge(gu_filled[s], i + 1)
                reuse(act, act_done[s], i)
                act.activation(SG[s], PS["t" if s else "p"][:, 0:DE], ACT.Silu).then_inc(silu_done[s], 1)

            def pair(i, s):
                silu(i, s)
                act.wait_ge(at_filled[s], i + 1)
                reuse(act, dn_filled[s], i)
                copy(aT[s], Sps[:, 1, 512:768].rearrange("p (f t) -> p f t", t=128)).then_inc(at_evac[s], 1)
                act.wait_ge(dn_filled[s], i + 1)
                reuse(act, y_out[s], 16 * i)
                copy(YO[s][:, 0:512], Sps[:, 0, 0:512]).then_inc(y0[s], 1)

            for s in range(2):
                pair(0, s)
            with act.Fori(1, PAIRS // 2) as i:
                for s in range(2):
                    pair(i, s)
            act.wait_ge(table_ready, 1)
            loop_further(act, further_blocks(act), pair)
            for j in range(NTILES):
                n = nrows(j)
                act.wait_ge(x2_ready, j + 1)
                if j:
                    act.wait_ge(fsq, j)
                act.activation(junk2[0:n, :], X[0:n, j, :], ACT.Square,
                               accum_out=ss[0:n, 10 + j:11 + j]).then_inc(fsq, 1)

        @block.vector
        def _(dve):
            v = nc.vector
            steps = [0]

            def link(ins):
                steps[0] += 1
                ins.then_inc(dve_step, 1)
                dve.wait_ge(dve_step, steps[0])

            v.memset(X[0:N4, T4, :], 0.0).then_inc(pad_zeroed, 1)
            v.memset(wg[:, :, :], 0.0).then_inc(wg_zeroed, 1)
            link(v.memset(R[:, :], 0.0))
            link(v.memset(padT[:, :, :], 0.0))
            link(v.memset(MVA[:, :, :, DV:DV + 1], 1.0))
            dve.wait_ge(const_made, 1)
            dve.wait_ge(ptab_in, 16)
            link(v.tensor_copy(pfl[:, :], pidx[:, :]))
            v.tensor_scalar(pages[:, :], pages[:, :], float(PAGE), pfl[:, :], ALU.mult, ALU.add).then_inc(pages_ready, 1)
            for c in range(2):
                link(v.tensor_scalar(dump[:, c, :], valid[:, :], -1.0, 1.0, ALU.mult, ALU.add))
                link(v.tensor_scalar(c1[:, :], pfl[:, :], float(DUMP + 64 * c), None, ALU.add))
                link(v.tensor_scalar(dump[:, c, :], dump[:, c, :], c1[:, :], None, ALU.mult))

            def transposed(item, src_banks, g, j):
                n = nrows(j)
                for half in range(2):
                    b, src = src_banks[half]
                    if b is not None:
                        after(dve, item, b)
                    o = hT[:, 4 * half:4 * half + 4, col(j):col(j) + n]
                    s_ = src[:, :].rearrange("p (k t) -> p k t", t=128)[:, :, 0:n]
                    if g is None:
                        ins = v.tensor_copy(o, s_)
                    else:
                        ins = v.tensor_tensor(o, s_, g[:, 4 * half:4 * half + 4, None].to_broadcast([128, 4, n]), ALU.mult)
                    if b in ("a0", "a1"):
                        ins.then_inc(freed[b], 1)
                    elif half == 1:
                        ins.then_inc(freed[src_banks[0][0]], 1)

            def tbanks(item):
                if banks_of(item) == ("a0", "a1"):
                    return [("a0", bank[0]), ("a1", bank[1])]
                b = banks_of(item)[0]
                return [(b, Sps[:, b == "Sb", 0:512]), (None, Sps[:, b == "Sb", 512:1024])]

            def decode_state(kind, item):
                r8 = slice(S0, N4)
                ig, lf = RC[r8, T4, 0:4], RC[r8, T4, 32:36]
                if kind == "mdec1":
                    dve.wait_ge(const_in, 16 * NCONST)
                    link(v.tensor_tensor(dr[r8, 28:32], dr[r8, 0:4], lf, ALU.add))
                    link(v.tensor_tensor(dr[r8, 4:8], dr[r8, 28:32], ig, ALU.max))
                    link(v.tensor_tensor(dr[r8, 16:20], dr[r8, 28:32], dr[r8, 4:8], ALU.subtract))
                    v.tensor_tensor(dr[r8, 20:24], ig, dr[r8, 4:8], ALU.subtract).then_inc(dm_ready, 1)
                    dve.wait_ge(dm_exp, 2)
                    v.nop().then_inc(dw_made, 1)
                    drained(dve, ("small", "mqk"), "t")
                    q = MQ4[r8].rearrange("p (h d) -> p h d", d=DQ)
                    k = MK[r8, T4, :].rearrange("p (h d) -> p h d", d=DQ)
                    link(v.tensor_tensor(nnew[r8], q, k, ALU.mult))
                    link(v.tensor_reduce(dr[r8, 32:36], nnew[r8], AX.X, ALU.add))
                    link(v.tensor_tensor(nnew[r8], q, nold[r8], ALU.mult))
                    link(v.tensor_reduce(dr[r8, 36:40], nnew[r8], AX.X, ALU.add))
                    link(v.tensor_tensor(dr[r8, 32:36], dr[r8, 32:36], dr[r8, 12:16], ALU.mult))
                    link(v.tensor_tensor(dr[r8, 36:40], dr[r8, 36:40], dr[r8, 8:12], ALU.mult))
                    link(v.tensor_tensor(dr[r8, 36:40], dr[r8, 36:40], dr[r8, 32:36], ALU.add))
                    link(v.scalar_tensor_tensor(dr[r8, 60:64], dr[r8, 36:40], -1.0, dr[r8, 24:28], ALU.mult, ALU.max))
                    link(v.tensor_tensor(dr[r8, 36:40], dr[r8, 36:40], dr[r8, 60:64], ALU.max))
                    link(v.reciprocal(dr[r8, 36:40], dr[r8, 36:40]))
                    link(v.tensor_tensor(dr[r8, 52:56], dr[r8, 32:36], dr[r8, 36:40], ALU.mult))
                    link(v.tensor_tensor(dr[r8, 56:60], dr[r8, 8:12], dr[r8, 36:40], ALU.mult))
                    link(v.tensor_tensor(nold[r8], nold[r8], dr[r8, 8:12, None].to_broadcast([NDEC, H, DQ]), ALU.mult))
                    link(v.tensor_tensor(nnew[r8], k, dr[r8, 12:16, None].to_broadcast([NDEC, H, DQ]), ALU.mult))
                    v.tensor_tensor(nnew[r8], nnew[r8], nold[r8], ALU.add).then_inc(cn_ready, 1)
                    dve.wait_ge(st_in, 16)
                    dve.wait_ge(qb_in, 16)
                    link(v.tensor_tensor(QB, QB, C0, ALU.mult))
                    v.tensor_reduce(cq[:, :], QB, AX.X, ALU.add).then_inc(qb_used, 1)
                    dve.wait_ge(qb_used, 1)
                    v.tensor_copy(padT[:, :, S0:N4], cq[:, :].rearrange("p (b h) -> p h b", h=H)).then_inc(pad_ready, 1)
                elif kind == "mdec2":
                    after(dve, item, "t")
                    for h in range(H):
                        link(v.tensor_scalar(HO[r8, T4, DV * h:DV * (h + 1)], PS["t"][r8, DV * h:DV * (h + 1)],
                                             dr[r8, 56 + h:57 + h], None, ALU.mult))
                    v.nop().then_inc(freed["t"], 1)
                    for h in range(H):
                        link(v.scalar_tensor_tensor(HO[r8, T4, DV * h:DV * (h + 1)], MVA[r8, T4, h, 0:DV], dr[r8, 52 + h:53 + h],
                                                    HO[r8, T4, DV * h:DV * (h + 1)], ALU.mult, ALU.add))
                elif kind == "mdec3":
                    dve.wait_ge(dw_in, 16)
                    dve.wait_ge(kb_in, 16)
                    dve.wait_ge(pad_ready, 1)
                    drained(dve, ("ft", "mv"), "p")
                    link(v.tensor_tensor(cq[:, :].rearrange("p (b h) -> p b h", h=H),
                                         vT4[:, :, S0:N4].rearrange("p h b -> p b h"),
                                         dwb[:, 1, :].rearrange("p (b h) -> p b h", h=H), ALU.mult))
                    link(v.tensor_tensor(QB, QB, cq[:, :, None].to_broadcast([128, 32, DQ]), ALU.mult))
                    link(v.tensor_tensor(C0, C0, dwb[:, 0, :, None].to_broadcast([128, 32, DQ]), ALU.mult))
                    v.tensor_tensor(C0, C0, QB, ALU.add).then_inc(cn_ready, 1)
                elif kind == "wsk":
                    drained(dve, ("tok", "mk", NT - 1), "pt"[(NT - 1) % 2])
                    for j in range(NTILES):
                        n = 128 if j < NT else NMETA
                        link(v.tensor_tensor(MK[0:n, j, :].rearrange("p (h d) -> p h d", d=DQ),
                                             MK[0:n, j, :].rearrange("p (h d) -> p h d", d=DQ),
                                             RC[0:n, j, 32:36, None].to_broadcast([n, H, DQ]), ALU.mult))
                    v.nop().then_inc(wsk_ready, 1)
                else:
                    j = item[1]
                    n = nrows(j)
                    drained(dve, ("acc", "mo", j) if j < NT else ("small", "mo"), "a%d" % (j % 2) if j < NT else "t")
                    mo = MO[0:n, j, :]
                    link(v.tensor_scalar(mo, mo, 1.0, None, ALU.add))
                    link(v.reciprocal(mo, mo))
                    mo = mo.rearrange("p (h d) -> p h d", d=DV)
                    link(v.tensor_tensor(mo, mo, gm[0:n, None, :].to_broadcast([n, 4, DV]), ALU.mult))

            def mask_products(b, m, dst):
                dve.wait_ge(sel_made, 1)
                after(dve, item, b)
                v.tensor_tensor(dst.rearrange("p (h d) -> p h d", d=DV), PS[b][:, :].rearrange("p (h d) -> p h d", d=DV),
                                m[:, :, None].to_broadcast([128, H, DV]), ALU.mult).then_inc(freed[b], 1)

            for item in ORDER:
                kind = item[0]
                if kind == "xt":
                    j = item[1]
                    n = nrows(j)
                    for i in ((0, 1) if j == 0 else (j + 1,) if j + 1 < NTILES else ()):
                        n = nrows(i)
                        dve.wait_ge(rsq, i + 1)
                        v.tensor_scalar(hn[i % 2][0:n], X[0:n, i, :], rr[0:n, i:i + 1], None, ALU.mult).then_inc(hn_ready, 1)
                    if j == 0:
                        dve.wait_ge(gmix_in, 16)
                    transposed(item, tbanks(item), gmix, j)
                elif kind == "gates":
                    dve.wait_ge(const_in, 16 * NCONST)
                    link(v.tensor_tensor(lamv[:, 0, :], lamv[:, 0, :], lamv[:, 1, :], ALU.mult))
                    link(v.tensor_tensor(lamv[:, 1, :], lamv[:, 2, :], lamv[:, 3, :], ALU.mult))
                    v.tensor_reduce(lam[:, 0:2], lamv[:, 0:2, :], AX.X, ALU.add).then_inc(lam_sum, 1)
                    dve.wait_ge(rows_ln, 1)
                    link(v.scalar_tensor_tensor(rF, rF, 0.0, rE, ALU.min, ALU.subtract))
                    link(v.memset(rE, 1.0))
                    link(v.tensor_copy(rB, rF))
                    link(v.memset(rB[:, NMETA:N4], 0.0))
                    link(v.tensor_tensor_scan(rB, rE, rB, 0.0, ALU.mult, ALU.add))
                    link(v.tensor_tensor(rA, rI, rB, ALU.subtract))
                    link(v.memset(rA[:, NMETA:N4], -1e30))
                    v.tensor_tensor_scan(rG, rE, rA, 0.0, ALU.mult, ALU.max).then_inc(rows_scan, 1)
                    dve.wait_ge(rows_scan, 1)
                    v.tensor_tensor(rM, rB, rG, ALU.add).then_inc(rows_scan, 1)
                    link(v.tensor_scalar(negG, rG[:, TOK - 1:TOK], -1.0, None, ALU.mult))
                    dve.wait_ge(rows_scan, 2)
                    link(v.tensor_copy(R[0:H, :], rA))
                    v.tensor_copy(R[0:H, S0:N4], rI[:, S0:N4]).then_inc(rows_scan, 1)
                elif kind == "rows":
                    dve.wait_ge(lam_exp, 1)
                    dve.wait_ge(g_out, 16)
                    dve.wait_ge(m_out, 16)
                    dve.wait_ge(rows_exp, 1)
                    link(v.tensor_tensor(lam[:, 4:5], lam[:, 3:4], lam[:, 2:3], ALU.subtract))
                    link(v.tensor_scalar(lam[:, 4:5], lam[:, 4:5], -LAM_INIT, None, ALU.add))
                    link(v.tensor_scalar(sgi[:, :], pidx[0:64, :], 1, None, ALU.bitwise_and))
                    link(v.tensor_copy(sgn[:, 0:1], sgi[:, :]))
                    link(v.tensor_scalar(sgn[:, 1:2], lam[0:64, 4:5], -1.0, None, ALU.add))
                    link(v.tensor_tensor(sgn[:, 2:3], sgn[:, 0:1], sgn[:, 1:2], ALU.mult))
                    link(v.tensor_scalar(sgn[:, 3:4], sgn[:, 2:3], 1.0, None, ALU.add))
                    link(v.tensor_scalar(gda[:, :], gda[:, :], 1.0 - LAM_INIT, None, ALU.mult))
                    link(v.memset(HO[0:S0, T4, :], 0.0))
                elif kind == "decscore":
                    for n, (b, p) in enumerate(DEC):
                        dve.wait_ge(page_in[n % 4], 16 * (n // 4 + 1))
                        if p == 0:
                            dve.wait_ge(page_in[4], 16 * (b + 1))
                        link(v.tensor_tensor(kring[n % 4], kring[n % 4], kring[4], ALU.mult))
                        v.tensor_reduce(Sd[:, p, 8 * b:8 * b + 8], kring[n % 4].rearrange("p (u d) -> p u d", d=DQ),
                                        AX.X, ALU.add).then_inc(page_used, 1)
                elif kind == "decsm":
                    dve.wait_ge(qk64_in, 32)
                    link(v.tensor_tensor(qk64[:, 0, :], qk64[:, 0, :], qk64[:, 1, :], ALU.mult))
                    link(v.tensor_reduce(Sq[:, PAST:PAST + 1], qk64[:, 0, :], AX.X, ALU.add))
                    after(dve, item, "t")
                    v.tensor_copy(Sq[:, 0:PAST], PS["t"][0:64, 0:PAST]).then_inc(freed["t"], 1)
                    drained(dve, item, "t")
                    v.tensor_reduce(dcol[:, 1:2], Sq[:, 0:PAST + 1], AX.X, ALU.max, negate=True).then_inc(dec_max, 1)
                    dve.wait_ge(dec_exp, 1)
                    link(v.reciprocal(dcol[:, 3:4], dcol[:, 2:3]))
                    link(v.tensor_tensor(dcol[:, 3:4], dcol[:, 3:4], sgn[:, 3:4], ALU.mult))
                    v.tensor_scalar(Sq[:, 0:PAST + 1], Sq[:, 0:PAST + 1], dcol[:, 3:4], None, ALU.mult).then_inc(dec_coef, 1)
                elif kind == "decmix":
                    after(dve, item, "p")
                    v.tensor_reduce(Wd[:, :, :], PS["p"][:, 0:128].rearrange("p (a r m) -> p a r m", a=NPAGES, m=2),
                                    AX.X, ALU.add).then_inc(freed["p"], 1)
                    mask_products("t", mask1, kring[4])
                elif kind == "decmix2":
                    mask_products("p", mask2, kring[0])
                    dve.wait_ge(decps_in, 16)
                    link(v.tensor_reduce(dr[S0:N4, 48:52], dr[S0:N4, 40:48].rearrange("p (h m) -> p h m", m=2), AX.X, ALU.add))
                    drained(dve, ("small", "dv"), "t")
                    dve.wait_ge(tok_out, 16 * 6)
                    after(dve, item, "t")
                    for h in range(H):
                        ins = v.scalar_tensor_tensor(HO[S0:N4, T4, 512 + DV * h:512 + DV * (h + 1)],
                                                     DVt[S0:N4, T4, DV * h:DV * (h + 1)], dr[S0:N4, 48 + h:49 + h],
                                                     PS["t"][S0:N4, DV * h:DV * (h + 1)], ALU.mult, ALU.add)
                    ins.then_inc(freed["t"], 1)
                elif kind == "qk":
                    j, h = item[1:]
                    u = UIDX[j, h]
                    n = 128 if j < NT else NMETA
                    w = 128 * (j + 1) + NMETA if j < NT else NMETA
                    d0 = 128 * j if j < NT else 0
                    P = P2[u % 2]
                    after(dve, item, "Sa")
                    after(dve, item, "Sb")
                    diag = Sps[0:n, :, d0:d0 + n]
                    link(v.tensor_tensor(diag, diag, maskneg[0:n, None, 0:n].to_broadcast([n, 2, n]), ALU.add))
                    v.tensor_reduce(sums[0:n, 0:2], Sps[0:n, :, 0:w], AX.X, ALU.max, negate=True).then_inc(maxed, 1)
                    drained(dve, item, "Sa")
                    drained(dve, item, "Sb")
                    link(v.reciprocal(sums[0:n, 4:6], sums[0:n, 2:4]))
                    link(v.tensor_copy(rsum[0:n, u:u + 1], sums[0:n, 4:5]))
                    link(v.scalar_tensor_tensor(sums[0:n, 6:7], sums[0:n, 2:3], lam[0:n, 4:5], sums[0:n, 5:6], ALU.mult, ALU.mult))
                    v.scalar_tensor_tensor(P[0:n, 0, 0:w], P[0:n, 1, 0:w], sums[0:n, 6:7], P[0:n, 0, 0:w],
                                           ALU.mult, ALU.add).then_inc(mixed, 1)
                elif kind == "mqk_s":
                    h = item[1]
                    WT, WTm = WTs[h % 2]
                    dve.wait_ge(decay_masked, h + 1)
                    for i in range(NT):
                        if i % 2 == 0:
                            after(dve, item, "Sb" if i else "Sa")
                        ins = v.tensor_tensor(WT[:, OFF[i]:OFF[i] + 512 - 128 * i], WT[:, OFF[i]:OFF[i] + 512 - 128 * i],
                                              Sps[:, i // 2, 512 * (i % 2):512 * (i % 2) + 512 - 128 * i], ALU.mult)
                        if i % 2:
                            ins.then_inc(freed["Sb" if i > 1 else "Sa"], 1)
                    after(dve, item, "t")
                    v.tensor_tensor(WTm[:, N4:TOK], WTm[:, N4:TOK], PS["t"][0:NMETA, :], ALU.mult).then_inc(freed["t"], 1)
                    after(dve, item, "p")
                    v.tensor_tensor(WTm[:, 0:NMETA], WTm[:, 0:NMETA], PS["p"][0:NMETA, 0:NMETA], ALU.mult).then_inc(freed["p"], 1)
                elif kind == "mpv":
                    h = item[1]
                    for b, jj, n in (("a0", (0, 3), 128), ("a1", (3, 4), 128), ("a1", (4, 5), NMETA)):
                        after(dve, item, b)
                        o = 129 * (jj[0] - (3 if b == "a1" else 0))
                        k = jj[1] - jj[0]
                        src = PS[b][0:n, o:o + 129 * k].rearrange("p (j d) -> p j d", d=129)
                        dd = src[:, :, DV:DV + 1]
                        link(v.scalar_tensor_tensor(den[0:n, 0:k, :], dd, -1.0, RC[0:n, jj[0]:jj[1], 64 + h:65 + h],
                                                    ALU.mult, ALU.max))
                        link(v.tensor_tensor(den[0:n, 0:k, :], den[0:n, 0:k, :], dd, ALU.max))
                        link(v.reciprocal(den[0:n, 0:k, :], den[0:n, 0:k, :]))
                        ins = v.tensor_tensor(HO[0:n, jj[0]:jj[1], DV * h:DV * (h + 1)], src[:, :, 0:DV],
                                              den[0:n, 0:k, :].to_broadcast([n, k, DV]), ALU.mult)
                        if b == "a0" or jj[0] == 4:
                            ins.then_inc(freed[b], 1)
                            drained(dve, item, b)
                        else:
                            link(ins)
                elif kind in ("mdec1", "mdec2", "mdec3", "wsk", "sig"):
                    decode_state(kind, item)
                elif kind == "on":
                    j = item[1]
                    n = nrows(j)
                    if j == 0:
                        drained(dve, ("pv",) + UNITS[-1], "p")
                    dve.wait_ge(rsq, RSQ8[j])
                    ho = HO[0:n, j, :].rearrange("p (u d) -> p u d", d=DV)
                    link(v.tensor_tensor(ho, ho, rr8[0:n, j, :, None].to_broadcast([n, 8, DV]), ALU.mult))
                    v.tensor_tensor(ho[:, 4:8], ho[:, 4:8], gda[0:n, None, :].to_broadcast([n, 4, DV]), ALU.mult)
                    v.tensor_tensor(HO[0:n, j, 0:512], HO[0:n, j, 0:512], MO[0:n, j, :], ALU.mult).then_inc(ho_ready, 1)
                elif kind == "wo":
                    j, half = item[1:]
                    n = nrows(j)
                    b = "a%d" % half
                    after(dve, item, b)
                    xs = X[0:n, j, 512 * half:512 * half + 512]
                    ins = v.tensor_tensor(xs, xs, PS[b][0:n, :], ALU.add)
                    if j == T4:
                        xs = X[0:n, j, 512:1024]
                        ins = v.tensor_tensor(xs, xs, PS[b][64:64 + n, :], ALU.add)
                    ins.then_inc(freed[b], 1)
                elif kind == "xn":
                    j = item[1]
                    n = nrows(j)
                    dve.wait_ge(rsq, RSQF[j])
                    v.tensor_scalar(HO[0:n, j, :], X[0:n, j, :], rr[0:n, 5 + j:6 + j], None, ALU.mult).then_inc(xn_ready, 1)
                elif kind == "rt":
                    j = item[1]
                    transposed(item, tbanks(item), gffn, j)
                elif kind == "logit":
                    j = item[1]
                    n = nrows(j)
                    if j == 0:
                        link(v.memset(Lt[:, :, :], 0.0))
                    after(dve, item, "t")
                    v.tensor_tensor(Lt[0:n, j, :], PS["t"][0:n, 0:36], br[0:n, :], ALU.add).then_inc(freed["t"], 1)
                elif kind == "rank":
                    drained(dve, ("logit", T4), "t")
                    b4 = lambda a: a[:, :, None].to_broadcast([128, NTILES, 4])
                    gl = L[:, :, 0:4]
                    gmax, gsum, v1, v2, dlt, ex, key, p1 = c5[0], c5[1], c5[2], c5[3], c5[4], c5[5], c5[6], c5[7]

                    def first(onehot, vals, best, width, tmp):
                        bw = lambda a: a[:, :, None].to_broadcast([128, NTILES, width])
                        link(v.tensor_tensor(tmp, vals, bw(best), ALU.is_equal))
                        link(v.tensor_tensor(tmp, tmp, kiota[:, None, 0:width].to_broadcast([128, NTILES, width]), ALU.mult))
                        link(v.tensor_reduce(key, tmp, AX.X, ALU.max))
                        link(v.tensor_tensor(onehot, tmp, bw(key), ALU.is_equal))

                    link(v.tensor_reduce(gmax, gl, AX.X, ALU.max))
                    v.tensor_tensor(Gx, gl, b4(gmax), ALU.subtract).then_inc(gexp_in, 1)
                    first(Go, gl, gmax, 4, Gk)
                    t4 = T160.rearrange("p (j g e) -> p j g e", g=4, e=8)
                    in_group = Go[:, :, :, None].to_broadcast([128, NTILES, 4, 8])
                    link(v.tensor_tensor(t4, L[:, :, 4:36].rearrange("p j (g e) -> p j g e", g=4), in_group, ALU.mult))
                    ein, o1, o2, tmp, rest = E8
                    link(v.tensor_reduce(ein, t4.rearrange("p j g e -> p j e g"), AX.X, ALU.add))
                    link(v.tensor_reduce(v1, ein, AX.X, ALU.max))
                    first(o1, ein, v1, 8, tmp)
                    link(v.scalar_tensor_tensor(rest, o1, -3e38, ein, ALU.mult, ALU.add))
                    link(v.tensor_reduce(v2, rest, AX.X, ALU.max))
                    first(o2, rest, v2, 8, tmp)
                    v.tensor_tensor(dlt, v2, v1, ALU.subtract).then_inc(gexp_in, 1)
                    link(v.tensor_tensor(Go, Go, valid[:, :, None].to_broadcast([128, NTILES, 4]), ALU.mult))
                    for dst, o in ((M1, o1), (M2, o2)):
                        d4 = dst.rearrange("p (j g e) -> p j g e", g=4, e=8)
                        link(v.tensor_tensor(d4, o[:, :, None, :].to_broadcast([128, NTILES, 4, 8]), in_group, ALU.mult))
                    link(v.tensor_tensor(MM, M1, M2, ALU.add))
                    link(v.memset(CUM[:, 0:32], 0.0))
                    for j in range(NTILES):
                        ins = v.tensor_tensor(CUM[:, 32 * j + 32:32 * j + 64], CUM[:, 32 * j:32 * j + 32],
                                              MM[:, 32 * j:32 * j + 32], ALU.add)
                        if j < NTILES - 1:
                            link(ins)
                    ins.then_inc(m_ready, 1)
                    dve.wait_ge(gexp, 2)
                    link(v.tensor_reduce(gsum, Gx, AX.X, ALU.add))
                    link(v.tensor_scalar(p1, ex, 1.0, None, ALU.add))
                    link(v.tensor_tensor(p1, p1, gsum, ALU.mult))
                    link(v.reciprocal(pw[:, 0, :], p1))
                    link(v.tensor_tensor(pw[:, 1, :], pw[:, 0, :], ex, ALU.mult))
                    after(dve, item, "p")
                    v.tensor_copy(PREF, PS["p"][:, 0:192]).then_inc(freed["p"], 1)
                    drained(dve, item, "p")
                    rank = PREF[:, 0:160].rearrange("p (j e) -> p j e", e=32)
                    cnt = PREF[:, 160:192]
                    extra, xend, dd, one32 = e32[0], e32[1], e32[2], e32[3]
                    cx = CX.rearrange("p (e q) -> p e q", q=MAXQ)
                    link(v.tensor_tensor(cx, cnt[:, :, None].to_broadcast([128, 32, MAXQ]),
                                         qiota[:, None, :].to_broadcast([128, 32, MAXQ]), ALU.is_gt))
                    link(v.tensor_reduce(extra, cx, AX.X, ALU.add))
                    link(v.memset(one32, 1.0))
                    link(v.tensor_tensor_scan(xend, one32, extra, 0.0, ALU.mult, ALU.add))
                    link(v.tensor_tensor(dd, xend, extra, ALU.subtract))
                    link(v.tensor_scalar(dd, dd, float(SLOTS), float(XROW - SLOTS), ALU.mult, ALU.add))
                    link(v.tensor_tensor(dd, dd, eiota[:, :], ALU.subtract))
                    t3 = T160.rearrange("p (j e) -> p j e", e=32)
                    link(v.tensor_scalar(t3, rank, float(SLOTS), None, ALU.is_ge))
                    link(v.tensor_tensor(t3, t3, dd[:, None, :].to_broadcast([128, NTILES, 32]), ALU.mult))
                    link(v.tensor_tensor(t3, t3, rank, ALU.add))
                    link(v.tensor_tensor(t3, t3, eiota[:, None, :].to_broadcast([128, NTILES, 32]), ALU.add))
                    for c, m_ in enumerate((M1, M2)):
                        link(v.tensor_tensor(m_, m_, T160, ALU.mult))
                        link(v.tensor_reduce(slot_of[:, c, :], m_.rearrange("p (j e) -> p j e", e=32), AX.X, ALU.add))
                    link(v.tensor_tensor(slot_of, slot_of, dump[:, :, :], ALU.add))
                    link(v.tensor_copy(slot_int[:, :, :], slot_of))
                    link(v.tensor_scalar(slot_int[:, :, :], slot_int[:, :, :], 127, None, ALU.bitwise_and))
                    link(v.tensor_copy(in_pair, slot_int[:, :, :]))
                    link(v.tensor_tensor(slot_of, slot_of, in_pair, ALU.subtract))
                    one = lambda a: a.rearrange("p c j -> p (c j)")[:, :, None]
                    v.tensor_tensor(in_onehot, riota[:, None, :].to_broadcast([128, 10, 128]),
                                    one(in_pair).to_broadcast([128, 10, 128]), ALU.is_equal)
                    link(v.tensor_tensor(pair_onehot[:, :, 0], piota[:, None, :].to_broadcast([128, 10, NPAIRS]),
                                         one(slot_of).to_broadcast([128, 10, NPAIRS]), ALU.is_equal))
                    v.tensor_tensor(pair_onehot[:, :, 1], pair_onehot[:, :, 0],
                                    tokf[:, :, None].to_broadcast([128, 10, NPAIRS]), ALU.mult).then_inc(onehots_ready, 1)
                elif kind == "invert":
                    after(dve, item, "p")
                    taken, row = PS["p"][:, 0:NPAIRS], PS["p"][:, NPAIRS:2 * NPAIRS]
                    link(v.tensor_scalar(GONE, taken, float(-NOROW), float(NOROW), ALU.mult, ALU.add))
                    link(v.tensor_tensor(slot_ids[:, :, 1], GONE, row, ALU.add))
                    v.tensor_scalar(slot_ids[:, :, 0], slot_ids[:, :, 1], NOROW | SECOND - 1, None, ALU.bitwise_and)\
                     .then_inc(ids_ready, 1)
                    dve.wait_ge(ids_ready, 1)
                    v.nop().then_inc(freed["p"], 1)
                    xend = e32[1]
                    x3 = XT32[0:1, :].rearrange("p (x e) -> p x e", e=32)
                    link(v.tensor_tensor(x3, xend[0:1, None, :].to_broadcast([1, XBLOCKS, 32]),
                                         xiota[:, :, None].to_broadcast([1, XBLOCKS, 32]), ALU.is_le))
                    link(v.tensor_reduce(xf[0:1, 0:XBLOCKS], x3, AX.X, ALU.add))
                    link(v.tensor_scalar(TE[0:1, 0:XBLOCKS], xf[0:1, 0:XBLOCKS], float(NEXP - 1), None, ALU.min))
                    link(v.tensor_copy(TE[0:1, XBLOCKS:XBLOCKS + 1], xend[0:1, 31:32]))
                    v.nop().then_inc(table_ready, 1)

            def pair(i, s):
                dve.wait_ge(xt_filled[s], i + 1)
                reuse(dve, gu_filled[s], i)
                for half in range(2):
                    ins = v.tensor_tensor(xT[s][:, 4 * half:4 * half + 4, :],
                                          bank[half][:, :].rearrange("p (k t) -> p k t", t=128),
                                          gffn[:, 4 * half:4 * half + 4, None].to_broadcast([128, 4, 128]), ALU.mult)
                ins.then_inc(xt_evac[s], 1)
                dve.wait_ge(silu_done[s], i + 1)
                reuse(dve, at_filled[s], i)
                v.tensor_tensor(AB[s], SG[s], PS["t" if s else "p"][:, DE:2 * DE], ALU.mult).then_inc(act_done[s], 1)
                dve.wait_ge(dn_filled[s], i + 1)
                reuse(dve, y_out[s], 16 * i)
                v.tensor_copy(YO[s][:, 512:1024], Sps[:, 0, 512:1024]).then_inc(y1[s], 1)

            def finish(j):
                n = nrows(j)
                dve.wait_ge(rsq, 3 * NTILES + j + 1)
                if j == 0:
                    dve.wait_ge(gfin_in, 16)
                v.scalar_tensor_tensor(X[0:n, j, :], X[0:n, j, :], rr[0:n, 10 + j:11 + j], gfin[0:n],
                                       ALU.mult, ALU.mult).then_inc(yfin, 1)

            for s in range(2):
                pair(0, s)
            with dve.Fori(1, PAIRS // 2) as i:
                for s in range(2):
                    pair(i, s)
            loop_further(dve, further_blocks(dve), pair)
            for j in range(NTILES):
                n = nrows(j)
                dve.wait_ge(y_in[j], 16 if j < NT else 32)
                for c in range(2):
                    ins = v.scalar_tensor_tensor(X[0:n, j, :], YG[j][0:n, c], pw[0:n, c, j:j + 1], X[0:n, j, :],
                                                 ALU.mult, ALU.add)
                    if c == 0:
                        link(ins)
                    else:
                        ins.then_inc(x2_ready, 1)
                if j:
                    finish(j - 1)
            finish(T4)

        @block.tensor
        def _(pe):
            def transpose_rows(rows, item, j):
                n = nrows(j)
                names = banks_of(item)
                for half in range(2):
                    b = names[min(half, len(names) - 1)]
                    if half == 0 or len(names) == 2:
                        before(pe, item, b)
                    dst = bank[half][:, :] if len(names) == 2 else Sps[:, b == "Sb", 512 * half:512 * half + 512]
                    for k in range(4):
                        mm = pe.transpose(dst[:, 128 * k:128 * k + n], rows[0:n, 4 * half + k:D:KC], ident[0:n, 0:n])
                    if len(names) == 2 or half == 1:
                        mm.then_inc(filled[b], 1)

            def mix_values(dst, rows):
                before(pe, item, dst)
                for b in rows:
                    for p in range(NPAGES):
                        n = b * NPAGES + p
                        pe.wait_ge(vpage_in[n % 8], 16 * (n // 8 + 1))
                        mm = pe.matmul(PS[dst][32 * (b % 4):32 * (b % 4) + 32, :], Wd[:, p, :], vring[n % 8],
                                       start=(p == 0), stop=(p == NPAGES - 1))
                    if b % 4 < 3:
                        mm.then_inc(vpage_used, 2)
                    else:
                        mm.then_inc(filled[dst], 1)
                        after(pe, item, dst)
                        pe.nop().then_inc(vpage_used, 2)

            for item in ORDER:
                kind = item[0]
                if kind == "xt":
                    j = item[1]
                    if j == 0:
                        pe.wait_ge(ident_made, 1)
                    pe.wait_ge(hn_ready, j + 1)
                    transpose_rows(hn[j % 2], item, j)
                elif kind == "gates":
                    for j in range(NTILES):
                        drained(pe, ("xt", j), banks_of(("xt", j))[-1])
                    pe.wait_ge(wg_in, 32)
                    before(pe, item, "t")
                    before(pe, item, "p")
                    for b, c0, c1_ in (("t", 0, 512), ("p", 512, TOK)):
                        for k in range(KC):
                            mm = pe.matmul(PS[b][0:36, 0:c1_ - c0], wg[:, k, :], hT[:, k, c0:c1_],
                                           start=(k == 0), stop=(k == KC - 1))
                        mm.then_inc(filled[b], 1)
                elif kind == "acc":
                    b, m = item[1:]
                    r = "a%d" % (m % 2)
                    n = BLOCKS.index(b)
                    w = blkslot[n % 3]
                    if m == 0:
                        pe.wait_ge(block_in[n % 3], 16 * (n // 3 + 1))
                    before(pe, item, r)
                    for k in range(KC):
                        if b in FEATURE:
                            mm = pe.matmul(PS[r][:, :], w[:, k, 128 * m:128 * (m + 1)], hT[:, k, 0:512],
                                           start=(k == 0), stop=(k == KC - 1))
                        else:
                            mm = pe.matmul(PS[r][:, :], hT[:, k, 128 * m:128 * (m + 1)], w[:, k, :],
                                           start=(k == 0), stop=(k == KC - 1))
                    mm.then_inc(filled[r], 1)
                elif kind == "small":
                    b = item[1]
                    w = blkslot[BLOCKS.index(b) % 3]
                    before(pe, item, "t")
                    for k in range(KC):
                        for u in range(2):
                            mm = pe.matmul(PS["t"][64 * u:64 * u + N4, 0:256], hT[:, k, 512:TOK],
                                           w[:, k, 256 * u:256 * u + 256], start=(k == 0), stop=(k == KC - 1))
                    mm.then_inc(filled["t"], 1)
                    pe.wait_ge(filled["t"], NTH[item, "t"] + 1)
                    pe.nop().then_inc(block_used, 1)
                elif kind == "ft":
                    b = item[1]
                    drained(pe, ("small", b), "t")
                    before(pe, item, "p")
                    for m in range(4):
                        cols = slice(128 * m, 128 * m + 128)
                        src = (MVA[0:N4, T4, m, 0:DV] if b == "mv" else tokst[0][0:N4, cols] if b == "dq" else
                               tokst[1][0:N4, cols] if b == "dk" else MQ4[:, cols] if m < 2 else
                               MK[0:N4, T4, 128 * (m - 2):128 * (m - 1)])
                        mm = pe.transpose(PS["p"][:, N4 * m:N4 * (m + 1)], src, ident[0:N4, 0:N4])
                    mm.then_inc(filled["p"], 1)
                elif kind == "tok":
                    name, j = item[1:]
                    b, m0 = ("dk", 0) if name == "dk" else ("mqk", 2)
                    if j == 0:
                        drained(pe, ("acc", b, 2), "a0")
                        drained(pe, ("acc", b, 3), "a1")
                    r = "pt"[j % 2]
                    before(pe, item, r)
                    for m in range(m0, 4):
                        mm = pe.transpose(PS[r][:, 128 * (m - m0):128 * (m - m0 + 1)], feat[b][:, m, col(j):col(j) + 128],
                                          ident[:, :])
                    mm.then_inc(filled[r], 1)
                elif kind == "rows":
                    pe.wait_ge(rows_exp, 1)
                    pe.wait_ge(rows_scan, 3)
                    before(pe, item, "t")
                    for j in range(NTILES):
                        n = nrows(j)
                        c0 = N4 + 128 * j if j < NT else 0
                        mm = pe.transpose(PS["t"][0:n, 68 * j:68 * (j + 1)], R[0:68, c0:c0 + n], ident[0:68, 0:68])
                    mm.then_inc(filled["t"], 1)
                elif kind == "decsm":
                    pe.wait_ge(page_used, len(DEC))
                    before(pe, item, "t")
                    for p in range(NPAGES):
                        mm = pe.transpose(PS["t"][0:64, 128 * p:128 * (p + 1)], Sd[:, p, :], ident[:, :])
                    mm.then_inc(filled["t"], 1)
                elif kind == "decmix":
                    pe.wait_ge(dec_coef, 1)
                    before(pe, item, "p")
                    for p in range(NPAGES):
                        mm = pe.transpose(PS["p"][:, 64 * p:64 * (p + 1)], Sq[:, 128 * p:128 * (p + 1)], ident[0:64, 0:64])
                    mm.then_inc(filled["p"], 1)
                    drained(pe, item, "p")
                    mix_values("t", range(0, 4))
                elif kind == "decmix2":
                    mix_values("p", range(4, 8))
                    drained(pe, ("decmix",), "t")
                    drained(pe, item, "p")
                    before(pe, item, "t")
                    for n, part in enumerate((kring[4], kring[0])):
                        mm = pe.matmul(PS["t"][0:N4, :], sel[:, :], part, start=(n == 0), stop=(n == 1))
                    mm.then_inc(filled["t"], 1)
                elif kind == "qk":
                    j, h = item[1:]
                    n = 128 if j < NT else NMETA
                    c0 = col(j)
                    if UIDX[j, h] == 0:
                        for b in ("dq", "dk"):
                            drained(pe, ("acc", b, 3), "a1")
                            drained(pe, ("ft", b), "p")
                    for m in range(2):
                        before(pe, item, ("Sa", "Sb")[m])
                        r = slice(64 * m, 64 * m + 64)
                        at_ = 0
                        if j < NT:
                            at_ = 128 * (j + 1)
                            pe.matmul(Sps[0:n, m, 0:at_], dqT[r, h, c0:c0 + n], dkT[r, h, 0:at_], start=True, stop=True)
                        mm = pe.matmul(Sps[0:n, m, at_:at_ + NMETA], dqT[r, h, c0:c0 + n], dkT[r, h, 512:512 + NMETA],
                                       start=True, stop=True)
                        mm.then_inc(filled[("Sa", "Sb")[m]], 1)
                elif kind == "tp":
                    j, h = item[1:]
                    n = 128 if j < NT else NMETA
                    P = P2[UIDX[j, h] % 2]
                    pe.wait_ge(mixed, UIDX[j, h] + 1)
                    before(pe, item, "p")
                    at_ = 128 * (j + 1) if j < NT else 0
                    pe.transpose(PS["p"][0:NMETA, 0:n], P[0:n, 0, at_:at_ + NMETA], ident[0:n, 0:n]).then_inc(filled["p"], 1)
                    if j < NT:
                        before(pe, item, "t")
                        for i in range(j + 1):
                            mm = pe.transpose(PS["t"][:, 128 * i:128 * (i + 1)], P[0:n, 0, 128 * i:128 * (i + 1)], ident[0:n, 0:n])
                        mm.then_inc(filled["t"], 1)
                elif kind == "pv":
                    j, h = item[1:]
                    n = 128 if j < NT else NMETA
                    drained(pe, ("tp", j, h), "p")
                    if UIDX[j, h] == 0:
                        drained(pe, ("acc", "dv", 3), "a1")
                        drained(pe, ("small", "dv"), "t")
                    before(pe, item, "p")
                    mm = pe.matmul(PS["p"][0:n, 0:DV], AT[0:NMETA, 4, 0:n], DVt[0:NMETA, T4, DV * h:DV * (h + 1)],
                                   start=True, stop=(j == T4))
                    for i in range(j + 1) if j < NT else ():
                        mm = pe.matmul(PS["p"][0:n, 0:DV], AT[:, i, 0:n], DVt[:, i, DV * h:DV * (h + 1)],
                                       start=False, stop=(i == j))
                    mm.then_inc(filled["p"], 1)
                elif kind == "mqk_s":
                    h = item[1]
                    r = slice(64 * (h % 2), 64 * (h % 2) + 64)
                    if h == 0:
                        drained(pe, ("acc", "mqk", 3), "a1")
                        drained(pe, ("ft", "mqk"), "p")
                    kT, qT = mqkT[r, 2 + h // 2, :], mqkT[r, h // 2, :]
                    for b in ("Sa", "Sb", "t", "p"):
                        before(pe, item, b)
                    for i in range(NT):
                        mm = pe.matmul(Sps[:, i // 2, 512 * (i % 2):512 * (i % 2) + 512 - 128 * i],
                                       kT[:, 128 * i:128 * (i + 1)], qT[:, 128 * i:512], start=True, stop=True)
                        if i % 2:
                            mm.then_inc(filled["Sb" if i > 1 else "Sa"], 1)
                    pe.matmul(PS["t"][0:NMETA, :], kT[:, 512:512 + NMETA], qT[:, 0:512], start=True, stop=True)\
                      .then_inc(filled["t"], 1)
                    pe.matmul(PS["p"][0:NMETA, 0:NMETA], kT[:, 512:512 + NMETA], qT[:, 512:512 + NMETA],
                              start=True, stop=True).then_inc(filled["p"], 1)
                elif kind == "mpv":
                    h = item[1]
                    WT, WTm = WTs[h % 2]
                    for b in ("Sa", "Sb", "t", "p"):
                        drained(pe, ("mqk_s", h), b)
                    if h == 0:
                        drained(pe, ("acc", "mv", 3), "a1")
                        drained(pe, ("small", "mv"), "t")
                    before(pe, item, "a0")
                    before(pe, item, "a1")
                    for j in range(NTILES):
                        n = 128 if j < NT else NMETA
                        b, o = ("a0", 129 * j) if j < 3 else ("a1", 129 * (j - 3))
                        c0 = N4 + 128 * j if j < NT else 0
                        for i in range(j + 1) if j < NT else ():
                            pe.matmul(PS[b][0:n, o:o + 129], WT[:, OFF[i] + 128 * (j - i):OFF[i] + 128 * (j - i) + 128],
                                      MVA[:, i, h, :], start=(i == 0), stop=False)
                        mm = pe.matmul(PS[b][0:n, o:o + 129], WTm[:, c0:c0 + n], MVA[0:NMETA, T4, h, :],
                                       start=(j == T4), stop=True)
                        if j in (2, 4):
                            mm.then_inc(filled[b], 1)
                elif kind == "mdec2":
                    pe.wait_ge(pad_ready, 1)
                    before(pe, item, "t")
                    for h in range(H):
                        mm = pe.transpose(PS["t"][0:N4, DV * h:DV * (h + 1)], padT[:, h, :], ident[:, :])
                    mm.then_inc(filled["t"], 1)
                elif kind == "cfin":
                    pe.wait_ge(wsk_ready, 1)
                    before(pe, item, "t")
                    for h in range(H):
                        for j in range(NTILES):
                            n = 128 if j < NT else NMETA
                            pe.matmul(PS["t"][:, DQ * h:DQ * (h + 1)], MVA[0:n, j, h, 0:DV], MK[0:n, j, DQ * h:DQ * (h + 1)],
                                      start=(j == 0), stop=(j == T4))
                    for j in range(NTILES):
                        n = 128 if j < NT else NMETA
                        mm = pe.matmul(PS["t"][0:1, 256:512], ones[0:n, 0:1], MK[0:n, j, :], start=(j == 0), stop=(j == T4))
                    mm.then_inc(filled["t"], 1)
                elif kind == "ot":
                    j = item[1]
                    pe.wait_ge(ho_ready, j + 1)
                    transpose_rows(HO[:, j, :], item, j)
                elif kind == "wo":
                    j, half = item[1:]
                    n = nrows(j)
                    bidx = 6 + half
                    if j == 0:
                        pe.wait_ge(block_in[bidx % 3], 16 * (bidx // 3 + 1))
                    drained(pe, ("ot", j), "Sa")
                    b = "a%d" % half
                    before(pe, item, b)
                    for k in range(KC):
                        if j < T4:
                            mm = pe.matmul(PS[b][0:n, :], hT[:, k, col(j):col(j) + n], blkslot[bidx % 3][:, k, :],
                                           start=(k == 0), stop=(k == KC - 1))
                            continue
                        for u in range(2):
                            mm = pe.matmul(PS[b][64 * u:64 * u + n, :], hT[:, k, 512:TOK], blkslot[(6 + u) % 3][:, k, :],
                                           start=(k == 0), stop=(k == KC - 1))
                    mm.then_inc(filled[b], 1)
                    if j == T4:
                        after(pe, item, b)
                        pe.nop().then_inc(block_used, 2)
                elif kind == "rt":
                    j = item[1]
                    pe.wait_ge(xn_ready, j + 1)
                    transpose_rows(HO[:, j, :], item, j)
                elif kind == "logit":
                    j = item[1]
                    n = nrows(j)
                    pe.wait_ge(const_in, 16 * NCONST)
                    drained(pe, ("rt", j), "Sb")
                    before(pe, item, "t")
                    for k in range(KC):
                        mm = pe.matmul(PS["t"][0:n, 0:36], hT[:, k, col(j):col(j) + n], wr[:, k, :],
                                       start=(k == 0), stop=(k == KC - 1))
                    mm.then_inc(filled["t"], 1)
                elif kind == "rank":
                    pe.wait_ge(m_ready, 1)
                    before(pe, item, "p")
                    pe.matmul(PS["p"][:, 0:160], tri[:, :], MM, start=True, stop=False)
                    pe.matmul(PS["p"][:, 0:160], ones[:, :], CUM[:, 0:160], start=False, stop=True)
                    mm = pe.matmul(PS["p"][:, 160:192], ones[:, :], CUM[:, 160:192], start=True, stop=True)
                    mm.then_inc(filled["p"], 1)
                elif kind == "invert":
                    pe.wait_ge(onehots_ready, 1)
                    before(pe, item, "p")
                    for n in range(10):
                        mm = pe.matmul(PS["p"][:, 0:2 * NPAIRS], in_onehot[:, n, :],
                                  pair_onehot[:, n].rearrange("p o a -> p (o a)"), start=(n == 0), stop=(n == 9))
                    mm.then_inc(filled["p"], 1)

            def pair(i, s):
                pe.wait_ge(xg_in[s], 16 * i + 16)
                reuse(pe, xt_evac[1 - s], i + s)
                for k in range(KC):
                    mm = pe.transpose(bank[k // 4][:, 128 * (k % 4):128 * (k % 4) + 128], XG[s][:, k:D:KC], ident[:, :])
                mm.then_inc(xt_filled[s], 1)
                pe.wait_ge(xt_evac[s], i + 1)
                reuse(pe, act_done[s], i)
                gu = PS["t" if s else "p"]
                for u in range(2):
                    pe.wait_ge(gu_in[2 * s + u], 32 * i + 32)
                for k in range(KC):
                    for u in range(2):
                        mm = pe.matmul(gu[64 * u:64 * u + 64, :], xT[s][:, k, 64 * u:64 * u + 64],
                                       Wgu[2 * s + u][:, :, k, :], start=(k == 0), stop=(k == KC - 1))
                mm.then_inc(gu_filled[s], 1)
                pe.wait_ge(act_done[s], i + 1)
                reuse(pe, at_evac[1 - s], i + s)
                for f in range(FC):
                    mm = pe.transpose(Sps[:, 1, 512 + 128 * f:640 + 128 * f], AB[s][:, f:DE:FC], ident[:, :])
                mm.then_inc(at_filled[s], 1)
                pe.wait_ge(at_evac[s], i + 1)
                reuse(pe, y0[1 - s], i + s)
                reuse(pe, y1[1 - s], i + s)
                for u in range(2):
                    pe.wait_ge(dn_in[2 * s + u], 16 * i + 16)
                for half in range(2):
                    for f in range(FC):
                        for u in range(2):
                            mm = pe.matmul(Sps[64 * u:64 * u + 64, 0, 512 * half:512 * half + 512],
                                           aT[s][:, f, 64 * u:64 * u + 64],
                                           Wdn[2 * s + u][:, f, 512 * half:512 * half + 512],
                                           start=(f == 0), stop=(f == FC - 1))
                mm.then_inc(dn_filled[s], 1)

            for b in ("a0", "a1", "Sa", "Sb", "t", "p"):
                pe.wait_ge(freed[b], TOTAL[b])
            for s in range(2):
                pair(0, s)
            with pe.Fori(1, PAIRS // 2) as i:
                for s in range(2):
                    pair(i, s)
            pe.wait_ge(table_ready, 1)
            loop_further(pe, further_blocks(pe), pair)


_INS = ["x_prompt", "x_sample", "cache_k", "cache_v", "state_C", "state_n", "state_m", "page_table", "meta_tokens",
        "norm_mix", "w_in", "b_gates", "head_norm_m", "lambda_q1", "lambda_k1", "lambda_q2", "lambda_k2",
        "head_norm_da", "w_out", "norm_ffn", "w_group", "b_group", "w_router", "b_router", "w_gate_e", "w_up_e",
        "w_down_e", "norm_final"]
_OUTS = [(1, SEQ, D), (NDEC, 1, D), (1, 1, NMETA + SEQ, H, 2 * DQ), (1, 1, NMETA + SEQ, H, DV), (1, 1, H, DV, DQ),
         (1, 1, H, DQ), (1, 1, H), (1, NDEC, 1, H, 2 * DQ), (1, NDEC, 1, H, DV), (1, NDEC, H, DV, DQ),
         (1, NDEC, H, DQ), (1, NDEC, H)]


def kernel(**inputs):
    import numpy as _np
    import concourse.bacc as _bacc
    from concourse.bass_utils import run_bass_kernel_spmd as _run

    nc = _bacc.Bacc("TRN2", target_bir_lowering=False, num_devices=1)
    arrays, args = {}, []
    for name in _INS:
        a = _np.ascontiguousarray(inputs[name])
        arrays["in_" + name] = a
        args.append(nc.dram_tensor("in_" + name, a.shape, mybir.dt.from_np(a.dtype), kind="ExternalInput").ap())
    for i, shape in enumerate(_OUTS):
        args.append(nc.dram_tensor("out_%d" % i, shape, mybir.dt.float32, kind="ExternalOutput").ap())
    build(nc, *args)
    r = _run(nc, [arrays], core_ids=[0])
    return tuple(r.results[0]["out_%d" % i] for i in range(len(_OUTS)))
```
